# Optimizing a Trainium2 kernel written in Bass

```python
import math
import jax, jax.numpy as jnp
from jax import lax
import numpy as np

D_MODEL = 1024
BATCH = 1
SEQ = 256
DEPTH = 2

CHUNK = 64
PLE_DIM = 256
NORM_EPS = 1e-6
A_HEADS = 8
A_KV_HEADS = 2
A_GROUP = A_HEADS // A_KV_HEADS
A_HEAD_DIM = 64
A_WINDOW = 128
A_WINDOW_CHUNKS = A_WINDOW // CHUNK
ROPE_THETA = 10000.0
B_HEADS = 4
B_HEAD_DIM = 128
B_WIDTH = B_HEADS * B_HEAD_DIM
B_CONV = 4
C_WIDTH = 512
C_BLOCKS = 8
C_BLOCK_DIM = C_WIDTH // C_BLOCKS
C_CONV = 4
LRU_C = 8.0
PEER_HEADS = 8
PEER_NKEYS = 128
PEER_EXPERTS = PEER_NKEYS * PEER_NKEYS
PEER_QDIM = 256
PEER_HALF = PEER_QDIM // 2
PEER_TOPK = 16
PEER_TOKEN_BLOCK = 128

A_Q_DIM = A_HEADS * A_HEAD_DIM
A_KV_DIM = A_KV_HEADS * A_HEAD_DIM
IN_SIZES = (A_Q_DIM, A_KV_DIM, A_KV_DIM, 3 * B_WIDTH, B_HEADS, B_HEADS, B_WIDTH, C_WIDTH, C_WIDTH, D_MODEL, D_MODEL, D_MODEL)
IN_COLS = sum(IN_SIZES)

kernel_name = 'hybrid_swa_deltanet_rglru_peer_trunk'

def rmsnorm(x, w):
    xf = x.astype(jnp.float32)
    y = xf * lax.rsqrt(jnp.mean(xf * xf, axis=-1, keepdims=True) + NORM_EPS)
    return (y * w.astype(jnp.float32)).astype(x.dtype)

def l2norm(x):
    xf = x.astype(jnp.float32)
    return xf * lax.rsqrt(jnp.sum(xf * xf, axis=-1, keepdims=True) + NORM_EPS)

def causal_depthwise_conv(x, w):
    k, c = w.shape
    return lax.conv_general_dilated(x, w[:, None, :].astype(x.dtype), window_strides=(1,), padding=[(k - 1, 0)], dimension_numbers=('NWC', 'WIO', 'NWC'), feature_group_count=c)

def rope(x, positions):
    half = x.shape[-1] // 2
    inv_freq = ROPE_THETA ** (-jnp.arange(half, dtype=jnp.float32) / half)
    ang = positions.astype(jnp.float32)[..., None] * inv_freq
    cos = jnp.cos(ang)[:, :, None, :]
    sin = jnp.sin(ang)[:, :, None, :]
    xf = x.astype(jnp.float32)
    x1, x2 = xf[..., :half], xf[..., half:]
    return jnp.concatenate([x1 * cos - x2 * sin, x2 * cos + x1 * sin], axis=-1).astype(x.dtype)

def sink_softmax(scores, sink):
    m = jnp.maximum(jnp.max(scores, axis=-1, keepdims=True), sink)
    e = jnp.exp(scores - m)
    return e / (jnp.sum(e, axis=-1, keepdims=True) + jnp.exp(sink - m))

def sliding_window_sink_attention(q, k, v, sinks, positions):
    b, s = q.shape[:2]
    n = s // CHUNK
    q = rope(q, positions)
    k = rope(k, positions)
    qb = q.reshape(b, n, CHUNK, A_KV_HEADS, A_GROUP, A_HEAD_DIM)
    kc = k.reshape(b, n, CHUNK, A_KV_HEADS, A_HEAD_DIM)
    vc = v.reshape(b, n, CHUNK, A_KV_HEADS, A_HEAD_DIM)
    shifts = list(range(A_WINDOW_CHUNKS - 1, -1, -1))

    def shift_chunks(t, j):
        return jnp.pad(t, ((0, 0), (j, 0), (0, 0), (0, 0), (0, 0)))[:, :n]

    kb = jnp.concatenate([shift_chunks(kc, j) for j in shifts], axis=2)
    vb = jnp.concatenate([shift_chunks(vc, j) for j in shifts], axis=2)
    chunk_idx = jnp.arange(n)
    valid = jnp.concatenate([jnp.broadcast_to((chunk_idx >= j)[:, None], (n, CHUNK)) for j in shifts], axis=1)
    scores = jnp.einsum('bnqhgd,bnkhd->bnhgqk', qb, kb).astype(jnp.float32) * (A_HEAD_DIM ** -0.5)
    scores = jnp.where(valid[None, :, None, None, None, :], scores, -jnp.inf)
    sink = sinks.astype(jnp.float32).reshape(A_KV_HEADS, A_GROUP)[None, None, :, :, None, None]
    probs = sink_softmax(scores, sink)
    out = jnp.einsum('bnhgqk,bnkhd->bnqhgd', probs.astype(vb.dtype), vb)
    return out.reshape(b, s, A_HEADS * A_HEAD_DIM)

def gated_delta_rule(q, k, v, g, beta):
    b, s, h, dk = q.shape
    n = s // CHUNK
    f32 = jnp.float32

    def to_chunks(t):
        return t.astype(f32).reshape(b, n, CHUNK, h, -1).transpose(1, 0, 3, 2, 4)

    q = to_chunks(q) * (dk ** -0.5)
    k = to_chunks(k)
    v = to_chunks(v)
    g = g.astype(f32).reshape(b, n, CHUNK, h).transpose(1, 0, 3, 2)
    beta = beta.astype(f32).reshape(b, n, CHUNK, h).transpose(1, 0, 3, 2)
    g = jnp.cumsum(g, axis=-1)
    tril = jnp.tril(jnp.ones((CHUNK, CHUNK), dtype=bool))
    strict = jnp.tril(jnp.ones((CHUNK, CHUNK), dtype=bool), -1)
    decay = jnp.exp(jnp.where(tril, g[..., :, None] - g[..., None, :], -jnp.inf))
    k_beta = k * beta[..., None]
    lower = jnp.where(strict, jnp.einsum('nbhid,nbhjd->nbhij', k_beta, k) * decay, 0.0)
    eye = jnp.eye(CHUNK, dtype=f32)
    t_mat = lax.linalg.triangular_solve(eye + lower, jnp.broadcast_to(eye, lower.shape), left_side=True, lower=True, unit_diagonal=True)
    u = jnp.einsum('nbhij,nbhjd->nbhid', t_mat, v * beta[..., None])
    w = jnp.einsum('nbhij,nbhjd->nbhid', t_mat, k_beta * jnp.exp(g)[..., None])
    qk = jnp.einsum('nbhid,nbhjd->nbhij', q, k) * decay

    def step(state, inp):
        q_c, k_c, u_c, w_c, g_c, qk_c = inp
        v_new = u_c - jnp.einsum('bhck,bhkv->bhcv', w_c, state)
        o = jnp.einsum('bhck,bhkv->bhcv', q_c * jnp.exp(g_c)[..., None], state) + jnp.einsum('bhij,bhjv->bhiv', qk_c, v_new)
        g_last = g_c[..., -1:]
        state = state * jnp.exp(g_last)[..., None] + jnp.einsum('bhck,bhcv->bhkv', k_c * jnp.exp(g_last - g_c)[..., None], v_new)
        return state, o

    state0 = jnp.zeros((b, h, dk, v.shape[-1]), f32)
    _, o = lax.scan(step, state0, (q, k, u, w, g, qk))
    return o.transpose(1, 0, 3, 2, 4).reshape(b, s, h, -1)

def rg_lru(x, w_a, b_a, w_i, b_i, lam):
    b, s, w = x.shape
    f32 = jnp.float32
    xf = x.astype(f32)
    xg = xf.reshape(b, s, C_BLOCKS, C_BLOCK_DIM)
    r = jax.nn.sigmoid(jnp.einsum('bsnc,ncd->bsnd', xg, w_a.astype(f32)).reshape(b, s, w) + b_a.astype(f32))
    i = jax.nn.sigmoid(jnp.einsum('bsnc,ncd->bsnd', xg, w_i.astype(f32)).reshape(b, s, w) + b_i.astype(f32))
    log_a = -LRU_C * r * jax.nn.softplus(-lam.astype(f32))
    a = jnp.exp(log_a)
    u = jnp.sqrt(-jnp.expm1(2.0 * log_a)) * (i * xf)

    def combine(left, right):
        a1, h1 = left
        a2, h2 = right
        return a1 * a2, a2 * h1 + h2

    _, hs = lax.associative_scan(combine, (a, u), axis=1)
    return hs.astype(x.dtype)

def peer_ffn(x, w_q, sub_keys, u_tab, v_tab):
    b, s, d = x.shape
    t = b * s
    xt = x.reshape(t, d)
    q = (xt @ w_q).astype(jnp.float32).reshape(t, PEER_HEADS, 2, PEER_HALF)
    sub_scores = jnp.einsum('thsd,hsnd->thsn', q, sub_keys.astype(jnp.float32))
    top_s, top_i = lax.top_k(sub_scores, PEER_TOPK)
    cand = top_s[:, :, 0, :, None] + top_s[:, :, 1, None, :]
    best_s, best_j = lax.top_k(cand.reshape(t, PEER_HEADS, PEER_TOPK * PEER_TOPK), PEER_TOPK)
    idx1 = jnp.take_along_axis(top_i[:, :, 0], best_j // PEER_TOPK, axis=-1)
    idx2 = jnp.take_along_axis(top_i[:, :, 1], best_j % PEER_TOPK, axis=-1)
    experts = idx1 * PEER_NKEYS + idx2
    gates = jax.nn.softmax(best_s, axis=-1)
    nb = t // PEER_TOKEN_BLOCK

    def expert_block(args):
        xb, eb, gb = args
        act = jax.nn.gelu(jnp.einsum('thkd,td->thk', u_tab[eb], xb).astype(jnp.float32))
        coef = (act * gb).astype(v_tab.dtype)
        return jnp.einsum('thk,thkd->td', coef, v_tab[eb])

    out = lax.map(expert_block, (xt.reshape(nb, PEER_TOKEN_BLOCK, d), experts.reshape(nb, PEER_TOKEN_BLOCK, PEER_HEADS, PEER_TOPK), gates.reshape(nb, PEER_TOKEN_BLOCK, PEER_HEADS, PEER_TOPK)))
    return out.reshape(b, s, d).astype(x.dtype)

def hybrid_layer(h, p_i, positions, norm_mix, w_in, attn_sinks, dn_conv, dn_a_log, dn_dt_bias, dn_norm, lru_conv_w, lru_conv_b, lru_w_a, lru_b_a, lru_w_i, lru_b_i, lru_lambda, w_branch_a, w_branch_b, w_branch_c, w_out, norm_ffn, peer_w_q, peer_sub_keys, peer_u, peer_v, norm_ple, ple_w_gate, ple_w_proj):
    b, s, _ = h.shape
    n = rmsnorm(h, norm_mix)
    z = n @ w_in
    split_points = np.cumsum(IN_SIZES)[:-1].tolist()
    a_q, a_k, a_v, b_qkv, b_beta, b_alpha, b_gate, c_x, c_y, g_a, g_b, g_c = jnp.split(z, split_points, axis=-1)

    y_a = sliding_window_sink_attention(a_q.reshape(b, s, A_HEADS, A_HEAD_DIM), a_k.reshape(b, s, A_KV_HEADS, A_HEAD_DIM), a_v.reshape(b, s, A_KV_HEADS, A_HEAD_DIM), attn_sinks, positions)

    qkv = jax.nn.silu(causal_depthwise_conv(b_qkv, dn_conv))
    bq, bk, bv = jnp.split(qkv, 3, axis=-1)
    bq = l2norm(bq.reshape(b, s, B_HEADS, B_HEAD_DIM))
    bk = l2norm(bk.reshape(b, s, B_HEADS, B_HEAD_DIM))
    bv = bv.reshape(b, s, B_HEADS, B_HEAD_DIM)
    beta = jax.nn.sigmoid(b_beta.astype(jnp.float32))
    g = -jnp.exp(dn_a_log.astype(jnp.float32)) * jax.nn.softplus(b_alpha.astype(jnp.float32) + dn_dt_bias.astype(jnp.float32))
    o_b = gated_delta_rule(bq, bk, bv, g, beta).astype(h.dtype)
    o_b = rmsnorm(o_b, dn_norm) * jax.nn.silu(b_gate.reshape(b, s, B_HEADS, B_HEAD_DIM))
    y_b = o_b.reshape(b, s, B_WIDTH)

    xc = causal_depthwise_conv(c_x, lru_conv_w) + lru_conv_b
    y_c = rg_lru(xc, lru_w_a, lru_b_a, lru_w_i, lru_b_i, lru_lambda) * jax.nn.gelu(c_y)

    mixed = jax.nn.sigmoid(g_a) * (y_a @ w_branch_a) + jax.nn.sigmoid(g_b) * (y_b @ w_branch_b) + jax.nn.sigmoid(g_c) * (y_c @ w_branch_c)
    h = h + mixed @ w_out

    h = h + peer_ffn(rmsnorm(h, norm_ffn), peer_w_q, peer_sub_keys, peer_u, peer_v)

    h = h + jax.nn.sigmoid(rmsnorm(h, norm_ple) @ ple_w_gate) * (p_i @ ple_w_proj)
    return h

def setup_inputs(seed: int = 0) -> dict:
    key = jax.random.key(seed)
    ks = jax.random.split(key, 40)
    f32 = jnp.float32

    def normal(k, shape, scale):
        return jax.random.normal(k, shape, f32) * scale

    def gain(k, shape):
        return 1.0 + 0.02 * jax.random.normal(k, shape, f32)

    offsets = jax.random.randint(ks[2], (BATCH, 1), 0, 4096, dtype=jnp.int32)
    positions = offsets + jnp.arange(SEQ, dtype=jnp.int32)[None, :]
    lru_u = jax.random.uniform(ks[16], (DEPTH, C_WIDTH), f32, 0.9, 0.999)
    lru_s = lru_u ** (1.0 / LRU_C)
    dt = jnp.exp(jax.random.uniform(ks[8], (DEPTH, B_HEADS), f32, math.log(1e-3), math.log(0.1)))
    return {
        'x': normal(ks[0], (BATCH, SEQ, D_MODEL), 1.0),
        'p': normal(ks[1], (DEPTH, BATCH, SEQ, PLE_DIM), 1.0),
        'positions': positions,
        'norm_mix': gain(ks[3], (DEPTH, D_MODEL)),
        'w_in': normal(ks[4], (DEPTH, D_MODEL, IN_COLS), D_MODEL ** -0.5),
        'attn_sinks': normal(ks[5], (DEPTH, A_HEADS), 0.5),
        'dn_conv': normal(ks[6], (DEPTH, B_CONV, 3 * B_WIDTH), B_CONV ** -0.5),
        'dn_a_log': jnp.log(jax.random.uniform(ks[7], (DEPTH, B_HEADS), f32, 1.0, 16.0)),
        'dn_dt_bias': dt + jnp.log(-jnp.expm1(-dt)),
        'dn_norm': gain(ks[9], (DEPTH, B_HEAD_DIM)),
        'lru_conv_w': normal(ks[10], (DEPTH, C_CONV, C_WIDTH), C_CONV ** -0.5),
        'lru_conv_b': normal(ks[11], (DEPTH, C_WIDTH), 0.01),
        'lru_w_a': normal(ks[12], (DEPTH, C_BLOCKS, C_BLOCK_DIM, C_BLOCK_DIM), C_BLOCK_DIM ** -0.5),
        'lru_b_a': normal(ks[13], (DEPTH, C_WIDTH), 0.01),
        'lru_w_i': normal(ks[14], (DEPTH, C_BLOCKS, C_BLOCK_DIM, C_BLOCK_DIM), C_BLOCK_DIM ** -0.5),
        'lru_b_i': normal(ks[15], (DEPTH, C_WIDTH), 0.01),
        'lru_lambda': jnp.log(lru_s) - jnp.log1p(-lru_s),
        'w_branch_a': normal(ks[17], (DEPTH, A_Q_DIM, D_MODEL), A_Q_DIM ** -0.5),
        'w_branch_b': normal(ks[18], (DEPTH, B_WIDTH, D_MODEL), B_WIDTH ** -0.5),
        'w_branch_c': normal(ks[19], (DEPTH, C_WIDTH, D_MODEL), C_WIDTH ** -0.5),
        'w_out': normal(ks[20], (DEPTH, D_MODEL, D_MODEL), D_MODEL ** -0.5),
        'norm_ffn': gain(ks[21], (DEPTH, D_MODEL)),
        'peer_w_q': normal(ks[22], (DEPTH, D_MODEL, PEER_HEADS * PEER_QDIM), D_MODEL ** -0.5),
        'peer_sub_keys': normal(ks[23], (DEPTH, PEER_HEADS, 2, PEER_NKEYS, PEER_HALF), PEER_HALF ** -0.5),
        'peer_u': normal(ks[24], (DEPTH, PEER_EXPERTS, D_MODEL), D_MODEL ** -0.5),
        'peer_v': normal(ks[25], (DEPTH, PEER_EXPERTS, D_MODEL), PEER_HEADS ** -0.5),
        'norm_ple': gain(ks[26], (DEPTH, D_MODEL)),
        'ple_w_gate': normal(ks[27], (DEPTH, D_MODEL, D_MODEL), D_MODEL ** -0.5),
        'ple_w_proj': normal(ks[28], (DEPTH, PLE_DIM, D_MODEL), PLE_DIM ** -0.5),
        'norm_final': gain(ks[29], (D_MODEL,)),
    }

def reference(x, p, positions, norm_mix, w_in, attn_sinks, dn_conv, dn_a_log, dn_dt_bias, dn_norm, lru_conv_w, lru_conv_b, lru_w_a, lru_b_a, lru_w_i, lru_b_i, lru_lambda, w_branch_a, w_branch_b, w_branch_c, w_out, norm_ffn, peer_w_q, peer_sub_keys, peer_u, peer_v, norm_ple, ple_w_gate, ple_w_proj, norm_final):
    h = x
    for i in range(DEPTH):
        h = hybrid_layer(h, p[i], positions, norm_mix[i], w_in[i], attn_sinks[i], dn_conv[i], dn_a_log[i], dn_dt_bias[i], dn_norm[i], lru_conv_w[i], lru_conv_b[i], lru_w_a[i], lru_b_a[i], lru_w_i[i], lru_b_i[i], lru_lambda[i], w_branch_a[i], w_branch_b[i], w_branch_c[i], w_out[i], norm_ffn[i], peer_w_q[i], peer_sub_keys[i], peer_u[i], peer_v[i], norm_ple[i], ple_w_gate[i], ple_w_proj[i])
    return rmsnorm(h, norm_final)


_drawn_inputs = setup_inputs


def setup_inputs(seed=0):
    import zlib

    import numpy as np

    out = dict(_drawn_inputs(seed))
    spreads = {}
    factors = {'attn_sinks': 7.524,
     'lru_b_a': 26.841,
     'lru_b_i': 20.209,
     'norm_ple': 17.572,
     'norm_final': 8.545}
    for name, (base, spread) in spreads.items():
        noise = np.random.default_rng([zlib.crc32(name.encode()), seed]).standard_normal(out[name].shape)
        drawn = base * np.exp(spread * noise) if base else spread * noise
        out[name] = __import__('jax').numpy.asarray(drawn.astype(out[name].dtype))
    for name, factor in factors.items():
        out[name] = (out[name] * factor).astype(out[name].dtype)
    return out
```

```python
from contextlib import ExitStack

import numpy as np

import concourse.bass as bass
from concourse import mybir

D_MODEL, SEQ, DEPTH, CHUNK = 1024, 256, 2, 64
A_HEADS, A_KV, A_DH = 8, 2, 64
B_HEADS, B_DH, C_WIDTH = 4, 128, 512
PLE_DIM = 256
HEADS, NKEYS, TOPK = 8, 128, 16
EPS = 1e-6
ROPE_THETA = 10000.0
LRU_C = 8.0
P = 128
KT = D_MODEL // P
MT_ = SEQ // P
RING = 6

STREAM = ([f"bqkv{i}" for i in range(6)] + ["aq0", "aq1", "akv", "cx0", "cx1", "bg0", "bg1"]
          + ["cy0", "cy1"] + [f"ga{i}" for i in range(4)] + [f"gb{i}" for i in range(4)]
          + [f"gc{i}" for i in range(4)] + ["lru"]
          + ["wa0", "wa1", "wb0", "wb1", "wc0", "wc1"] + [f"wo{i}" for i in range(4)]
          + [f"wq{i}" for i in range(8)] + ["keys"]
          + [f"u{i}" for i in range(64)] + [f"v{i}" for i in range(64)]
          + ["pp"] + [f"pg{i}" for i in range(4)])
NPAIR = len(STREAM)
assert NPAIR % RING == 0
AT = {name: n for n, name in enumerate(STREAM)}

UNIT = {"bqkv": 0, "aq": 12, "ak": 16, "av": 17, "cx": 18, "bg": 22, "cy": 26, "ga": 30, "gb": 38, "gc": 46}
NUNIT = 54
PROJ = STREAM[:27]

CONST = {}
_at = 0
for _name, _n in [("ident", P), ("ones", P), ("tri", P), ("blk", P), ("chunk", 2 * P), ("level", 6 * P),
                  ("rot", P), ("mask0", P), ("mask1", 2 * P), ("iota", P), ("freq", 1), ("sign", 1),
                  ("final", KT)]:
    CONST[_name] = (_at, _at + _n)
    _at += _n
NCONST = _at
SMALL = {}
_at = 0
for _name, _n in [("n_mix", KT), ("n_ffn", KT), ("n_ple", KT), ("bconv", 48), ("cconv", 16), ("cbias", 4),
                  ("ba", 4), ("bi", 4), ("lam", 4), ("dnorm", 1), ("sink", A_HEADS), ("alog", B_HEADS),
                  ("dt", B_HEADS), ("wba", KT * 8)]:
    SMALL[_name] = (_at, _at + _n)
    _at += _n
NSMALL = _at


def build_trunk(nc, stream, small_in, p_in, x_in, pos_in, const_in, out):
    f32, i32, u32 = mybir.dt.float32, mybir.dt.int32, mybir.dt.uint32
    ALU = mybir.AluOpType
    ACT = mybir.ActivationFunctionType
    AX = mybir.AxisListType.X
    ADD, SUB, MUL, MAX = ALU.add, ALU.subtract, ALU.mult, ALU.max
    ctx = ExitStack()
    with ctx:
        def sb(name, shape, dt=f32):
            return ctx.enter_context(nc.sbuf_tensor(name, shape, dt))

        ring = [sb(f"ring{i}", [P, 2048]) for i in range(RING)]
        h = sb("h", [P, KT, SEQ])
        n = sb("n", [P, KT, SEQ])
        big = sb("big", [P, 32768])
        const = sb("const", [P, NCONST])
        small = sb("small", [P, NSMALL])
        ple = sb("ple", [P, 2, SEQ])
        cos = sb("cos", [P, SEQ])
        sin = sb("sin", [P, SEQ])
        tiny = sb("tiny", [P, 320])
        eps = sb("eps", [P, 1])
        hot1 = sb("hot1", [P, 8, P])
        hot2 = sb("hot2", [P, 8, P])
        route = sb("route", [P, 3, SEQ])
        bank = [ctx.enter_context(nc.psum_tensor(f"bank{i}", [P, 512], f32)) for i in range(8)]

        def c(name):
            a, b = CONST[name]
            return const[:, a:b]

        def s(name):
            a, b = SMALL[name]
            return small[:, a:b]

        def area(at, *shape):
            size = int(np.prod(shape))
            v = big[:, at:at + size]
            if len(shape) == 2:
                v = v.rearrange("p (a b) -> p a b", a=shape[0])
            elif len(shape) == 3:
                v = v.rearrange("p (a b c) -> p a b c", a=shape[0], b=shape[1])
            return v

        def two(b):
            return bank[b][:, :].rearrange("p (u t) -> p u t", u=2)

        def four(b):
            return bank[b][:, :].rearrange("p (u t) -> p u t", u=4)

        ident, ones, tri = c("ident"), c("ones"), c("tri")

        z = area(0, NUNIT, SEQ)
        CV = NUNIT * SEQ
        cv = area(CV, 12, SEQ)
        sq = area(CV, KT, SEQ)
        F0 = CV + 12 * SEQ
        rms = area(F0, SEQ)
        rstd = area(F0 + SEQ, SEQ)
        qk = area(F0, 5, SEQ)
        sc0 = area(F0 + 1280, A_HEADS, P)
        sc1 = area(F0 + 2304, A_HEADS, SEQ)
        pt0 = area(F0 + 4352, A_HEADS, P)
        pt1 = area(F0 + 5376, 2, 1024)
        ropet = area(F0 + 4352, 5, SEQ)
        ya = area(12 * SEQ, 4, SEQ)
        xc = area(F0, 4, SEQ)
        lr = area(F0 + 1024, 4, SEQ)
        li = area(F0 + 2048, 4, SEQ)
        lt = area(F0 + 3072, 4, SEQ)
        lw = area(F0 + 4096, 4, SEQ)
        lroot = area(F0 + 5120, 4, SEQ)
        yc = area(18 * SEQ, 4, SEQ)
        G0 = F0 + 7424
        l2 = area(G0, 8, SEQ)
        egb = area(G0, 2, 512)
        dec = area(G0 + 1024, 2, 512)
        lo = area(G0 + 2048, 2, 512)
        qkd = area(G0 + 3072, 2, 512)
        ct = area(G0 + 4096, 2, 512)
        mm_ = area(G0 + 5120, 2, 512)
        mt = area(G0 + 6144, 2, 512)
        xx = area(G0 + 7168, 2, 512)
        vn = area(G0 + 5120, 512)
        state = area(G0 + 5632, 512)
        ob = area(1024, 4, SEQ)
        osq = area(2048, 4, SEQ)
        ors = area(0, 4, SEQ)
        vtok = area(16 * SEQ, 2, P)
        mix = area(CV, KT, SEQ)
        mixt = area(F0, 2, SEQ)
        assert G0 + 8192 <= 32768
        mix_tmp = area(G0, 512)
        act_h = area(0, NKEYS, SEQ)
        Q0 = 16384
        qt = area(Q0, 16, SEQ)
        sub = area(Q0 + 4096, 2, 2048)
        sub2 = area(Q0 + 8192, 2048)
        cand = area(Q0 + 12288, 2048)
        cand2 = area(Q0 + 14336, 2048)
        tops = area(Q0, 2, 256)
        topi = big[:, Q0 + 512:Q0 + 1024].bitcast(u32).rearrange("p (m k) -> p m k", m=2)
        topf = area(Q0 + 1024, 2, 256)
        best = area(Q0 + 1536, 2, P)
        besti = big[:, Q0 + 1792:Q0 + 2048].bitcast(u32).rearrange("p (m k) -> p m k", m=2)
        half = big[:, Q0 + 2048:Q0 + 2304].bitcast(u32).rearrange("p (m k) -> p m k", m=2)
        halff = area(Q0 + 2304, 2, P)
        picks = hot1[:, 0:6, :].rearrange("p (m k) c -> p m k c", m=2)
        gsum = area(Q0 + 3328, 2, HEADS)
        mx = tiny[:, 0:16].rearrange("p (m a) -> p m a", m=2)
        nmx = tiny[:, 16:32].rearrange("p (m a) -> p m a", m=2)
        den = tiny[:, 32:48].rearrange("p (m a) -> p m a", m=2)
        esink = tiny[:, 48:64].rearrange("p (m a) -> p m a", m=2)
        sp = tiny[:, 64:76]
        sa, se, ss, ssq, spo = (tiny[:, 76 + 12 * i:88 + 12 * i] for i in range(5))
        beta = tiny[:, 136:144].rearrange("p (m a) -> p m a", m=2)
        ag = tiny[:, 144:152].rearrange("p (m a) -> p m a", m=2)
        gs = tiny[:, 152:184].rearrange("p (m k a) -> p m k a", m=2, k=4)
        egs = tiny[:, 184:216].rearrange("p (m k a) -> p m k a", m=2, k=4)
        bg_ = tiny[:, 216:224].rearrange("p (m a) -> p m a", m=2)
        nea = tiny[:, 224:228]
        lrs = tiny[:, 228:232]

        def sem(name):
            return ctx.enter_context(nc.semaphore(name))

        slot = [sem(f"slot{i}") for i in range(RING)]
        names = """
            small_in used squares sums n_ready pj_free ba_full rot_full roped vtok_ready scores_full
            l2sq_ready masked l2_full normed pt_full l2_root pt_ready pv_full alpha_ready g_full ya_ready
            gcb_full bb_full qkn_ready g_dif kk_full dec_exp qk_full level_ready m_ready x_full x_ready
            qkd_ready p_full silu_ready tok_full tok_ready w_full w_ready qg_ready s_ready vn_full
            o_ready vn_ready o_full s_full xc_ready osq_ready osum_full lru_gates br_read sub_ready
            sub_full picks_ready tr_full hot_ready gates_full coef_ready achain h_new rms_ready
            conv_ready sp_in sp_exp rowmax_ready exps_ready g_exp dif_ready tanh_ready o_root lru_sqrt
            exp_in exp_out vchain yb_ready yc_ready rstd_ready""".split()
        S = {name: sem(name) for name in names}
        layer_sems = range(slot[0].num, S[names[-1]].num + 1)
        assert len(layer_sems) == RING + len(names)
        io = sem("io")
        setup = sem("setup")
        setup2 = sem("setup2")
        angle = sem("angle")
        trig = sem("trig")
        stored = sem("stored")
        stored_out = sem("stored_out")

        class Order:
            def __init__(self, engine, chain):
                self.engine, self.chain, self.n = engine, chain, 0

            def link(self, ins):
                self.n += 1
                ins.then_inc(self.chain, 1)
                self.engine.wait_ge(self.chain, self.n)

        with nc.Block() as block:
            @block.sync
            def _(sync):
                sync.dma_start(const[:, :], const_in).then_inc(io, 16)
                sync.dma_start(h[:, :, :], x_in).then_inc(io, 16)
                sync.dma_start(area(0, 256).bitcast(i32), pos_in.partition_broadcast(P)).then_inc(io, 16)
                sync.wait_ge(io, 48)

            @block.vector
            def _(dve):
                o = Order(dve, setup)
                ang, turns, rest, cosr = area(256, 256), area(512, 256), area(768, 256), area(1024, 256)
                dve.wait_ge(io, 48)
                o.link(nc.vector.tensor_copy(turns, area(0, 256).bitcast(i32)))
                o.link(nc.vector.tensor_scalar(ang, turns, c("freq"), None, MUL))
                o.link(nc.vector.tensor_scalar(turns, ang, float(1 / (2 * np.pi)), 12582912.0, MUL, ADD))
                o.link(nc.vector.tensor_scalar(turns, turns, -12582912.0, None, ADD))
                step1 = 6.28125
                step2 = round((2 * np.pi - step1) * 2 ** 20) / 2 ** 20
                step3 = float(2 * np.pi - step1 - step2)
                o.link(nc.vector.scalar_tensor_tensor(rest, turns, -step1, ang, MUL, ADD))
                o.link(nc.vector.scalar_tensor_tensor(rest, turns, -step2, rest, MUL, ADD))
                o.link(nc.vector.scalar_tensor_tensor(rest, turns, -step3, rest, MUL, ADD))
                o.link(nc.vector.tensor_scalar(cosr, rest, float(np.pi / 2), None, ADD))
                o.link(nc.vector.tensor_scalar(turns, cosr, float(np.pi), float(2 * np.pi), ALU.is_gt, MUL))
                o.link(nc.vector.tensor_tensor(cosr, cosr, turns, SUB))
                top = 3.1415925
                nc.vector.tensor_scalar(rest, rest, -top, top, MAX, ALU.min).then_inc(angle, 1)
                nc.vector.tensor_scalar(cosr, cosr, -top, top, MAX, ALU.min).then_inc(angle, 1)
                dve.wait_ge(trig, 2)
                nc.vector.tensor_scalar(sin[:, :], sin[:, :], c("sign"), None, MUL).then_inc(setup2, 1)
                dve.wait_ge(setup2, 1)

            @block.gpsimd
            def _(pool):
                nc.gpsimd.memset(eps[:, :], EPS).then_inc(stored, 1)
                pool.wait_ge(stored, 1)

            @block.scalar
            def _(act):
                act.wait_ge(angle, 2)
                nc.scalar.activation(sin[:, :], area(768, 256), ACT.Sin).then_inc(trig, 1)
                nc.scalar.activation(cos[:, :], area(1024, 256), ACT.Sin).then_inc(trig, 1)

        with nc.Fori(0, DEPTH) as layer:
            with nc.Block() as block:

                @block.sync
                def _(sync):
                    def load(i, pair):
                        sync.dma_start(ring[i][:, :], stream[pair]).then_inc(slot[i], 16)
                    sync.dma_start(small[:, :], small_in[layer]).then_inc(S["small_in"], 16)
                    sync.dma_start(ple[:, :, :], p_in[layer]).then_inc(S["small_in"], 16)
                    for i in range(RING):
                        load(i, layer * NPAIR + i)
                    with sync.Fori(1, NPAIR // RING) as lap:
                        for i in range(RING):
                            sync.wait_ge(S["used"], (lap - 1) * RING + (i + 1))
                            load(i, layer * NPAIR + lap * RING + i)

                @block.tensor
                def _(pe):
                    mmul = nc.tensor.matmul

                    def arrived(pair, lap=None):
                        i, k = pair % RING, 16 * (pair // RING + 1)
                        pe.wait_ge(slot[i], k if lap is None else lap * 16 + k)
                        return ring[i]


                    def norm_sums(k):
                        pe.wait_ge(S["squares"], k)
                        for t in range(KT):
                            last = mmul(bank[2][:, 0:SEQ], ones, sq[:, t, :], start=t == 0, stop=t == KT - 1)
                        last.then_inc(S["sums"], 1)
                        pe.wait_ge(S["n_ready"], k)

                    def project(name, use, lap=None):
                        pair = AT[name]
                        w = arrived(pair, lap)
                        if use >= 2:
                            pe.wait_ge(S["pj_free"], use - 1 if lap is None else lap * RING + (use - 1))
                        for u in range(2):
                            for t in range(KT):
                                at = (u * KT + t) * P
                                last = mmul(two(use % 2)[:, u, :], w[:, at:at + P], n[:, t, :],
                                            start=t == 0, stop=t == KT - 1)
                        last.then_inc(S["used"], 1)

                    use = iter(range(27))

                    def fill(name):
                        project(name, next(use))

                    def heads(m):
                        return [(hd, slice(hd * P, (hd + 1) * P)) for hd in range(B_HEADS)]

                    norm_sums(1)
                    for i in range(6):
                        fill(f"bqkv{i}")
                    wba = s("wba")
                    for m in range(MT_):
                        for t in range(KT):
                            last = mmul(bank[3][:, m * 8:(m + 1) * 8], n[:, t, m * P:(m + 1) * P],
                                        wba[:, t * 8:(t + 1) * 8], start=t == 0, stop=t == KT - 1)
                    last.then_inc(S["ba_full"], 1)
                    for name in ("aq0", "aq1", "akv", "cx0"):
                        fill(name)
                    pe.wait_ge(S["pj_free"], 9)
                    for u in range(5):
                        last = mmul(two(4 + u // 2)[:, u % 2, :], c("rot"), z[:, 12 + u, :], start=True, stop=True)
                    last.then_inc(S["rot_full"], 1)
                    for m in range(MT_):
                        last = nc.tensor.transpose(bank[7][:, m * P:(m + 1) * P], z[:, 17, m * P:(m + 1) * P], ident)
                    last.then_inc(S["rot_full"], 1)
                    for name in ("cx1", "bg0", "bg1", "cy0"):
                        fill(name)

                    pe.wait_ge(S["roped"], 1)
                    pe.wait_ge(S["vtok_ready"], 1)
                    for m in range(MT_):
                        for hd in range(A_HEADS):
                            half_ = slice(64 * (hd // 4), 64 * (hd // 4) + 64)
                            keys = (m + 1) * P
                            dst = four(2 + hd // 4)[:, hd % 4, :] if m == 0 else two(4 + hd // 2)[:, hd % 2, :]
                            last = mmul(dst, qk[half_, hd % 4, m * P:(m + 1) * P], qk[half_, 4, 0:keys],
                                        start=True, stop=True)
                        last.then_inc(S["scores_full"], 1)
                    fill("cy1")
                    pe.wait_ge(S["l2sq_ready"], 1)
                    pe.wait_ge(S["masked"], 6)
                    for b in range(4):
                        last = mmul(bank[2 + b][:, :], ones, l2[:, 2 * b:2 * b + 2, :], start=True, stop=True)
                    last.then_inc(S["l2_full"], 1)
                    fill("ga0")
                    pe.wait_ge(S["normed"], 1)
                    for hd in range(A_HEADS):
                        last = nc.tensor.transpose(four(6 + hd // 4)[:, hd % 4, :], sc0[:, hd, :], ident)
                    last.then_inc(S["pt_full"], 1)
                    pe.wait_ge(S["normed"], 2)
                    pe.wait_ge(S["l2_root"], 4)
                    for kt in range(MT_):
                        for hd in range(A_HEADS):
                            last = nc.tensor.transpose(four(2 + 2 * kt + hd // 4)[:, hd % 4, :],
                                                       sc1[:, hd, kt * P:(kt + 1) * P], ident)
                    last.then_inc(S["pt_full"], 1)
                    fill("ga1")
                    pe.wait_ge(S["pt_ready"], 6)
                    for g in range(A_KV):
                        mmul(bank[2 + g][:, :], vtok[:, 0, :], pt0[:, 4 * g:4 * g + 4, :], start=True, stop=True)
                        for kt in range(MT_):
                            last = mmul(bank[4 + g][:, :], vtok[:, kt, :], pt1[:, kt, g * 512:(g + 1) * 512],
                                        start=kt == 0, stop=kt == MT_ - 1)
                    last.then_inc(S["pv_full"], 1)
                    fill("ga2")

                    pe.wait_ge(S["alpha_ready"], 1)
                    for m in range(MT_):
                        chunk = c("chunk")
                        for k, w in enumerate((tri, c("blk"), chunk[:, 0:P], chunk[:, P:2 * P])):
                            at = m * 16 + k * 4
                            last = mmul(bank[6][:, at:at + 4], w, ag[:, m, :], start=True, stop=True)
                    last.then_inc(S["g_full"], 1)
                    pe.wait_ge(S["ya_ready"], 1)
                    for m, b in enumerate((7, 2)):
                        for hd, at in heads(m):
                            last = mmul(bank[b][:, at], ag[:, m, hd:hd + 1].to_broadcast([P, P]), tri,
                                        start=True, stop=True)
                    last.then_inc(S["gcb_full"], 1)
                    for m, b in enumerate((3, 4)):
                        for hd, at in heads(m):
                            last = mmul(bank[b][:, at], beta[:, m, hd:hd + 1].to_broadcast([P, P]), ident,
                                        start=True, stop=True)
                    last.then_inc(S["bb_full"], 1)
                    fill("ga3")
                    pe.wait_ge(S["qkn_ready"], 1)
                    pe.wait_ge(S["g_dif"], 1)
                    for m, b in enumerate((5, 6)):
                        for hd, at in heads(m):
                            k = cv[:, 4 + hd, m * P:(m + 1) * P]
                            last = mmul(bank[b][:, at], k, k, start=True, stop=True)
                    last.then_inc(S["kk_full"], 1)
                    pe.wait_ge(S["dec_exp"], 1)
                    for m, b in enumerate((7, 2)):
                        for hd, at in heads(m):
                            last = mmul(bank[b][:, at], cv[:, 4 + hd, m * P:(m + 1) * P],
                                        cv[:, hd, m * P:(m + 1) * P], start=True, stop=True)
                    last.then_inc(S["qk_full"], 1)
                    fill("gb0")
                    between = iter(("gb1", "gb2", "gb3", "gc0", "gc1"))
                    for level in range(6):
                        pe.wait_ge(S["level_ready"], level + 1)
                        if level:
                            pe.wait_ge(S["m_ready"], level)
                        for m, b in enumerate((3, 4)):
                            for hd, at in heads(m):
                                last = mmul(bank[b][:, at], ct[:, m, at], mm_[:, m, at] if level else ident,
                                            start=True, stop=True)
                        last.then_inc(S["x_full"], 1)
                        if not level:
                            continue
                        fill(next(between))
                        pe.wait_ge(S["x_ready"], 2 * level)
                        pe.wait_ge(S["qkd_ready"], 1)
                        if level < 5:
                            for m, b in enumerate((5, 6)):
                                for hd, at in heads(m):
                                    mmul(bank[b][:, at], mt[:, m, at], xx[:, m, at], start=True, stop=True)
                        for m, b in enumerate((7, 2)):
                            for hd, at in heads(m):
                                last = mmul(bank[b][:, at], xx[:, m, at], mt[:, m, at], start=True, stop=True)
                        last.then_inc(S["p_full"], 1)
                    pe.wait_ge(S["silu_ready"], 6)
                    for m in range(MT_):
                        for hd, at in heads(m):
                            nc.tensor.transpose(bank[3 + m][:, at], cv[:, 4 + hd, m * P:(m + 1) * P], ident)
                            last = nc.tensor.transpose(bank[5 + m][:, at], cv[:, 8 + hd, m * P:(m + 1) * P], ident)
                    last.then_inc(S["tok_full"], 1)
                    fill("gc2")
                    pe.wait_ge(S["m_ready"], 6)
                    pe.wait_ge(S["tok_ready"], 1)
                    for m, b in enumerate((7, 2)):
                        for hd, at in heads(m):
                            last = mmul(bank[b][:, at], ct[:, m, at], mt[:, m, at], start=True, stop=True)
                    last.then_inc(S["w_full"], 1)
                    pe.wait_ge(S["w_ready"], 2)
                    pe.wait_ge(S["qg_ready"], 1)
                    for ch in range(SEQ // CHUNK):
                        m, r = ch // 2, ch % 2
                        rows = slice(CHUNK * r, CHUNK * (r + 1))
                        if ch:
                            pe.wait_ge(S["s_ready"], ch)
                        for hd, at in heads(m):
                            dst = bank[3 + ch % 2][:, at]
                            last = mmul(dst, mt[:, m, at], xx[:, m, at], start=True, stop=not ch)
                            if ch:
                                last = mmul(dst, dec[:, m, at], state[:, at], start=False, stop=True)
                        last.then_inc(S["vn_full"], 1)
                        if ch >= 2:
                            pe.wait_ge(S["o_ready"], ch - 1)
                        pe.wait_ge(S["vn_ready"], ch + 1)
                        for hd, at in heads(m):
                            dst = bank[5 + ch % 2][:, hd * CHUNK:(hd + 1) * CHUNK]
                            mine = slice(hd * P + CHUNK * r, hd * P + CHUNK * (r + 1))
                            if ch:
                                mmul(dst, state[:, at], egb[:, m, mine], start=True, stop=False)
                            last = mmul(dst, vn[rows, at], qkd[rows, m, mine], start=not ch, stop=True)
                        last.then_inc(S["o_full"], 1)
                        if ch < 3:
                            for hd, at in heads(m):
                                last = mmul(bank[7][:, at], lo[rows, m, at], vn[rows, at], start=True, stop=True)
                            last.then_inc(S["s_full"], 1)
                        if ch == 0:
                            fill("gc3")

                    pe.wait_ge(S["xc_ready"], 1)
                    pe.wait_ge(S["o_ready"], 4)
                    w = arrived(AT["lru"])
                    for k in range(8):
                        last = mmul(two(3 + k // 2)[:, k % 2, :], w[:, k * P:(k + 1) * P], xc[:, k % 4, :],
                                    start=True, stop=True)
                    last.then_inc(S["used"], 1)
                    pe.wait_ge(S["osq_ready"], 1)
                    for k, b in enumerate((7, 2)):
                        last = mmul(bank[b][:, :], ones, osq[:, 2 * k:2 * k + 2, :], start=True, stop=True)
                    last.then_inc(S["osum_full"], 1)

                    for q, (name, y, ready) in enumerate((("wa0", ya, "ya_ready"), ("wa1", ya, "ya_ready"),
                                                          ("wb0", ob, "yb_ready"), ("wb1", ob, "yb_ready"),
                                                          ("wc0", yc, "yc_ready"), ("wc1", yc, "yc_ready"))):
                        w = arrived(AT[name])
                        pe.wait_ge(S[ready], 1)
                        if q < 2:
                            pe.wait_ge(S["lru_gates"], 8)
                        else:
                            pe.wait_ge(S["br_read"], q - 1)
                        for j in range(4):
                            for t in range(4):
                                at = (j * 4 + t) * P
                                last = mmul(two(3 + 2 * (q % 2) + j // 2)[:, j % 2, :], w[:, at:at + P], y[:, t, :],
                                            start=t == 0, stop=t == 3)
                        last.then_inc(S["used"], 1)
                    pe.wait_ge(S["br_read"], 6)
                    for i, b in enumerate((7, 2, 3, 4)):
                        w = arrived(AT[f"wo{i}"])
                        for u in range(2):
                            for t in range(KT):
                                at = (u * KT + t) * P
                                last = mmul(two(b)[:, u, :], w[:, at:at + P], mix[:, t, :],
                                            start=t == 0, stop=t == KT - 1)
                        last.then_inc(S["used"], 1)

                    norm_sums(2)
                    for i in range(8):
                        project(f"wq{i}", 27 + i)
                    w = arrived(AT["keys"])
                    pe.wait_ge(S["pj_free"], 35)
                    for m in range(MT_):
                        for hs in range(16):
                            b = 2 + (4 * m + hs // 4) % 6
                            if m and hs == 8:
                                pe.wait_ge(S["sub_ready"], 2)
                            last = mmul(four(b)[:, hs % 4, :], qt[:, hs, m * P:(m + 1) * P],
                                        w[:, hs * P:(hs + 1) * P], start=True, stop=True)
                        if m == 0:
                            last.then_inc(S["sub_full"], 1)
                    last.then_inc(S["used"], 1)
                    with pe.Fori(0, 10) as lap:
                        for i in range(RING):
                            project(f"u{i}", 35 + i, lap)
                    for i in range(60, 64):
                        project(f"u{i}", 35 + i)
                    pe.wait_ge(S["picks_ready"], 2)
                    pe.wait_ge(S["sub_ready"], 8)
                    for m in range(MT_):
                        for k in range(3):
                            last = nc.tensor.transpose(four(6 + m)[:, k, :], picks[:, m, k, :], ident)
                    last.then_inc(S["tr_full"], 1)
                    with pe.Fori(0, SEQ // 8) as it:
                        for g in range(2):
                            pe.wait_ge(S["hot_ready"], it * 2 + (g + 1))
                            for k in range(4):
                                last = mmul(four(6 + g)[:, k, :], hot1[:, 4 * g + k, :], hot2[:, 4 * g + k, :],
                                            start=True, stop=True)
                            last.then_inc(S["gates_full"], 1)
                    pe.wait_ge(S["coef_ready"], SEQ // 4)

                    def values(pair, j, lap=None, first=False, final=False):
                        w = arrived(pair, lap)
                        for e in range(2):
                            for t in range(KT):
                                at = (e * KT + t) * P
                                rhs = act_h[:, j + e, :] if lap is None else act_h[:, bass.ds(j + e, 1), :].squeeze(1)
                                last = mmul(two(2 + t // 2)[:, t % 2, :], w[:, at:at + P], rhs,
                                            start=first and not e and t % 2 == 0, stop=final and e == 1,
                                            skip_group_check=True)
                        last.then_inc(S["used"], 1)

                    values(AT["v0"], 0, first=True)
                    values(AT["v1"], 2)
                    with pe.Fori(0, 10) as lap:
                        for i in range(RING):
                            values(AT["v2"] + i, lap * (2 * RING) + (4 + 2 * i), lap)
                    values(AT["v62"], 124)
                    values(AT["v63"], 126, final=True)

                    norm_sums(3)
                    w = arrived(AT["pp"])
                    for t in range(KT):
                        for k in range(2):
                            at = (t * 2 + k) * P
                            last = mmul(two(2 + t // 2)[:, t % 2, :], w[:, at:at + P], ple[:, k, :],
                                        start=k == 0, stop=k == 1)
                    last.then_inc(S["used"], 1)
                    for i in range(4):
                        project(f"pg{i}", 99 + i)

                @block.scalar
                def _(act):
                    A = nc.scalar.activation
                    o = Order(act, S["achain"])

                    def used(name, lap=None):
                        k = AT[name] + 1
                        act.wait_ge(S["used"], k if lap is None else lap * RING + k)

                    def empty(name, use, out_, func, lap=None):
                        used(name, lap)
                        A(out_, two(use % 2), func).then_inc(S["pj_free"], 1)

                    use = iter(range(27))

                    def fill(name):
                        k = next(use)
                        func = ACT.Copy if k < 11 else ACT.Silu if k < 13 else ACT.Gelu_apprx_tanh if k < 15 else ACT.Sigmoid
                        empty(name, k, z[:, 2 * k:2 * k + 2, :], func)

                    def root_mean_square(k):
                        if k > 1:
                            act.wait_ge(S["h_new"], 4 * (k - 1))
                        A(sq[:, :, :], h[:, :, :], ACT.Square).then_inc(S["squares"], 1)
                        act.wait_ge(S["sums"], k)
                        A(rms, bank[2][:, 0:SEQ], ACT.Sqrt, scale=1.0 / D_MODEL, bias=eps[:, :]).then_inc(S["rms_ready"], 1)

                    root_mean_square(1)
                    for name in STREAM[:11]:
                        fill(name)
                    for name in STREAM[11:13]:
                        fill(name)
                    for i in range(6):
                        act.wait_ge(S["conv_ready"], i + 1)
                        A(cv[:, 2 * i:2 * i + 2, :], cv[:, 2 * i:2 * i + 2, :], ACT.Silu).then_inc(S["silu_ready"], 1)
                        if i == 3:
                            act.wait_ge(S["silu_ready"], 4)
                            A(l2[:, :, :], cv[:, 0:8, :], ACT.Square).then_inc(S["l2sq_ready"], 1)
                    act.wait_ge(S["sp_in"], 1)
                    A(nea, s("alog"), ACT.Exp).then_inc(S["sp_exp"], 1)
                    A(se, sa, ACT.Exp, scale=-1.0).then_inc(S["sp_exp"], 1)
                    A(beta, beta, ACT.Exp, scale=-1.0).then_inc(S["sp_exp"], 1)
                    act.wait_ge(S["roped"], 1)
                    act.wait_ge(S["rot_full"], 2)
                    A(vtok[:, :, :], bank[7][:, 0:2 * P].rearrange("p (m c) -> p m c", m=2), ACT.Copy)\
                        .then_inc(S["vtok_ready"], 1)
                    fill("cy0")
                    act.wait_ge(S["rowmax_ready"], 1)
                    for m, sc in ((0, sc0), (1, sc1)):
                        for hd in range(A_HEADS):
                            A(sc[:, hd, :], sc[:, hd, :], ACT.Exp, bias=nmx[:, m, hd:hd + 1],
                              accum_out=den[:, m, hd:hd + 1]).then_inc(S["exps_ready"], 1)
                    A(esink, esink, ACT.Exp).then_inc(S["exps_ready"], 1)
                    fill("cy1")
                    act.wait_ge(S["l2_full"], 1)
                    for b in range(4):
                        A(l2[:, 2 * b:2 * b + 2, :], two(2 + b), ACT.Sqrt, bias=eps[:, :]).then_inc(S["l2_root"], 1)
                    fill("ga0")
                    act.wait_ge(S["pt_full"], 1)
                    for b in range(2):
                        A(pt0[:, 4 * b:4 * b + 4, :], four(6 + b), ACT.Copy).then_inc(S["pt_ready"], 1)
                    act.wait_ge(S["pt_full"], 2)
                    for b in range(4):
                        A(pt1[:, b // 2, (b % 2) * 512:(b % 2 + 1) * 512], bank[2 + b][:, :], ACT.Copy)\
                            .then_inc(S["pt_ready"], 1)
                    fill("ga1")
                    fill("ga2")
                    act.wait_ge(S["g_dif"], 1)
                    A(egs, gs, ACT.Exp).then_inc(S["g_exp"], 1)
                    act.wait_ge(S["dif_ready"], 1)
                    A(dec[:, :, :], dec[:, :, :], ACT.Exp)
                    A(egb[:, 0, :], bank[7][:, :], ACT.Exp)
                    A(egb[:, 1, :], bank[2][:, :], ACT.Exp).then_inc(S["dec_exp"], 1)
                    fill("ga3")
                    fill("gb0")
                    for level, name in zip(range(1, 6), ("gb1", "gb2", "gb3", "gc0", "gc1")):
                        act.wait_ge(S["x_full"], level + 1)
                        for m in range(MT_):
                            A(xx[:, m, :], bank[3 + m][:, :], ACT.Copy).then_inc(S["x_ready"], 1)
                        fill(name)
                    fill("gc2")
                    act.wait_ge(S["w_full"], 1)
                    for m, b in enumerate((7, 2)):
                        A(dec[:, m, :], bank[b][:, :], ACT.Copy, scale=-1.0).then_inc(S["w_ready"], 1)
                    for ch in range(SEQ // CHUNK):
                        act.wait_ge(S["o_full"], ch + 1)
                        A(ob[:, :, ch * CHUNK:(ch + 1) * CHUNK],
                          bank[5 + ch % 2][:, 0:256].rearrange("p (a i) -> p a i", a=4), ACT.Copy)\
                            .then_inc(S["o_ready"], 1)
                        if ch == 0:
                            fill("gc3")
                    act.wait_ge(S["o_ready"], 4)
                    A(osq[:, :, :], ob[:, :, :], ACT.Square).then_inc(S["osq_ready"], 1)
                    used("lru")
                    for k, dst, b in [(k, lr, "ba") for k in range(4)] + [(k, li, "bi") for k in range(4)]:
                        src = two((3 if b == "ba" else 5) + k // 2)[:, k % 2, :]
                        A(dst[:, k, :], src, ACT.Sigmoid, bias=s(b)[:, k:k + 1]).then_inc(S["lru_gates"], 1)
                    act.wait_ge(S["lru_gates"], 4)
                    for k in range(4):
                        A(lt[:, k, :], lr[:, k, :], ACT.Tanh, scale=lrs[:, k:k + 1]).then_inc(S["tanh_ready"], 1)
                    act.wait_ge(S["osum_full"], 1)
                    for k, b in enumerate((7, 2)):
                        A(ors[:, 2 * k:2 * k + 2, :], two(b), ACT.Sqrt, scale=1.0 / B_DH, bias=eps[:, :])\
                            .then_inc(S["o_root"], 1)
                    act.wait_ge(S["tanh_ready"], 4)
                    A(lroot[:, :, :], lt[:, :, :], ACT.Sqrt).then_inc(S["lru_sqrt"], 1)

                    root_mean_square(2)
                    for i in range(8):
                        empty(f"wq{i}", 27 + i, qt[:, 2 * i:2 * i + 2, :], ACT.Copy)
                    act.wait_ge(S["sub_full"], 1)
                    for k in range(8):
                        if k == 4:
                            used("keys")
                        A(sub[:, k // 4, (k % 4) * 512:(k % 4 + 1) * 512], bank[2 + k % 6][:, :], ACT.Copy)\
                            .then_inc(S["sub_ready"], 1)

                    def gelus(i, lap=None, done=0):
                        q = 2 * i if lap is None else lap * (2 * RING) + 2 * (done + i)
                        dst = act_h[:, q:q + 2, :] if lap is None else act_h[:, bass.ds(q, 2), :]
                        empty(f"u{done + i}", 35 + done + i, dst, ACT.Gelu_apprx_tanh, lap)

                    with act.Fori(0, 5) as lap:
                        for i in range(RING):
                            gelus(i, lap)
                    act.wait_ge(S["exp_in"], 1)
                    A(picks[:, :, 2, :], picks[:, :, 2, :], ACT.Exp).then_inc(S["exp_out"], 1)
                    act.wait_ge(S["picks_ready"], 2)
                    with act.Fori(0, 5) as lap:
                        for i in range(RING):
                            gelus(i, lap, 30)
                    for i in range(60, 64):
                        gelus(i)

                    root_mean_square(3)
                    for i in range(4):
                        empty(f"pg{i}", 99 + i, z[:, 2 * i:2 * i + 2, :], ACT.Sigmoid)

                @block.vector
                def _(dve):
                    V = nc.vector
                    o = Order(dve, S["vchain"])
                    TS, TT, STT = V.tensor_scalar, V.tensor_tensor, V.scalar_tensor_tensor

                    def over(ap, count):
                        return ap.unsqueeze(1).to_broadcast([P, count, ap.shape[1]])

                    def along(ap, count):
                        return ap.unsqueeze(2).to_broadcast([P, ap.shape[1], count])

                    def normalise(k, weight):
                        dve.wait_ge(S["rms_ready"], k)
                        o.link(V.reciprocal(rstd, rms))
                        for t in range(KT):
                            last = STT(n[:, t, :], h[:, t, :], s(weight)[:, t:t + 1], rstd, MUL, MUL)
                        last.then_inc(S["n_ready"], 1)

                    def conv(dst, src, w, bias=None):
                        units = range(len(src))
                        for u in units:
                            last = TS(dst[u], src[u], w[u][3], None, MUL) if bias is None else \
                                TS(dst[u], src[u], w[u][3], bias[u], MUL, ADD)
                        for tap in (2, 1, 0):
                            o.link(last)
                            back = 3 - tap
                            for u in units:
                                last = STT(dst[u][:, back:], src[u][:, :SEQ - back], w[u][tap], dst[u][:, back:], MUL, ADD)
                        return last

                    dve.wait_ge(S["small_in"], 32)
                    normalise(1, "n_mix")

                    for i in range(6):
                        dve.wait_ge(S["pj_free"], i + 1)
                        us = (2 * i, 2 * i + 1)
                        w = s("bconv")
                        conv([cv[:, u, :] for u in us], [z[:, u, :] for u in us],
                             [[w[:, 4 * u + k:4 * u + k + 1] for k in range(4)] for u in us]).then_inc(S["conv_ready"], 1)
                    dve.wait_ge(S["ba_full"], 1)
                    for m in range(MT_):
                        V.tensor_copy(beta[:, m, :], bank[3][:, m * 8:m * 8 + 4])
                        TT(sp[:, 4 * m:4 * m + 4], bank[3][:, m * 8 + 4:m * 8 + 8], s("dt"), ADD)
                    o.link(TS(sp[:, 8:12], s("lam"), -1.0, None, MUL))
                    STT(sa, sp, -1.0, sp, MUL, MAX).then_inc(S["sp_in"], 1)
                    dve.wait_ge(S["sp_exp"], 3)
                    o.link(TS(ss, se, 2.0, None, ADD))
                    o.link(V.reciprocal(ss, ss))
                    o.link(TT(ss, ss, se, MUL))
                    o.link(TT(ssq, ss, ss, MUL))
                    o.link(TS(spo, ssq, 1.0 / 17, None, MUL))
                    for k in range(7, 0, -1):
                        o.link(STT(spo, spo, 1.0 / (2 * k + 1), ssq, ADD, MUL))
                    o.link(STT(spo, spo, 1.0, ss, ADD, MUL))
                    o.link(TS(spo, spo, 2.0, None, MUL))
                    o.link(STT(sp, sp, 0.0, spo, MAX, ADD))
                    o.link(TS(beta, beta, 1.0, None, ADD))
                    V.reciprocal(beta, beta)
                    V.tensor_scalar(lrs, sp[:, 8:12], LRU_C / 2, None, MUL)
                    for m in range(MT_):
                        last = STT(ag[:, m, :], sp[:, 4 * m:4 * m + 4], -1.0, nea, MUL, MUL)
                    last.then_inc(S["alpha_ready"], 1)

                    dve.wait_ge(S["rot_full"], 1)
                    TT(ropet[:, 0:2, :], two(4), over(sin[:, :], 2), MUL)
                    TT(ropet[:, 2:4, :], two(5), over(sin[:, :], 2), MUL)
                    TT(ropet[:, 4, :], bank[6][:, 0:SEQ], sin[:, :], MUL)
                    o.link(TT(qk[:, :, :], z[:, 12:17, :], over(cos[:, :], 5), MUL))
                    TT(qk[:, :, :], qk[:, :, :], ropet[:, :, :], ADD).then_inc(S["roped"], 1)
                    scale = float(A_DH) ** -0.5
                    dve.wait_ge(S["scores_full"], 1)
                    for b in range(2):
                        STT(sc0[:, 4 * b:4 * b + 4, :], four(2 + b), scale, over(c("mask0"), 4), MUL, ADD)\
                            .then_inc(S["masked"], 1)
                    dve.wait_ge(S["scores_full"], 2)
                    for b in range(4):
                        STT(sc1[:, 2 * b:2 * b + 2, :], two(4 + b), scale, over(c("mask1"), 2), MUL, ADD)\
                            .then_inc(S["masked"], 1)
                    dve.wait_ge(S["masked"], 6)
                    V.tensor_reduce(mx[:, 0, :], sc0[:, :, :], AX, MAX)
                    o.link(V.tensor_reduce(mx[:, 1, :], sc1[:, :, :], AX, MAX))
                    o.link(TT(mx, mx, over(s("sink"), 2), MAX))
                    TS(nmx, mx, -1.0, None, MUL)
                    TT(esink, over(s("sink"), 2), mx, SUB).then_inc(S["rowmax_ready"], 1)
                    dve.wait_ge(S["exps_ready"], 17)
                    o.link(TT(den, den, esink, ADD))
                    o.link(V.reciprocal(den, den))
                    TT(sc0[:, :, :], sc0[:, :, :], along(den[:, 0, :], P), MUL).then_inc(S["normed"], 1)
                    TT(sc1[:, :, :], sc1[:, :, :], along(den[:, 1, :], SEQ), MUL).then_inc(S["normed"], 1)
                    dve.wait_ge(S["l2_root"], 4)
                    o.link(V.reciprocal(l2[:, :, :], l2[:, :, :]))
                    dve.wait_ge(S["silu_ready"], 4)
                    STT(cv[:, 0:4, :], cv[:, 0:4, :], float(B_DH) ** -0.5, l2[:, 0:4, :], MUL, MUL)
                    TT(cv[:, 4:8, :], cv[:, 4:8, :], l2[:, 4:8, :], MUL).then_inc(S["qkn_ready"], 1)
                    dve.wait_ge(S["pv_full"], 1)
                    for m in range(MT_):
                        for g in range(A_KV):
                            mine = slice(64 * g, 64 * g + 64)
                            last = V.tensor_copy(ya[mine, :, m * P:(m + 1) * P], four(2 + 2 * m + g)[mine, :, :])
                    last.then_inc(S["ya_ready"], 1)

                    dve.wait_ge(S["g_full"], 1)
                    o.link(V.tensor_copy(gs, bank[6][:, 0:32].rearrange("p (m k a) -> p m k a", m=2, k=4)))
                    TT(gs[:, :, 1, :], gs[:, :, 1, :], gs[:, :, 0, :], SUB).then_inc(S["g_dif"], 1)
                    dve.wait_ge(S["gcb_full"], 1)
                    for m, b in enumerate((7, 2)):
                        for hd in range(B_HEADS):
                            at = slice(hd * P, (hd + 1) * P)
                            last = TS(dec[:, m, at], bank[b][:, at], gs[:, m, 0, hd:hd + 1], 0.0, SUB, ALU.min)
                    last.then_inc(S["dif_ready"], 1)
                    dve.wait_ge(S["g_exp"], 1)
                    TT(bg_, beta, egs[:, :, 0, :], MUL)
                    dve.wait_ge(S["dec_exp"], 1)
                    heads8 = dec[:, :, :].rearrange("p m (a i) -> p (m a) i", i=P)
                    o.link(TT(heads8, heads8, over(tri, 8), MUL))
                    dve.wait_ge(S["kk_full"], 1)
                    dve.wait_ge(S["bb_full"], 1)
                    for m in range(MT_):
                        last = TT(lo[:, m, :], bank[5 + m][:, :], dec[:, m, :], MUL)
                    o.link(last)
                    for m in range(MT_):
                        last = TT(lo[:, m, :], bank[3 + m][:, :], lo[:, m, :], MUL)
                    o.link(last)
                    lo8, ct8, mt8 = (x[:, :, :].rearrange("p m (a i) -> p (m a) i", i=P) for x in (lo, ct, mt))

                    def part(level):
                        mask = c("level")[:, level * P:(level + 1) * P]
                        TT(ct8, lo8, over(mask, 8), MUL).then_inc(S["level_ready"], 1)

                    part(0)
                    dve.wait_ge(S["qk_full"], 1)
                    for m, b in enumerate((7, 2)):
                        last = TT(qkd[:, m, :], bank[b][:, :], dec[:, m, :], MUL)
                    last.then_inc(S["qkd_ready"], 1)
                    dve.wait_ge(S["level_ready"], 1)
                    o.link(STT(mt8, ct8, -1.0, over(ident, 8), MUL, ADD))
                    dve.wait_ge(S["x_full"], 1)
                    for m in range(MT_):
                        last = STT(mm_[:, m, :].rearrange("p (a i) -> p a i", i=P), four(3 + m), -1.0,
                                   over(ident, 4), MUL, ADD)
                    last.then_inc(S["m_ready"], 1)
                    part(1)
                    for level in range(1, 6):
                        dve.wait_ge(S["x_full"], level + 1)
                        if level < 5:
                            part(level + 1)
                        dve.wait_ge(S["p_full"], level)
                        if level < 5:
                            for m in range(MT_):
                                TT(mm_[:, m, :], mm_[:, m, :], bank[5 + m][:, :], SUB)
                        for m, b in enumerate((7, 2)):
                            last = TT(mt[:, m, :], mt[:, m, :], bank[b][:, :], SUB)
                        last.then_inc(S["m_ready"], 1)
                    for m in range(MT_):
                        e = egb[:, m, :].rearrange("p (a i) -> p a i", i=P)
                        last = TT(e, cv[:, 0:4, m * P:(m + 1) * P], e, MUL)
                    last.then_inc(S["qg_ready"], 1)
                    dve.wait_ge(S["tok_full"], 1)
                    for m in range(MT_):
                        def by_head(x):
                            return x[:, m, :].rearrange("p (a i) -> p a i", i=P)
                        TT(by_head(ct), four(3 + m), along(bg_[:, m, :], P), MUL)
                        TT(by_head(lo), four(3 + m), along(egs[:, m, 1, :], P), MUL)
                        last = TT(by_head(xx), four(5 + m), along(beta[:, m, :], P), MUL)
                    last.then_inc(S["tok_ready"], 1)
                    w, b = s("cconv"), s("cbias")
                    conv([xc[:, u, :] for u in range(4)], [z[:, 18 + u, :] for u in range(4)],
                         [[w[:, 4 * u + k:4 * u + k + 1] for k in range(4)] for u in range(4)],
                         [b[:, u:u + 1] for u in range(4)]).then_inc(S["xc_ready"], 1)
                    for ch in range(SEQ // CHUNK):
                        m, r = ch // 2, ch % 2
                        rows = slice(CHUNK * r, CHUNK * (r + 1))
                        dve.wait_ge(S["vn_full"], ch + 1)
                        V.tensor_copy(vn[rows, :], bank[3 + ch % 2][rows, :]).then_inc(S["vn_ready"], 1)
                        if ch == 3:
                            break
                        dve.wait_ge(S["s_full"], ch + 1)
                        if not ch:
                            last = V.tensor_copy(state, bank[7][:, :])
                        else:
                            for hd in range(B_HEADS):
                                at = slice(hd * P, (hd + 1) * P)
                                last = STT(state[:, at], state[:, at], egs[:, m, 2 + r, hd:hd + 1], bank[7][:, at],
                                           MUL, ADD)
                        last.then_inc(S["s_ready"], 1)
                        dve.wait_ge(S["s_ready"], ch + 1)
                    dve.wait_ge(S["lru_gates"], 8)
                    TT(li[:, :, :], li[:, :, :], xc[:, :, :], MUL)
                    dve.wait_ge(S["tanh_ready"], 4)
                    TS(lr[:, :, :], lt[:, :, :], -1.0, 1.0, MUL, ADD)
                    o.link(TS(lw[:, :, :], lt[:, :, :], 1.0, None, ADD))
                    o.link(V.reciprocal(lw[:, :, :], lw[:, :, :]))
                    dve.wait_ge(S["o_root"], 2)
                    o.link(V.reciprocal(ors[:, :, :], ors[:, :, :]))
                    o.link(STT(ob[:, :, :], ob[:, :, :], s("dnorm"), ors[:, :, :], MUL, MUL))
                    TT(ob[:, :, :], ob[:, :, :], z[:, 22:26, :], MUL).then_inc(S["yb_ready"], 1)
                    TT(lr[:, :, :], lr[:, :, :], lw[:, :, :], MUL)
                    dve.wait_ge(S["lru_sqrt"], 1)
                    o.link(TT(lt[:, :, :], lroot[:, :, :], lw[:, :, :], MUL))
                    o.link(STT(li[:, :, :], li[:, :, :], 2.0, lt[:, :, :], MUL, MUL))
                    for u in range(4):
                        last = V.tensor_tensor_scan(xc[:, u, :], lr[:, u, :], li[:, u, :], 0.0, MUL, ADD)
                    o.link(last)
                    TT(yc[:, :, :], xc[:, :, :], z[:, 26:30, :], MUL).then_inc(S["yc_ready"], 1)

                    for q, name in enumerate(("wa0", "wa1", "wb0", "wb1", "wc0", "wc1")):
                        dve.wait_ge(S["used"], AT[name] + 1)
                        for k in range(2):
                            t = 4 * (q % 2) + 2 * k
                            gate = z[:, 30 + 8 * (q // 2) + t:32 + 8 * (q // 2) + t, :]
                            src = two(3 + 2 * (q % 2) + k)
                            if q < 2:
                                last = TT(mix[:, t:t + 2, :], src, gate, MUL)
                            else:
                                o.link(TT(mixt, src, gate, MUL))
                                last = TT(mix[:, t:t + 2, :], mix[:, t:t + 2, :], mixt, ADD)
                                if k == 0:
                                    o.link(last)
                        last.then_inc(S["br_read"], 1)
                        dve.wait_ge(S["br_read"], q + 1)
                    for i, bk in enumerate((7, 2, 3, 4)):
                        dve.wait_ge(S["used"], AT[f"wo{i}"] + 1)
                        TT(h[:, 2 * i:2 * i + 2, :], h[:, 2 * i:2 * i + 2, :], two(bk), ADD).then_inc(S["h_new"], 1)
                    normalise(2, "n_ffn")

                    def best16(values, rest, top, index):
                        all_ = range(len(values))
                        for k in all_:
                            last = V.max(top[k][:, 0:8], values[k])
                        o.link(last)
                        for k in all_:
                            V.max_index(index[k][:, 0:8], top[k][:, 0:8], values[k])
                            last = V.match_replace(rest[k], top[k][:, 0:8], values[k], -3.4028235e38)
                        o.link(last)
                        for k in all_:
                            last = V.max(top[k][:, 8:16], rest[k])
                        o.link(last)
                        for k in all_:
                            last = V.max_index(index[k][:, 8:16], top[k][:, 8:16], rest[k])
                        o.link(last)

                    def cut(x, size, count):
                        return [x[:, k * size:(k + 1) * size] for k in range(count)]

                    dve.wait_ge(S["sub_ready"], 8)
                    iota16 = c("iota")[:, 0:TOPK]
                    shape4 = [P, HEADS, TOPK, TOPK]
                    for m in range(MT_):
                        best16(cut(sub[:, m, :], P, 16), cut(sub2, P, 16),
                               cut(tops[:, m, :], TOPK, 16), cut(topi[:, m, :], TOPK, 16))
                        V.tensor_copy(topf[:, m, :], topi[:, m, :])
                        sides = tops[:, m, :].rearrange("p (h s k) -> p h s k", s=2, k=TOPK)
                        pairs = cand.rearrange("p (h a b) -> p h a b", a=TOPK, b=TOPK)
                        o.link(TT(pairs, sides[:, :, 0, :].unsqueeze(3).to_broadcast(shape4),
                                  sides[:, :, 1, :].unsqueeze(2).to_broadcast(shape4), ADD))
                        best16(cut(cand, 256, HEADS), cut(cand2, 256, HEADS),
                               cut(best[:, m, :], TOPK, HEADS), cut(besti[:, m, :], TOPK, HEADS))
                        keys_ = topf[:, m, :].rearrange("p (h s k) -> p h s k", s=2, k=TOPK)
                        for side in range(2):
                            if side == 0:
                                o.link(TS(half[:, m, :], besti[:, m, :], 4, None, ALU.logical_shift_right))
                            else:
                                o.link(TS(half[:, m, :], besti[:, m, :], 15, None, ALU.bitwise_and))
                            o.link(V.tensor_copy(halff[:, m, :], half[:, m, :]))
                            flat = cand.rearrange("p (k c) -> p k c", c=TOPK)
                            o.link(TT(flat, along(halff[:, m, :], TOPK), over(iota16, P), ALU.is_equal))
                            o.link(TT(pairs, pairs, keys_[:, :, side, :].unsqueeze(2).to_broadcast(shape4), MUL))
                            o.link(V.tensor_reduce(picks[:, m, side, :], flat, AX, ADD))
                        bests = best[:, m, :].rearrange("p (h k) -> p h k", k=TOPK)
                        gate = picks[:, m, 2, :].rearrange("p (h k) -> p h k", k=TOPK)
                        last = TT(gate, bests, bests[:, :, 0:1].to_broadcast([P, HEADS, TOPK]), SUB)
                        if m == 0:
                            o.link(last)
                    last.then_inc(S["exp_in"], 1)
                    dve.wait_ge(S["exp_out"], 1)
                    for m in range(MT_):
                        gate = picks[:, m, 2, :].rearrange("p (h k) -> p h k", k=TOPK)
                        o.link(V.tensor_reduce(gsum[:, m, :], gate, AX, ADD))
                        o.link(V.reciprocal(gsum[:, m, :], gsum[:, m, :]))
                        TT(gate, gate, along(gsum[:, m, :], TOPK), MUL).then_inc(S["picks_ready"], 1)
                    dve.wait_ge(S["tr_full"], 1)
                    for m in range(MT_):
                        last = V.tensor_copy(route[:, :, m * P:(m + 1) * P], four(6 + m)[:, 0:3, :])
                    o.link(last)
                    dve.wait_ge(S["pj_free"], 99)
                    by_token = act_h[:, :, :].rearrange("p j t -> p t j")
                    with dve.Fori(0, SEQ // 8) as it:
                        for g in range(2):
                            for k in range(4):
                                at = it * 8 + (4 * g + k)
                                TS(hot1[:, 4 * g + k, :], c("iota"), route[:, 0, bass.ds(at, 1)],
                                   route[:, 2, bass.ds(at, 1)], ALU.is_equal, MUL)
                                last = TS(hot2[:, 4 * g + k, :], c("iota"), route[:, 1, bass.ds(at, 1)], None,
                                          ALU.is_equal)
                            last.then_inc(S["hot_ready"], 1)
                        for g in range(2):
                            dve.wait_ge(S["gates_full"], it * 2 + (g + 1))
                            coefs = by_token[:, bass.ds(it * 8 + 4 * g, 4), :]
                            TT(coefs, four(6 + g), coefs, MUL).then_inc(S["coef_ready"], 1)
                    dve.wait_ge(S["used"], AT["v63"] + 1)
                    for i in range(4):
                        TT(h[:, 2 * i:2 * i + 2, :], h[:, 2 * i:2 * i + 2, :], two(2 + i), ADD).then_inc(S["h_new"], 1)
                    normalise(3, "n_ple")
                    dve.wait_ge(S["used"], AT["pp"] + 1)
                    for i in range(4):
                        dve.wait_ge(S["pj_free"], 100 + i)
                        o.link(TT(mixt, two(2 + i), z[:, 2 * i:2 * i + 2, :], MUL))
                        last = TT(h[:, 2 * i:2 * i + 2, :], h[:, 2 * i:2 * i + 2, :], mixt, ADD)
                        last.then_inc(S["h_new"], 1)
                        dve.wait_ge(S["h_new"], 9 + i)

            nc.all_engine_barrier(sems_to_clear=layer_sems)

        with nc.Block() as block:
            @block.scalar
            def _(act):
                nc.scalar.activation(sq[:, :, :], h[:, :, :], ACT.Square).then_inc(S["squares"], 1)
                act.wait_ge(S["sums"], 1)
                nc.scalar.activation(rms, bank[2][:, 0:SEQ], ACT.Sqrt, scale=1.0 / D_MODEL, bias=eps[:, :])\
                    .then_inc(S["rms_ready"], 1)

            @block.tensor
            def _(pe):
                pe.wait_ge(S["squares"], 1)
                for t in range(KT):
                    last = nc.tensor.matmul(bank[2][:, 0:SEQ], ones, sq[:, t, :], start=t == 0, stop=t == KT - 1)
                last.then_inc(S["sums"], 1)

            @block.vector
            def _(dve):
                dve.wait_ge(S["rms_ready"], 1)
                nc.vector.reciprocal(rstd, rms).then_inc(S["rstd_ready"], 1)
                dve.wait_ge(S["rstd_ready"], 1)
                for t in range(KT):
                    nc.vector.scalar_tensor_tensor(n[:, t, :], h[:, t, :], c("final")[:, t:t + 1], rstd, MUL, MUL)\
                        .then_inc(S["n_ready"], 1)

            @block.sync
            def _(sync):
                for half_ in range(2):
                    sync.wait_ge(S["n_ready"], 4 * half_ + 4)
                    sync.dma_start(out[:, 4 * half_:4 * half_ + 4, :], n[:, 4 * half_:4 * half_ + 4, :])\
                        .then_inc(stored_out, 16)
                sync.wait_ge(stored_out, 32)


def constants():
    p = np.arange(P)
    f = np.float32
    chunk = p // CHUNK
    same = chunk[:, None] == chunk[None, :]
    out = np.zeros((P, NCONST), f)

    def put(name, value):
        a, b = CONST[name]
        out[:, a:b] = value
    put("ident", np.eye(P))
    put("ones", 1.0)
    put("tri", same & (p[:, None] <= p[None, :]))
    put("blk", same)
    put("chunk", np.repeat(chunk[:, None] == np.arange(2)[None, :], P, axis=1))
    levels = []
    for level in range(6):
        size = 1 << level
        levels.append((p[:, None] // (2 * size) == p[None, :] // (2 * size))
                      & (p[:, None] // size % 2 == 0) & (p[None, :] // size % 2 == 1))
    put("level", np.concatenate(levels, 1))
    half = A_DH // 2
    partner = p // A_DH * A_DH + (p + half) % A_DH
    put("rot", p[:, None] == partner[None, :])
    for m, name in enumerate(("mask0", "mask1")):
        q, k = (m * P + p)[:, None] // CHUNK, np.arange((m + 1) * P)[None, :] // CHUNK
        put(name, np.where((k == q) | (k == q - 1), 0.0, -1e30))
    put("iota", p[None, :])
    put("freq", (ROPE_THETA ** (-np.arange(half, dtype=f) / f(half))).astype(f)[p % half][:, None])
    put("sign", np.where(p % A_DH < half, -1.0, 1.0)[:, None])
    return out


def units(w):
    k, m = w.shape
    return w.reshape(k // P, P, m // P, P).transpose(2, 1, 0, 3)


def pairs(u):
    return u.reshape(-1, 2, P, 1024).transpose(0, 2, 1, 3).reshape(-1, P, 2048)


def lay_out(x, p, positions, norm_mix, w_in, attn_sinks, dn_conv, dn_a_log, dn_dt_bias, dn_norm, lru_conv_w,
            lru_conv_b, lru_w_a, lru_b_a, lru_w_i, lru_b_i, lru_lambda, w_branch_a, w_branch_b, w_branch_c,
            w_out, norm_ffn, peer_w_q, peer_sub_keys, peer_u, peer_v, norm_ple, ple_w_gate, ple_w_proj,
            norm_final):
    const = constants()
    const[:, slice(*CONST["final"])] = norm_final.reshape(KT, P).T
    order = np.concatenate([np.arange(hd * A_DH, (hd + 1) * A_DH) for i in range(4) for hd in (i, 4 + i)])
    sizes = [512, 128, 128, 1536, 4, 4, 512, 512, 512, 1024, 1024, 1024]
    stream = np.empty((DEPTH * NPAIR, P, 2048), np.float32)
    small = np.zeros((DEPTH, P, NSMALL), np.float32)
    for l in range(DEPTH):
        aq, ak, av, bqkv, bbeta, balpha, bgate, cx, cy, ga, gb, gc = np.split(w_in[l], np.cumsum(sizes)[:-1], axis=1)
        base = l * NPAIR

        def put(name, value):
            at = base + AT[name]
            stream[at:at + len(value)] = value
        main = np.concatenate([bqkv, aq[:, order], ak, av, cx, bgate, cy, ga, gb, gc], axis=1)
        put("bqkv0", pairs(units(main)))
        lru = np.zeros((P, 16, P), np.float32)
        for i, w in enumerate((lru_w_a[l], lru_w_i[l])):
            for t in range(4):
                for e in range(2):
                    lru[64 * e:64 * e + 64, 4 * i + t, 64 * e:64 * e + 64] = w[2 * t + e]
        put("lru", lru.reshape(1, P, 2048))
        for name, w in (("wa0", w_branch_a[l][order]), ("wb0", w_branch_b[l]), ("wc0", w_branch_c[l])):
            put(name, units(w).reshape(2, 4, P, 512).transpose(0, 2, 1, 3).reshape(2, P, 2048))
        put("wo0", pairs(units(w_out[l])))
        put("wq0", pairs(units(peer_w_q[l])))
        put("keys", peer_sub_keys[l].transpose(3, 0, 1, 2).reshape(1, P, 2048))
        put("u0", pairs(peer_u[l].reshape(NKEYS, NKEYS, KT, P).transpose(1, 3, 2, 0)))
        put("v0", pairs(peer_v[l].reshape(NKEYS, NKEYS, D_MODEL).transpose(1, 0, 2)))
        put("pp", units(ple_w_proj[l]).transpose(1, 0, 2, 3).reshape(1, P, 2048))
        put("pg0", pairs(units(ple_w_gate[l])))

        def col(name, value):
            a, b = SMALL[name]
            small[l, :, a:b] = value
        col("n_mix", norm_mix[l].reshape(KT, P).T)
        col("n_ffn", norm_ffn[l].reshape(KT, P).T)
        col("n_ple", norm_ple[l].reshape(KT, P).T)
        col("bconv", dn_conv[l].reshape(4, 12, P).transpose(2, 1, 0).reshape(P, 48))
        col("cconv", lru_conv_w[l].reshape(4, 4, P).transpose(2, 1, 0).reshape(P, 16))
        col("cbias", lru_conv_b[l].reshape(4, P).T)
        col("ba", lru_b_a[l].reshape(4, P).T)
        col("bi", lru_b_i[l].reshape(4, P).T)
        col("lam", lru_lambda[l].reshape(4, P).T)
        col("dnorm", dn_norm[l][:, None])
        col("sink", attn_sinks[l][None, :])
        col("alog", dn_a_log[l][None, :])
        col("dt", dn_dt_bias[l][None, :])
        col("wba", np.concatenate([bbeta, balpha], 1).reshape(KT, P, 8).transpose(1, 0, 2).reshape(P, 64))
    return {
        "stream": stream,
        "small": small,
        "p": np.ascontiguousarray(p[:, 0].transpose(0, 2, 1).reshape(DEPTH, 2, P, SEQ).transpose(0, 2, 1, 3)),
        "x": np.ascontiguousarray(x[0].T.reshape(KT, P, SEQ).transpose(1, 0, 2)),
        "positions": np.ascontiguousarray(positions[0]),
        "const": const,
    }


def kernel(**inputs):
    import concourse.bacc as _bacc
    from concourse.bass_utils import run_bass_kernel_spmd as _run

    arrays = lay_out(**{k: np.asarray(v) for k, v in inputs.items()})
    nc = _bacc.Bacc("TRN2", target_bir_lowering=False, num_devices=1, dynamic_dma_scratch_size=1024)
    aps = {name: nc.dram_tensor(f"in_{name}", a.shape, mybir.dt.from_np(a.dtype), kind="ExternalInput").ap()
           for name, a in arrays.items()}
    out = nc.dram_tensor("out", (P, KT, SEQ), mybir.dt.float32, kind="ExternalOutput").ap()
    build_trunk(nc, aps["stream"], aps["small"], aps["p"], aps["x"], aps["positions"], aps["const"], out)
    r = _run(nc, [{f"in_{k}": v for k, v in arrays.items()}], core_ids=[0])
    got = r.results[0]["out"]
    return np.ascontiguousarray(got.transpose(2, 1, 0).reshape(1, SEQ, D_MODEL))
```

```python
from contextlib import ExitStack

import numpy as np

import concourse.bass as bass
from concourse import mybir

D_MODEL, SEQ, DEPTH, CHUNK = 1024, 256, 2, 64
A_HEADS, A_KV, A_DH = 8, 2, 64
B_HEADS, B_DH, C_WIDTH = 4, 128, 512
PLE_DIM = 256
HEADS, NKEYS, TOPK = 8, 128, 16
EPS = 1e-6
ROPE_THETA = 10000.0
LRU_C = 8.0
P = 128
KT = D_MODEL // P
MT_ = SEQ // P
RING = 4
HIGHS = 2

STREAM = ([f"bqkv{i}" for i in range(6)] + ["aq0", "aq1", "akv", "cx0", "cx1", "bg0", "bg1"]
          + ["cy0", "cy1"] + [f"ga{i}" for i in range(4)] + [f"gb{i}" for i in range(4)]
          + [f"gc{i}" for i in range(4)] + ["lru"]
          + ["wa0", "wa1", "wb0", "wb1", "wc0", "wc1"] + [f"wo{i}" for i in range(4)]
          + [f"wq{i}" for i in range(8)] + ["keys"]
          + [f"u{i}" for i in range(64)] + [f"v{i}" for i in range(64)]
          + ["pp"] + [f"pg{i}" for i in range(4)])
NPAIR = len(STREAM)
assert NPAIR % RING == 0
AT = {name: n for n, name in enumerate(STREAM)}

UNIT = {"bqkv": 0, "aq": 12, "ak": 16, "av": 17, "cx": 18, "bg": 22, "cy": 26, "ga": 30, "gb": 38, "gc": 46}
NUNIT = 54
WHOLE = [AT[name] for name in ("lru", "keys", "pp")]


def split_units(pair, unit=0):
    return 2 * (pair - sum(w < pair for w in WHOLE)) + unit + 1


MOVING, _at = {}, 0
for _name, _n in [("norm1", 4), ("ya", 2), ("ob", 2), ("yc", 2), ("mix", 4), ("norm2", 4), ("coef", 64), ("norm3", 4)]:
    MOVING[_name] = _at
    _at += _n

CONST = {}
_at = 0
for _name, _n in [("ident", P), ("ones", P), ("tri", P), ("blk", P), ("chunk", 2 * P), ("level", 6 * P),
                  ("rot", P), ("mask0", P), ("mask1", 2 * P), ("iota", P), ("freq", 1), ("sign", 1),
                  ("final", KT)]:
    CONST[_name] = (_at, _at + _n)
    _at += _n
NCONST = _at
SMALL = {}
_at = 0
for _name, _n in [("n_mix", KT), ("n_ffn", KT), ("n_ple", KT), ("bconv", 48), ("cconv", 16), ("cbias", 4),
                  ("ba", 4), ("bi", 4), ("lam", 4), ("dnorm", 1), ("sink", A_HEADS), ("alog", B_HEADS),
                  ("dt", B_HEADS), ("wba", KT * 8)]:
    SMALL[_name] = (_at, _at + _n)
    _at += _n
NSMALL = _at


def build_trunk(nc, stream, small_in, p_in, x_in, pos_in, const_in, out):
    f32, f32r, i32, u32 = mybir.dt.float32, mybir.dt.float32r, mybir.dt.int32, mybir.dt.uint32
    ALU = mybir.AluOpType
    ACT = mybir.ActivationFunctionType
    AX = mybir.AxisListType.X
    ADD, SUB, MUL, MAX = ALU.add, ALU.subtract, ALU.mult, ALU.max
    ctx = ExitStack()
    with ctx:
        start_of = {}

        def sb(name, shape, dt=f32):
            start_of[name] = (nc.sbuf_base + 31) // 32 * 32
            return ctx.enter_context(nc.sbuf_tensor(name, shape, dt))

        def over_(name, shape, dt, under, words=0):
            return nc.alloc_sbuf_tensor_at(name, shape, dt, offset=start_of[under] + 4 * words)

        ring = [sb(f"ring{i}", [P, 2048]) for i in range(RING)]
        low = [over_(f"low{i}", [P, 2048], f32r, f"ring{i}") for i in range(RING)]
        high = [sb(f"high{i}", [P, 2048], f32r) for i in range(HIGHS)]
        h = sb("h", [P, KT, SEQ])
        n = sb("n", [P, KT, SEQ])
        n_low = over_("n_low", [P, KT, SEQ], f32r, "n")
        n_high = sb("n_high", [P, KT, SEQ], f32r)
        big = sb("big", [P, 32768])
        const = sb("const", [P, NCONST])
        small = sb("small", [P, NSMALL])
        ple = sb("ple", [P, 2, SEQ])
        cos = sb("cos", [P, SEQ])
        sin = sb("sin", [P, SEQ])
        tiny = sb("tiny", [P, 320])
        eps = sb("eps", [P, 1])
        hot1 = over_("hot1", [P, 16, P], f32, "n_high")
        hot2 = over_("hot2", [P, 16, P], f32, "n")
        picks_ = sb("picks", [P, 6, P])
        route = sb("route", [P, 3, SEQ])
        bank = [ctx.enter_context(nc.psum_tensor(f"bank{i}", [P, 512], f32)) for i in range(8)]

        def c(name):
            a, b = CONST[name]
            return const[:, a:b]

        def s(name):
            a, b = SMALL[name]
            return small[:, a:b]

        def area(at, *shape):
            size = int(np.prod(shape))
            v = big[:, at:at + size]
            if len(shape) == 2:
                v = v.rearrange("p (a b) -> p a b", a=shape[0])
            elif len(shape) == 3:
                v = v.rearrange("p (a b c) -> p a b c", a=shape[0], b=shape[1])
            return v

        def two(b):
            return bank[b][:, :].rearrange("p (u t) -> p u t", u=2)

        def four(b):
            return bank[b][:, :].rearrange("p (u t) -> p u t", u=4)

        ident, ones, tri = c("ident"), c("ones"), c("tri")

        z = area(0, NUNIT, SEQ)
        CV = NUNIT * SEQ
        cv = area(CV, 12, SEQ)
        sq = area(CV, KT, SEQ)
        F0 = CV + 12 * SEQ
        rms = area(F0, SEQ)
        rstd = area(F0 + SEQ, SEQ)
        qk = area(F0, 5, SEQ)
        sc0 = area(F0 + 1280, A_HEADS, P)
        sc1 = area(F0 + 2304, A_HEADS, SEQ)
        pt0 = area(F0 + 4352, A_HEADS, P)
        pt1 = area(F0 + 5376, 2, 1024)
        ropet = area(F0 + 4352, 5, SEQ)
        ya = area(12 * SEQ, 4, SEQ)
        xc = area(F0, 4, SEQ)
        lr = area(F0 + 1024, 4, SEQ)
        li = area(F0 + 2048, 4, SEQ)
        lt = area(F0 + 3072, 4, SEQ)
        lw = area(F0 + 4096, 4, SEQ)
        lroot = area(F0 + 5120, 4, SEQ)
        yc = area(18 * SEQ, 4, SEQ)
        G0 = F0 + 7424
        l2 = area(G0, 8, SEQ)
        egb = area(G0, 2, 512)
        dec = area(G0 + 1024, 2, 512)
        lo = area(G0 + 2048, 2, 512)
        qkd = area(G0 + 3072, 2, 512)
        ct = area(G0 + 4096, 2, 512)
        mm_ = area(G0 + 5120, 2, 512)
        mt = area(G0 + 6144, 2, 512)
        xx = area(G0 + 7168, 2, 512)
        vn = area(G0 + 5120, 512)
        state = area(G0 + 5632, 512)
        ob = area(1024, 4, SEQ)
        osq = area(2048, 4, SEQ)
        ors = area(0, 4, SEQ)
        vtok = area(16 * SEQ, 2, P)
        mix = area(CV, KT, SEQ)
        mixt = area(F0, 2, SEQ)
        assert G0 + 8192 <= 32768
        yc_high = over_("yc_high", [P, 4, SEQ], f32r, "big", G0)
        yc_low = over_("yc_low", [P, 4, SEQ], f32r, "big", G0 + 1024)
        act_h = area(0, NKEYS, SEQ)
        Q0 = 16384
        qt = area(Q0, 16, SEQ)
        sub = area(Q0 + 4096, 2, 2048)
        sub2 = area(Q0 + 8192, 2048)
        cand = area(Q0 + 12288, 2048)
        cand2 = area(Q0 + 14336, 2048)
        tops = area(Q0, 2, 256)
        topi = big[:, Q0 + 512:Q0 + 1024].bitcast(u32).rearrange("p (m k) -> p m k", m=2)
        topf = area(Q0 + 1024, 2, 256)
        best = area(Q0 + 1536, 2, P)
        besti = big[:, Q0 + 1792:Q0 + 2048].bitcast(u32).rearrange("p (m k) -> p m k", m=2)
        half = big[:, Q0 + 2048:Q0 + 2304].bitcast(u32).rearrange("p (m k) -> p m k", m=2)
        halff = area(Q0 + 2304, 2, P)
        picks = picks_[:, :, :].rearrange("p (m k) c -> p m k c", m=2)
        gsum = area(Q0 + 3328, 2, HEADS)
        mx = tiny[:, 0:16].rearrange("p (m a) -> p m a", m=2)
        nmx = tiny[:, 16:32].rearrange("p (m a) -> p m a", m=2)
        den = tiny[:, 32:48].rearrange("p (m a) -> p m a", m=2)
        esink = tiny[:, 48:64].rearrange("p (m a) -> p m a", m=2)
        sp = tiny[:, 64:76]
        sa, se, ss, ssq, spo = (tiny[:, 76 + 12 * i:88 + 12 * i] for i in range(5))
        beta = tiny[:, 136:144].rearrange("p (m a) -> p m a", m=2)
        ag = tiny[:, 144:152].rearrange("p (m a) -> p m a", m=2)
        gs = tiny[:, 152:184].rearrange("p (m k a) -> p m k a", m=2, k=4)
        egs = tiny[:, 184:216].rearrange("p (m k a) -> p m k a", m=2, k=4)
        bg_ = tiny[:, 216:224].rearrange("p (m a) -> p m a", m=2)
        nea = tiny[:, 224:228]
        lrs = tiny[:, 228:232]

        GROUPS = SEQ // 4
        GATE_BANKS = (6, 7, 0, 1)
        PLE_BANKS = (6, 7, 0, 1)

        def sem(name):
            return ctx.enter_context(nc.semaphore(name))

        slot = [sem(f"slot{i}") for i in range(RING)]
        names = """
            small_in used low_ready x_low squares sums pj_free ba_full rot_full roped vtok_ready
            scores_full l2sq_ready masked l2_full normed pt_full l2_root pt_ready pv_full alpha_ready
            g_full ya_ready gcb_full bb_full qkn_ready g_dif kk_full dec_exp qk_full level_ready m_ready
            x_full x_ready qkd_ready p_full silu_ready tok_full tok_ready w_full w_ready qg_ready s_ready
            vn_full o_ready vn_ready o_full s_full xc_ready osq_ready osum_full lru_gates br_read
            sub_ready sub_full picks_ready tr_full hot1_ready hot2_ready coef_ready gates_full achain
            high_ready x_high n_ready h_new rms_ready conv_ready sp_in sp_exp rowmax_ready exps_ready
            g_exp dif_ready tanh_ready o_root lru_sqrt yb_ready yc_ready exp_in exp_out route_ready
            distance ones_ready vchain rstd_ready""".split()
        S = {name: sem(name) for name in names}
        layer_sems = range(slot[0].num, S[names[-1]].num + 1)
        assert len(layer_sems) == RING + len(names)
        io = sem("io")
        setup = sem("setup")
        setup2 = sem("setup2")
        angle = sem("angle")
        trig = sem("trig")
        stored = sem("stored")
        stored_out = sem("stored_out")

        class Order:
            def __init__(self, engine, chain):
                self.engine, self.chain, self.n = engine, chain, 0

            def link(self, ins):
                self.n += 1
                ins.then_inc(self.chain, 1)
                self.engine.wait_ge(self.chain, self.n)

        with nc.Block() as block:
            @block.sync
            def _(sync):
                sync.dma_start(const[:, :], const_in).then_inc(io, 16)
                sync.dma_start(h[:, :, :], x_in).then_inc(io, 16)
                sync.dma_start(area(0, 256).bitcast(i32), pos_in.partition_broadcast(P)).then_inc(io, 16)
                sync.wait_ge(io, 48)

            @block.vector
            def _(dve):
                o = Order(dve, setup)
                ang, turns, rest, cosr = area(256, 256), area(512, 256), area(768, 256), area(1024, 256)
                dve.wait_ge(io, 48)
                o.link(nc.vector.tensor_copy(turns, area(0, 256).bitcast(i32)))
                o.link(nc.vector.tensor_scalar(ang, turns, c("freq"), None, MUL))
                o.link(nc.vector.tensor_scalar(turns, ang, float(1 / (2 * np.pi)), 12582912.0, MUL, ADD))
                o.link(nc.vector.tensor_scalar(turns, turns, -12582912.0, None, ADD))
                step1 = 6.28125
                step2 = round((2 * np.pi - step1) * 2 ** 20) / 2 ** 20
                step3 = float(2 * np.pi - step1 - step2)
                o.link(nc.vector.scalar_tensor_tensor(rest, turns, -step1, ang, MUL, ADD))
                o.link(nc.vector.scalar_tensor_tensor(rest, turns, -step2, rest, MUL, ADD))
                o.link(nc.vector.scalar_tensor_tensor(rest, turns, -step3, rest, MUL, ADD))
                o.link(nc.vector.tensor_scalar(cosr, rest, float(np.pi / 2), None, ADD))
                o.link(nc.vector.tensor_scalar(turns, cosr, float(np.pi), float(2 * np.pi), ALU.is_gt, MUL))
                o.link(nc.vector.tensor_tensor(cosr, cosr, turns, SUB))
                top = 3.1415925
                nc.vector.tensor_scalar(rest, rest, -top, top, MAX, ALU.min).then_inc(angle, 1)
                nc.vector.tensor_scalar(cosr, cosr, -top, top, MAX, ALU.min).then_inc(angle, 1)
                dve.wait_ge(trig, 2)
                nc.vector.tensor_scalar(sin[:, :], sin[:, :], c("sign"), None, MUL).then_inc(setup2, 1)
                dve.wait_ge(setup2, 1)

            @block.gpsimd
            def _(pool):
                nc.gpsimd.memset(eps[:, :], EPS).then_inc(stored, 1)
                pool.wait_ge(stored, 1)

            @block.scalar
            def _(act):
                act.wait_ge(angle, 2)
                nc.scalar.activation(sin[:, :], area(768, 256), ACT.Sin).then_inc(trig, 1)
                nc.scalar.activation(cos[:, :], area(1024, 256), ACT.Sin).then_inc(trig, 1)

        with nc.Fori(0, DEPTH) as layer:
            with nc.Block() as block:

                @block.sync
                def _(sync):
                    def load(i, pair):
                        sync.dma_start(ring[i][:, :], stream[pair]).then_inc(slot[i], 16)
                    sync.dma_start(small[:, :], small_in[layer]).then_inc(S["small_in"], 16)
                    sync.dma_start(ple[:, :, :], p_in[layer]).then_inc(S["small_in"], 16)
                    for i in range(RING):
                        load(i, layer * NPAIR + i)
                    with sync.Fori(1, NPAIR // RING) as lap:
                        for i in range(RING):
                            sync.wait_ge(S["used"], (lap - 1) * (2 * RING) + 2 * (i + 1))
                            load(i, layer * NPAIR + lap * RING + i)

                @block.tensor
                def _(pe):
                    mmul = nc.tensor.matmul

                    def arrived(pair, lap=None):
                        i, k = pair % RING, 16 * (pair // RING + 1)
                        pe.wait_ge(slot[i], k if lap is None else lap * 16 + k)
                        return ring[i]

                    def parts(pair, unit, lap=None):
                        k = split_units(pair, unit)
                        pe.wait_ge(S["low_ready"], k if lap is None else lap * (2 * RING) + k)
                        return high[pair % HIGHS], low[pair % RING]

                    def moving(name, step=None):
                        pe.wait_ge(S["x_low"], MOVING[name] + step + 1)

                    def product(dst, w, at, x_high, x_low, first, final, loose=False):
                        w_high, w_low = w[0][:, at:at + P], w[1][:, at:at + P]
                        mmul(dst, w_high, x_high, start=first, stop=False, skip_group_check=loose)
                        mmul(dst, w_high, x_low, start=False, stop=False, skip_group_check=loose)
                        return mmul(dst, w_low, x_high, start=False, stop=final, skip_group_check=loose)

                    def norm_sums(k, b=6):
                        for t in range(KT):
                            if t % 2 == 0:
                                pe.wait_ge(S["squares"], 4 * (k - 1) + t // 2 + 1)
                            last = mmul(bank[b][:, 0:SEQ], ones, sq[:, t, :], start=t == 0, stop=t == KT - 1)
                        last.then_inc(S["sums"], 1)

                    def project(name, use, lap=None, fresh=None, base=0):
                        pair = AT[name]
                        for u in range(2):
                            w = parts(pair, u, lap)
                            if use >= 2 and not u:
                                pe.wait_ge(S["pj_free"], use - 1 if lap is None else lap * RING + (use - 1))
                            for t in range(KT):
                                if fresh and not u and t % 2 == 0:
                                    moving(fresh, t // 2)
                                last = product(two(base + use % 2)[:, u, :], w, (u * KT + t) * P,
                                               n_high[:, t, :], n_low[:, t, :], t == 0, t == KT - 1)
                            last.then_inc(S["used"], 1)

                    use = iter(range(27))

                    def fill(name):
                        project(name, next(use))

                    def heads(m):
                        return [(hd, slice(hd * P, (hd + 1) * P)) for hd in range(B_HEADS)]

                    norm_sums(1)
                    project("bqkv0", next(use), fresh="norm1")
                    for i in range(1, 6):
                        fill(f"bqkv{i}")
                    wba = s("wba")
                    for m in range(MT_):
                        for t in range(KT):
                            for k, part_ in enumerate((n_high, n_low)):
                                last = mmul(bank[3][:, m * 8:(m + 1) * 8],
                                            part_[:, t, m * P:(m + 1) * P].bitcast(f32), wba[:, t * 8:(t + 1) * 8],
                                            start=not t and not k, stop=t == KT - 1 and k == 1)
                    last.then_inc(S["ba_full"], 1)
                    for name in ("aq0", "aq1", "akv", "cx0"):
                        fill(name)
                    pe.wait_ge(S["pj_free"], 9)
                    for u in range(5):
                        last = mmul(two(4 + u // 2)[:, u % 2, :], c("rot"), z[:, 12 + u, :], start=True, stop=True)
                    last.then_inc(S["rot_full"], 1)
                    for m in range(MT_):
                        last = nc.tensor.transpose(bank[7][:, m * P:(m + 1) * P], z[:, 17, m * P:(m + 1) * P], ident)
                    last.then_inc(S["rot_full"], 1)
                    for name in ("cx1", "bg0", "bg1", "cy0"):
                        fill(name)

                    pe.wait_ge(S["roped"], 1)
                    pe.wait_ge(S["vtok_ready"], 1)
                    for m in range(MT_):
                        for hd in range(A_HEADS):
                            half_ = slice(64 * (hd // 4), 64 * (hd // 4) + 64)
                            keys = (m + 1) * P
                            dst = four(2 + hd // 4)[:, hd % 4, :] if m == 0 else two(4 + hd // 2)[:, hd % 2, :]
                            last = mmul(dst, qk[half_, hd % 4, m * P:(m + 1) * P], qk[half_, 4, 0:keys],
                                        start=True, stop=True)
                        last.then_inc(S["scores_full"], 1)
                    fill("cy1")
                    pe.wait_ge(S["l2sq_ready"], 1)
                    pe.wait_ge(S["masked"], 6)
                    for b in range(4):
                        last = mmul(bank[2 + b][:, :], ones, l2[:, 2 * b:2 * b + 2, :], start=True, stop=True)
                    last.then_inc(S["l2_full"], 1)
                    fill("ga0")
                    pe.wait_ge(S["normed"], 1)
                    for hd in range(A_HEADS):
                        last = nc.tensor.transpose(four(6 + hd // 4)[:, hd % 4, :], sc0[:, hd, :], ident)
                    last.then_inc(S["pt_full"], 1)
                    pe.wait_ge(S["normed"], 2)
                    pe.wait_ge(S["l2_root"], 4)
                    for kt in range(MT_):
                        for hd in range(A_HEADS):
                            last = nc.tensor.transpose(four(2 + 2 * kt + hd // 4)[:, hd % 4, :],
                                                       sc1[:, hd, kt * P:(kt + 1) * P], ident)
                    last.then_inc(S["pt_full"], 1)
                    fill("ga1")
                    pe.wait_ge(S["pt_ready"], 6)
                    for g in range(A_KV):
                        mmul(bank[2 + g][:, :], vtok[:, 0, :], pt0[:, 4 * g:4 * g + 4, :], start=True, stop=True)
                        for kt in range(MT_):
                            last = mmul(bank[4 + g][:, :], vtok[:, kt, :], pt1[:, kt, g * 512:(g + 1) * 512],
                                        start=kt == 0, stop=kt == MT_ - 1)
                    last.then_inc(S["pv_full"], 1)
                    fill("ga2")

                    pe.wait_ge(S["alpha_ready"], 1)
                    for m in range(MT_):
                        chunk = c("chunk")
                        for k, w in enumerate((tri, c("blk"), chunk[:, 0:P], chunk[:, P:2 * P])):
                            at = m * 16 + k * 4
                            last = mmul(bank[6][:, at:at + 4], w, ag[:, m, :], start=True, stop=True)
                    last.then_inc(S["g_full"], 1)
                    pe.wait_ge(S["ya_ready"], 1)
                    for m, b in enumerate((7, 2)):
                        for hd, at in heads(m):
                            last = mmul(bank[b][:, at], ag[:, m, hd:hd + 1].to_broadcast([P, P]), tri,
                                        start=True, stop=True)
                    last.then_inc(S["gcb_full"], 1)
                    for m, b in enumerate((3, 4)):
                        for hd, at in heads(m):
                            last = mmul(bank[b][:, at], beta[:, m, hd:hd + 1].to_broadcast([P, P]), ident,
                                        start=True, stop=True)
                    last.then_inc(S["bb_full"], 1)
                    fill("ga3")
                    pe.wait_ge(S["qkn_ready"], 1)
                    pe.wait_ge(S["g_dif"], 1)
                    for m, b in enumerate((5, 6)):
                        for hd, at in heads(m):
                            k = cv[:, 4 + hd, m * P:(m + 1) * P]
                            last = mmul(bank[b][:, at], k, k, start=True, stop=True)
                    last.then_inc(S["kk_full"], 1)
                    pe.wait_ge(S["dec_exp"], 1)
                    for m, b in enumerate((7, 2)):
                        for hd, at in heads(m):
                            last = mmul(bank[b][:, at], cv[:, 4 + hd, m * P:(m + 1) * P],
                                        cv[:, hd, m * P:(m + 1) * P], start=True, stop=True)
                    last.then_inc(S["qk_full"], 1)
                    fill("gb0")
                    between = iter(("gb1", "gb2", "gb3", "gc0", "gc1"))
                    for level in range(6):
                        pe.wait_ge(S["level_ready"], level + 1)
                        if level:
                            pe.wait_ge(S["m_ready"], level)
                        for m, b in enumerate((3, 4)):
                            for hd, at in heads(m):
                                last = mmul(bank[b][:, at], ct[:, m, at], mm_[:, m, at] if level else ident,
                                            start=True, stop=True)
                        last.then_inc(S["x_full"], 1)
                        if not level:
                            continue
                        fill(next(between))
                        pe.wait_ge(S["x_ready"], 2 * level)
                        pe.wait_ge(S["qkd_ready"], 1)
                        if level < 5:
                            for m, b in enumerate((5, 6)):
                                for hd, at in heads(m):
                                    mmul(bank[b][:, at], mt[:, m, at], xx[:, m, at], start=True, stop=True)
                        for m, b in enumerate((7, 2)):
                            for hd, at in heads(m):
                                last = mmul(bank[b][:, at], xx[:, m, at], mt[:, m, at], start=True, stop=True)
                        last.then_inc(S["p_full"], 1)
                    pe.wait_ge(S["silu_ready"], 6)
                    for m in range(MT_):
                        for hd, at in heads(m):
                            nc.tensor.transpose(bank[3 + m][:, at], cv[:, 4 + hd, m * P:(m + 1) * P], ident)
                            last = nc.tensor.transpose(bank[5 + m][:, at], cv[:, 8 + hd, m * P:(m + 1) * P], ident)
                    last.then_inc(S["tok_full"], 1)
                    fill("gc2")
                    pe.wait_ge(S["m_ready"], 6)
                    pe.wait_ge(S["tok_ready"], 1)
                    for m, b in enumerate((7, 2)):
                        for hd, at in heads(m):
                            last = mmul(bank[b][:, at], ct[:, m, at], mt[:, m, at], start=True, stop=True)
                    last.then_inc(S["w_full"], 1)
                    pe.wait_ge(S["w_ready"], 2)
                    pe.wait_ge(S["qg_ready"], 1)
                    for ch in range(SEQ // CHUNK):
                        m, r = ch // 2, ch % 2
                        rows = slice(CHUNK * r, CHUNK * (r + 1))
                        if ch:
                            pe.wait_ge(S["s_ready"], ch)
                        for hd, at in heads(m):
                            dst = bank[3 + ch % 2][:, at]
                            last = mmul(dst, mt[:, m, at], xx[:, m, at], start=True, stop=not ch)
                            if ch:
                                last = mmul(dst, dec[:, m, at], state[:, at], start=False, stop=True)
                        last.then_inc(S["vn_full"], 1)
                        if ch >= 2:
                            pe.wait_ge(S["o_ready"], ch - 1)
                        pe.wait_ge(S["vn_ready"], ch + 1)
                        for hd, at in heads(m):
                            dst = bank[5 + ch % 2][:, hd * CHUNK:(hd + 1) * CHUNK]
                            mine = slice(hd * P + CHUNK * r, hd * P + CHUNK * (r + 1))
                            if ch:
                                mmul(dst, state[:, at], egb[:, m, mine], start=True, stop=False)
                            last = mmul(dst, vn[rows, at], qkd[rows, m, mine], start=not ch, stop=True)
                        last.then_inc(S["o_full"], 1)
                        if ch < 3:
                            for hd, at in heads(m):
                                last = mmul(bank[7][:, at], lo[rows, m, at], vn[rows, at], start=True, stop=True)
                            last.then_inc(S["s_full"], 1)
                        if ch == 0:
                            fill("gc3")

                    pe.wait_ge(S["xc_ready"], 1)
                    pe.wait_ge(S["o_ready"], 4)
                    w = arrived(AT["lru"])
                    for k in range(8):
                        last = mmul(two(3 + k // 2)[:, k % 2, :], w[:, k * P:(k + 1) * P], xc[:, k % 4, :],
                                    start=True, stop=True)
                    last.then_inc(S["used"], 2)
                    pe.wait_ge(S["osq_ready"], 1)
                    for k, b in enumerate((7, 2)):
                        last = mmul(bank[b][:, :], ones, osq[:, 2 * k:2 * k + 2, :], start=True, stop=True)
                    last.then_inc(S["osum_full"], 1)

                    y_parts = {"ya": (n_high[:, 0:4, :], n_low[:, 0:4, :]), "ob": (n_high[:, 4:8, :], n_low[:, 4:8, :]),
                               "yc": (yc_high, yc_low)}
                    for q, (name, y) in enumerate((("wa0", "ya"), ("wa1", "ya"), ("wb0", "ob"), ("wb1", "ob"),
                                                   ("wc0", "yc"), ("wc1", "yc"))):
                        moving(y, 1)
                        if q < 2:
                            pe.wait_ge(S["lru_gates"], 8)
                        else:
                            pe.wait_ge(S["br_read"], q - 1)
                        for u in range(2):
                            w = parts(AT[name], u)
                            for j in (2 * u, 2 * u + 1):
                                for t in range(4):
                                    last = product(two(3 + 2 * (q % 2) + j // 2)[:, j % 2, :], w, (j * 4 + t) * P,
                                                   y_parts[y][0][:, t, :], y_parts[y][1][:, t, :], t == 0, t == 3)
                            last.then_inc(S["used"], 1)
                    pe.wait_ge(S["br_read"], 6)
                    for i, b in enumerate((7, 2, 3, 4)):
                        for u in range(2):
                            w = parts(AT[f"wo{i}"], u)
                            for t in range(KT):
                                if not i and not u and t % 2 == 0:
                                    moving("mix", t // 2)
                                last = product(two(b)[:, u, :], w, (u * KT + t) * P, n_high[:, t, :], n_low[:, t, :],
                                               t == 0, t == KT - 1)
                            last.then_inc(S["used"], 1)

                    norm_sums(2)
                    for i in range(8):
                        project(f"wq{i}", 27 + i, fresh=None if i else "norm2")
                    w = arrived(AT["keys"])
                    pe.wait_ge(S["pj_free"], 35)
                    for m in range(MT_):
                        for hs in range(16):
                            b = 2 + (4 * m + hs // 4) % 6
                            if m and hs == 8:
                                pe.wait_ge(S["sub_ready"], 2)
                            last = mmul(four(b)[:, hs % 4, :], qt[:, hs, m * P:(m + 1) * P],
                                        w[:, hs * P:(hs + 1) * P], start=True, stop=True)
                        if m == 0:
                            last.then_inc(S["sub_full"], 1)
                    last.then_inc(S["used"], 2)
                    with pe.Fori(0, 64 // RING) as lap:
                        for i in range(RING):
                            project(f"u{i}", 35 + i, lap)
                    pe.wait_ge(S["picks_ready"], 2)
                    pe.wait_ge(S["sub_ready"], 8)
                    for m in range(MT_):
                        for k in range(3):
                            last = nc.tensor.transpose(four(6 + m)[:, k, :], picks[:, m, k, :], ident)
                    last.then_inc(S["tr_full"], 1)
                    pe.wait_ge(S["pj_free"], 99)

                    def gates(g, at, after=None):
                        pe.wait_ge(S["hot1_ready"], at + 1)
                        pe.wait_ge(S["hot2_ready"], at + 1)
                        if after is not None:
                            pe.wait_ge(S["coef_ready"], after)
                        for k in range(4):
                            last = mmul(four(GATE_BANKS[g])[:, k, :], hot1[:, 4 * g + k, :], hot2[:, 4 * g + k, :],
                                        start=True, stop=True)
                        last.then_inc(S["gates_full"], 1)

                    for g in range(4):
                        gates(g, g)
                    with pe.Fori(0, GROUPS // 4 - 1) as it:
                        for g in range(4):
                            gates(g, it * 4 + (4 + g), it * 4 + (g + 1))

                    def values(pair, lap=None, first=False, final=False):
                        v = pair - AT["v0"]
                        k = MOVING["coef"] + v + 1
                        pe.wait_ge(S["x_low"], k if lap is None else lap * RING + k)
                        for e in range(2):
                            w = parts(pair, e, lap)
                            at = 2 * (v % 4) + e
                            for t in range(KT):
                                last = product(two(2 + t // 2)[:, t % 2, :], w, (e * KT + t) * P,
                                               n_high[:, at, :], n_low[:, at, :],
                                               first and not e and t % 2 == 0, final and e == 1, loose=True)
                            last.then_inc(S["used"], 1)

                    for v in range(4):
                        values(AT["v0"] + v, first=not v)
                    with pe.Fori(0, 64 // RING - 2) as lap:
                        for v in range(4, 8):
                            values(AT["v0"] + v, lap)
                    for v in range(60, 64):
                        values(AT["v0"] + v, final=v == 63)

                    w = arrived(AT["pp"])
                    for t in range(KT):
                        if t == KT // 2:
                            norm_sums(3, 2)
                        for k in range(2):
                            at = (t * 2 + k) * P
                            last = mmul(two(PLE_BANKS[t // 2])[:, t % 2, :], w[:, at:at + P], ple[:, k, :],
                                        start=k == 0, stop=k == 1)
                    last.then_inc(S["used"], 2)
                    for i in range(4):
                        project(f"pg{i}", 99 + i, fresh=None if i else "norm3", base=3)

                @block.scalar
                def _(act):
                    A = nc.scalar.activation
                    o = Order(act, S["achain"])

                    def used(units, lap=None):
                        act.wait_ge(S["used"], units if lap is None else lap * (2 * RING) + units)

                    def split(pair, unit, lap=None):
                        if pair in WHOLE or pair >= NPAIR:
                            return
                        if not unit:
                            i, k = pair % RING, 16 * (pair // RING + 1)
                            act.wait_ge(slot[i], k if lap is None else lap * 16 + k)
                        if pair >= HIGHS:
                            used(2 * (pair - HIGHS) + unit + 1, lap)
                        cols = slice(unit * 1024, (unit + 1) * 1024)
                        A(high[pair % HIGHS][:, cols], ring[pair % RING][:, cols], ACT.Copy).then_inc(S["high_ready"], 1)

                    def empty(name, use, out_, func, lap=None, base=0):
                        pair = AT[name]
                        split(pair + HIGHS, 0, lap)
                        used(2 * (pair + 1), lap)
                        A(out_, two(base + use % 2), func).then_inc(S["pj_free"], 1)
                        split(pair + HIGHS, 1, lap)

                    def split_moving(dst, src):
                        A(dst, src, ACT.Copy).then_inc(S["x_high"], 1)

                    def split_n(k, i):
                        act.wait_ge(S["n_ready"], 4 * (k - 1) + i + 1)
                        split_moving(n_high[:, 2 * i:2 * i + 2, :], n[:, 2 * i:2 * i + 2, :])

                    use = iter(range(27))

                    def fill(name):
                        k = next(use)
                        func = ACT.Copy if k < 11 else ACT.Silu if k < 13 else ACT.Gelu_apprx_tanh if k < 15 else ACT.Sigmoid
                        empty(name, k, z[:, 2 * k:2 * k + 2, :], func)

                    def square(k, i):
                        if k > 1:
                            act.wait_ge(S["h_new"], 4 * (k - 2) + i + 1)
                        A(sq[:, 2 * i:2 * i + 2, :], h[:, 2 * i:2 * i + 2, :], ACT.Square).then_inc(S["squares"], 1)

                    def root(k, b=6):
                        act.wait_ge(S["sums"], k)
                        A(rms, bank[b][:, 0:SEQ], ACT.Sqrt, scale=1.0 / D_MODEL, bias=eps[:, :]).then_inc(S["rms_ready"], 1)

                    for i in range(4):
                        square(1, i)
                    root(1)
                    split(0, 0)
                    for i in range(4):
                        split_n(1, i)
                    split(0, 1)
                    split(1, 0)
                    split(1, 1)
                    for name in STREAM[:13]:
                        fill(name)
                    for i in range(6):
                        act.wait_ge(S["conv_ready"], i + 1)
                        A(cv[:, 2 * i:2 * i + 2, :], cv[:, 2 * i:2 * i + 2, :], ACT.Silu).then_inc(S["silu_ready"], 1)
                        if i == 3:
                            act.wait_ge(S["silu_ready"], 4)
                            A(l2[:, :, :], cv[:, 0:8, :], ACT.Square).then_inc(S["l2sq_ready"], 1)
                    act.wait_ge(S["sp_in"], 1)
                    A(nea, s("alog"), ACT.Exp).then_inc(S["sp_exp"], 1)
                    A(se, sa, ACT.Exp, scale=-1.0).then_inc(S["sp_exp"], 1)
                    A(beta, beta, ACT.Exp, scale=-1.0).then_inc(S["sp_exp"], 1)
                    act.wait_ge(S["roped"], 1)
                    act.wait_ge(S["rot_full"], 2)
                    A(vtok[:, :, :], bank[7][:, 0:2 * P].rearrange("p (m c) -> p m c", m=2), ACT.Copy)\
                        .then_inc(S["vtok_ready"], 1)
                    fill("cy0")
                    act.wait_ge(S["rowmax_ready"], 1)
                    for m, sc in ((0, sc0), (1, sc1)):
                        for hd in range(A_HEADS):
                            A(sc[:, hd, :], sc[:, hd, :], ACT.Exp, bias=nmx[:, m, hd:hd + 1],
                              accum_out=den[:, m, hd:hd + 1]).then_inc(S["exps_ready"], 1)
                    A(esink, esink, ACT.Exp).then_inc(S["exps_ready"], 1)
                    fill("cy1")
                    act.wait_ge(S["l2_full"], 1)
                    for b in range(4):
                        A(l2[:, 2 * b:2 * b + 2, :], two(2 + b), ACT.Sqrt, bias=eps[:, :]).then_inc(S["l2_root"], 1)
                    fill("ga0")
                    act.wait_ge(S["pt_full"], 1)
                    for b in range(2):
                        A(pt0[:, 4 * b:4 * b + 4, :], four(6 + b), ACT.Copy).then_inc(S["pt_ready"], 1)
                    act.wait_ge(S["pt_full"], 2)
                    for b in range(4):
                        A(pt1[:, b // 2, (b % 2) * 512:(b % 2 + 1) * 512], bank[2 + b][:, :], ACT.Copy)\
                            .then_inc(S["pt_ready"], 1)
                    fill("ga1")
                    fill("ga2")
                    act.wait_ge(S["g_dif"], 1)
                    A(egs, gs, ACT.Exp).then_inc(S["g_exp"], 1)
                    act.wait_ge(S["dif_ready"], 1)
                    A(dec[:, :, :], dec[:, :, :], ACT.Exp)
                    A(egb[:, 0, :], bank[7][:, :], ACT.Exp)
                    A(egb[:, 1, :], bank[2][:, :], ACT.Exp).then_inc(S["dec_exp"], 1)
                    fill("ga3")
                    fill("gb0")
                    for level, name in zip(range(1, 6), ("gb1", "gb2", "gb3", "gc0", "gc1")):
                        act.wait_ge(S["x_full"], level + 1)
                        for m in range(MT_):
                            A(xx[:, m, :], bank[3 + m][:, :], ACT.Copy).then_inc(S["x_ready"], 1)
                        fill(name)
                    fill("gc2")
                    act.wait_ge(S["w_full"], 1)
                    for m, b in enumerate((7, 2)):
                        A(dec[:, m, :], bank[b][:, :], ACT.Copy, scale=-1.0).then_inc(S["w_ready"], 1)
                    for ch in range(SEQ // CHUNK):
                        act.wait_ge(S["o_full"], ch + 1)
                        A(ob[:, :, ch * CHUNK:(ch + 1) * CHUNK],
                          bank[5 + ch % 2][:, 0:256].rearrange("p (a i) -> p a i", a=4), ACT.Copy)\
                            .then_inc(S["o_ready"], 1)
                        if ch == 0:
                            fill("gc3")
                    act.wait_ge(S["o_ready"], 4)
                    A(osq[:, :, :], ob[:, :, :], ACT.Square).then_inc(S["osq_ready"], 1)
                    for i in range(2):
                        split_moving(n_high[:, 2 * i:2 * i + 2, :], ya[:, 2 * i:2 * i + 2, :])
                    used(2 * (AT["lru"] + 1))
                    for k, dst, b in [(k, lr, "ba") for k in range(4)] + [(k, li, "bi") for k in range(4)]:
                        src = two((3 if b == "ba" else 5) + k // 2)[:, k % 2, :]
                        A(dst[:, k, :], src, ACT.Sigmoid, bias=s(b)[:, k:k + 1]).then_inc(S["lru_gates"], 1)
                    act.wait_ge(S["lru_gates"], 4)
                    for k in range(4):
                        A(lt[:, k, :], lr[:, k, :], ACT.Tanh, scale=lrs[:, k:k + 1]).then_inc(S["tanh_ready"], 1)
                    act.wait_ge(S["osum_full"], 1)
                    for k, b in enumerate((7, 2)):
                        A(ors[:, 2 * k:2 * k + 2, :], two(b), ACT.Sqrt, scale=1.0 / B_DH, bias=eps[:, :])\
                            .then_inc(S["o_root"], 1)
                    act.wait_ge(S["tanh_ready"], 4)
                    A(lroot[:, :, :], lt[:, :, :], ACT.Sqrt).then_inc(S["lru_sqrt"], 1)
                    wa0 = AT["wa0"]
                    split(wa0 + 1, 0)
                    split(wa0 + 1, 1)
                    act.wait_ge(S["yb_ready"], 1)
                    for i in range(2):
                        split_moving(n_high[:, 2 * i + 4:2 * i + 6, :], ob[:, 2 * i:2 * i + 2, :])
                    for pair in range(wa0 + 2, wa0 + 4):
                        split(pair, 0)
                        split(pair, 1)
                    act.wait_ge(S["yc_ready"], 1)
                    for i in range(2):
                        split_moving(yc_high[:, 2 * i:2 * i + 2, :], yc[:, 2 * i:2 * i + 2, :])
                    for pair in range(wa0 + 4, wa0 + 6):
                        split(pair, 0)
                        split(pair, 1)
                    wo0 = AT["wo0"]
                    for half_ in range(2):
                        split(wo0 + half_, 0)
                        split(wo0 + half_, 1)
                        act.wait_ge(S["br_read"], 5 + half_)
                        for i in (2 * half_, 2 * half_ + 1):
                            split_moving(n_high[:, 2 * i:2 * i + 2, :], mix[:, 2 * i:2 * i + 2, :])
                    for i in range(4):
                        if i:
                            square(2, i - 1)
                        split(wo0 + 2 + i, 0)
                        if i < 3:
                            split(wo0 + 2 + i, 1)
                    square(2, 3)
                    split(wo0 + 5, 1)
                    root(2)
                    for i in range(4):
                        split_n(2, i)
                    for i in range(8):
                        empty(f"wq{i}", 27 + i, qt[:, 2 * i:2 * i + 2, :], ACT.Copy)
                    act.wait_ge(S["sub_full"], 1)
                    for k in range(8):
                        if k == 4:
                            used(2 * (AT["keys"] + 1))
                        A(sub[:, k // 4, (k % 4) * 512:(k % 4 + 1) * 512], bank[2 + k % 6][:, :], ACT.Copy)\
                            .then_inc(S["sub_ready"], 1)
                        if k == 3:
                            split(AT["u1"], 0)
                            split(AT["u1"], 1)

                    def gelus(laps, done):
                        with act.Fori(0, laps) as lap:
                            for i in range(done, done + RING):
                                empty(f"u{i}", 35 + i, act_h[:, bass.ds(lap * (2 * RING) + 2 * i, 2), :],
                                      ACT.Gelu_apprx_tanh, lap)

                    gelus(6, 0)
                    act.wait_ge(S["exp_in"], 1)
                    A(picks[:, :, 2, :], picks[:, :, 2, :], ACT.Exp).then_inc(S["exp_out"], 1)
                    gelus(2, 24)
                    act.wait_ge(S["picks_ready"], 2)
                    gelus(8, 32)
                    act.wait_ge(S["route_ready"], 1)

                    def distances(g, token):
                        for k in range(4):
                            last = A(hot2[:, 4 * g + k, :], c("iota"), ACT.Square, scale=-1.0,
                                     bias=route[:, 1, bass.ds(token + k, 1)])
                        last.then_inc(S["distance"], 1)

                    def second(g, group):
                        act.wait_ge(S["distance"], group + 1)
                        four_ = hot2[:, 4 * g:4 * g + 4, :]
                        A(four_, four_, ACT.Relu, scale=-1.0, bias=ones[:, 0:1]).then_inc(S["hot2_ready"], 1)

                    for g in range(4):
                        distances(g, 4 * g)
                        if g:
                            second(g - 1, g - 1)
                    with act.Fori(0, GROUPS // 4 - 1) as it:
                        for g in range(4):
                            act.wait_ge(S["gates_full"], it * 4 + (g + 1))
                            distances(g, it * 16 + (16 + 4 * g))
                            second((g + 3) % 4, it * 4 + (g + 3))
                    second(3, GROUPS - 1)
                    act.wait_ge(S["coef_ready"], GROUPS)

                    def coefs(i, lap=None):
                        src = act_h[:, 2 * i:2 * i + 2, :] if lap is None else \
                            act_h[:, bass.ds(lap * (2 * RING) + 2 * i, 2), :]
                        at = 2 * (i % 4)
                        split_moving(n_high[:, at:at + 2, :], src)

                    for i in range(2):
                        coefs(i)
                    with act.Fori(0, 60 // RING) as lap:
                        for i in range(2, 6):
                            split(AT["v0"] + i, 0, lap)
                            coefs(i, lap)
                            split(AT["v0"] + i, 1, lap)
                    for i in range(62, 64):
                        split(AT["v0"] + i, 0)
                        coefs(i)
                        split(AT["v0"] + i, 1)
                    split(AT["pg0"], 0)
                    split(AT["pg0"], 1)
                    for i in range(4):
                        square(3, i)
                    root(3, 2)
                    for i in range(4):
                        split_n(3, i)
                    split(AT["pg1"], 0)
                    split(AT["pg1"], 1)
                    for i in range(4):
                        empty(f"pg{i}", 99 + i, z[:, 2 * i:2 * i + 2, :], ACT.Sigmoid, base=3)

                @block.gpsimd
                def _(pool):
                    TT = nc.gpsimd.tensor_tensor

                    def lower(pair, lap=None):
                        for unit in range(2):
                            k = split_units(pair, unit)
                            pool.wait_ge(S["high_ready"], k if lap is None else lap * (2 * RING) + k)
                            cols = slice(unit * 1024, (unit + 1) * 1024)
                            TT(low[pair % RING][:, cols], ring[pair % RING][:, cols],
                               high[pair % HIGHS][:, cols].bitcast(f32), SUB).then_inc(S["low_ready"], 1)

                    def lower_all(first, end):
                        laps = (end - first) // RING
                        with pool.Fori(0, laps) as lap:
                            for i in range(RING):
                                lower(first + i, lap)
                        for pair in range(first + laps * RING, end):
                            lower(pair)

                    lower_all(0, AT["lru"])
                    lower_all(AT["lru"] + 1, AT["keys"])
                    lower_all(AT["u0"], AT["v0"] + HIGHS)
                    with pool.Fori(0, GROUPS // 4) as it:
                        for g in range(4):
                            pool.wait_ge(S["ones_ready"], it * 4 + (g + 1))
                            hot = hot1[:, 4 * g:4 * g + 4, :]
                            gate = route[:, 2, bass.ds(it * 16 + 4 * g, 4)].unsqueeze(2).to_broadcast([P, 4, P])
                            TT(hot, hot, gate, MUL).then_inc(S["hot1_ready"], 1)
                    lower_all(AT["v0"] + HIGHS, AT["pp"])
                    lower_all(AT["pg0"], NPAIR)

                @block.vector
                def _(dve):
                    V = nc.vector
                    o = Order(dve, S["vchain"])
                    TS, TT, STT = V.tensor_scalar, V.tensor_tensor, V.scalar_tensor_tensor

                    def over(ap, count):
                        return ap.unsqueeze(1).to_broadcast([P, count, ap.shape[1]])

                    def along(ap, count):
                        return ap.unsqueeze(2).to_broadcast([P, ap.shape[1], count])

                    def used(name):
                        dve.wait_ge(S["used"], 2 * (AT[name] + 1))

                    def lower(name, step, dst, src, high_):
                        dve.wait_ge(S["x_high"], MOVING[name] + step + 1)
                        TT(dst, src, high_.bitcast(f32), SUB).then_inc(S["x_low"], 1)

                    def lower_n(name, i, src=n):
                        t = slice(2 * i, 2 * i + 2)
                        lower(name, i, n_low[:, t, :], src[:, t, :], n_high[:, t, :])

                    def normalise(k, weight):
                        dve.wait_ge(S["rms_ready"], k)
                        o.link(V.reciprocal(rstd, rms))
                        for i in range(4):
                            for t in (2 * i, 2 * i + 1):
                                last = STT(n[:, t, :], h[:, t, :], s(weight)[:, t:t + 1], rstd, MUL, MUL)
                            last.then_inc(S["n_ready"], 1)
                        for i in range(4):
                            lower_n(f"norm{k}", i)

                    def conv(dst, src, w, bias=None):
                        units = range(len(src))
                        for u in units:
                            last = TS(dst[u], src[u], w[u][3], None, MUL) if bias is None else \
                                TS(dst[u], src[u], w[u][3], bias[u], MUL, ADD)
                        for tap in (2, 1, 0):
                            o.link(last)
                            back = 3 - tap
                            for u in units:
                                last = STT(dst[u][:, back:], src[u][:, :SEQ - back], w[u][tap], dst[u][:, back:], MUL, ADD)
                        return last

                    dve.wait_ge(S["small_in"], 32)
                    normalise(1, "n_mix")

                    for i in range(6):
                        dve.wait_ge(S["pj_free"], i + 1)
                        us = (2 * i, 2 * i + 1)
                        w = s("bconv")
                        conv([cv[:, u, :] for u in us], [z[:, u, :] for u in us],
                             [[w[:, 4 * u + k:4 * u + k + 1] for k in range(4)] for u in us]).then_inc(S["conv_ready"], 1)
                    dve.wait_ge(S["ba_full"], 1)
                    for m in range(MT_):
                        V.tensor_copy(beta[:, m, :], bank[3][:, m * 8:m * 8 + 4])
                        TT(sp[:, 4 * m:4 * m + 4], bank[3][:, m * 8 + 4:m * 8 + 8], s("dt"), ADD)
                    o.link(TS(sp[:, 8:12], s("lam"), -1.0, None, MUL))
                    STT(sa, sp, -1.0, sp, MUL, MAX).then_inc(S["sp_in"], 1)
                    dve.wait_ge(S["sp_exp"], 3)
                    o.link(TS(ss, se, 2.0, None, ADD))
                    o.link(V.reciprocal(ss, ss))
                    o.link(TT(ss, ss, se, MUL))
                    o.link(TT(ssq, ss, ss, MUL))
                    o.link(TS(spo, ssq, 1.0 / 17, None, MUL))
                    for k in range(7, 0, -1):
                        o.link(STT(spo, spo, 1.0 / (2 * k + 1), ssq, ADD, MUL))
                    o.link(STT(spo, spo, 1.0, ss, ADD, MUL))
                    o.link(TS(spo, spo, 2.0, None, MUL))
                    o.link(STT(sp, sp, 0.0, spo, MAX, ADD))
                    o.link(TS(beta, beta, 1.0, None, ADD))
                    V.reciprocal(beta, beta)
                    V.tensor_scalar(lrs, sp[:, 8:12], LRU_C / 2, None, MUL)
                    for m in range(MT_):
                        last = STT(ag[:, m, :], sp[:, 4 * m:4 * m + 4], -1.0, nea, MUL, MUL)
                    last.then_inc(S["alpha_ready"], 1)

                    dve.wait_ge(S["rot_full"], 1)
                    TT(ropet[:, 0:2, :], two(4), over(sin[:, :], 2), MUL)
                    TT(ropet[:, 2:4, :], two(5), over(sin[:, :], 2), MUL)
                    TT(ropet[:, 4, :], bank[6][:, 0:SEQ], sin[:, :], MUL)
                    o.link(TT(qk[:, :, :], z[:, 12:17, :], over(cos[:, :], 5), MUL))
                    TT(qk[:, :, :], qk[:, :, :], ropet[:, :, :], ADD).then_inc(S["roped"], 1)
                    scale = float(A_DH) ** -0.5
                    dve.wait_ge(S["scores_full"], 1)
                    for b in range(2):
                        STT(sc0[:, 4 * b:4 * b + 4, :], four(2 + b), scale, over(c("mask0"), 4), MUL, ADD)\
                            .then_inc(S["masked"], 1)
                    dve.wait_ge(S["scores_full"], 2)
                    for b in range(4):
                        STT(sc1[:, 2 * b:2 * b + 2, :], two(4 + b), scale, over(c("mask1"), 2), MUL, ADD)\
                            .then_inc(S["masked"], 1)
                    dve.wait_ge(S["masked"], 6)
                    V.tensor_reduce(mx[:, 0, :], sc0[:, :, :], AX, MAX)
                    o.link(V.tensor_reduce(mx[:, 1, :], sc1[:, :, :], AX, MAX))
                    o.link(TT(mx, mx, over(s("sink"), 2), MAX))
                    TS(nmx, mx, -1.0, None, MUL)
                    TT(esink, over(s("sink"), 2), mx, SUB).then_inc(S["rowmax_ready"], 1)
                    dve.wait_ge(S["exps_ready"], 17)
                    o.link(TT(den, den, esink, ADD))
                    o.link(V.reciprocal(den, den))
                    TT(sc0[:, :, :], sc0[:, :, :], along(den[:, 0, :], P), MUL).then_inc(S["normed"], 1)
                    TT(sc1[:, :, :], sc1[:, :, :], along(den[:, 1, :], SEQ), MUL).then_inc(S["normed"], 1)
                    dve.wait_ge(S["l2_root"], 4)
                    o.link(V.reciprocal(l2[:, :, :], l2[:, :, :]))
                    dve.wait_ge(S["silu_ready"], 4)
                    STT(cv[:, 0:4, :], cv[:, 0:4, :], float(B_DH) ** -0.5, l2[:, 0:4, :], MUL, MUL)
                    TT(cv[:, 4:8, :], cv[:, 4:8, :], l2[:, 4:8, :], MUL).then_inc(S["qkn_ready"], 1)
                    dve.wait_ge(S["pv_full"], 1)
                    for m in range(MT_):
                        for g in range(A_KV):
                            mine = slice(64 * g, 64 * g + 64)
                            last = V.tensor_copy(ya[mine, :, m * P:(m + 1) * P], four(2 + 2 * m + g)[mine, :, :])
                    last.then_inc(S["ya_ready"], 1)

                    dve.wait_ge(S["g_full"], 1)
                    o.link(V.tensor_copy(gs, bank[6][:, 0:32].rearrange("p (m k a) -> p m k a", m=2, k=4)))
                    TT(gs[:, :, 1, :], gs[:, :, 1, :], gs[:, :, 0, :], SUB).then_inc(S["g_dif"], 1)
                    dve.wait_ge(S["gcb_full"], 1)
                    for m, b in enumerate((7, 2)):
                        for hd in range(B_HEADS):
                            at = slice(hd * P, (hd + 1) * P)
                            last = TS(dec[:, m, at], bank[b][:, at], gs[:, m, 0, hd:hd + 1], 0.0, SUB, ALU.min)
                    last.then_inc(S["dif_ready"], 1)
                    dve.wait_ge(S["g_exp"], 1)
                    TT(bg_, beta, egs[:, :, 0, :], MUL)
                    dve.wait_ge(S["dec_exp"], 1)
                    heads8 = dec[:, :, :].rearrange("p m (a i) -> p (m a) i", i=P)
                    o.link(TT(heads8, heads8, over(tri, 8), MUL))
                    dve.wait_ge(S["kk_full"], 1)
                    dve.wait_ge(S["bb_full"], 1)
                    for m in range(MT_):
                        last = TT(lo[:, m, :], bank[5 + m][:, :], dec[:, m, :], MUL)
                    o.link(last)
                    for m in range(MT_):
                        last = TT(lo[:, m, :], bank[3 + m][:, :], lo[:, m, :], MUL)
                    o.link(last)
                    lo8, ct8, mt8 = (x[:, :, :].rearrange("p m (a i) -> p (m a) i", i=P) for x in (lo, ct, mt))

                    def part(level):
                        mask = c("level")[:, level * P:(level + 1) * P]
                        TT(ct8, lo8, over(mask, 8), MUL).then_inc(S["level_ready"], 1)

                    part(0)
                    dve.wait_ge(S["qk_full"], 1)
                    for m, b in enumerate((7, 2)):
                        last = TT(qkd[:, m, :], bank[b][:, :], dec[:, m, :], MUL)
                    last.then_inc(S["qkd_ready"], 1)
                    dve.wait_ge(S["level_ready"], 1)
                    o.link(STT(mt8, ct8, -1.0, over(ident, 8), MUL, ADD))
                    dve.wait_ge(S["x_full"], 1)
                    for m in range(MT_):
                        last = STT(mm_[:, m, :].rearrange("p (a i) -> p a i", i=P), four(3 + m), -1.0,
                                   over(ident, 4), MUL, ADD)
                    last.then_inc(S["m_ready"], 1)
                    part(1)
                    for level in range(1, 6):
                        dve.wait_ge(S["x_full"], level + 1)
                        if level < 5:
                            part(level + 1)
                        dve.wait_ge(S["p_full"], level)
                        if level < 5:
                            for m in range(MT_):
                                TT(mm_[:, m, :], mm_[:, m, :], bank[5 + m][:, :], SUB)
                        for m, b in enumerate((7, 2)):
                            last = TT(mt[:, m, :], mt[:, m, :], bank[b][:, :], SUB)
                        last.then_inc(S["m_ready"], 1)
                    for m in range(MT_):
                        e = egb[:, m, :].rearrange("p (a i) -> p a i", i=P)
                        last = TT(e, cv[:, 0:4, m * P:(m + 1) * P], e, MUL)
                    last.then_inc(S["qg_ready"], 1)
                    dve.wait_ge(S["tok_full"], 1)
                    for m in range(MT_):
                        def by_head(x):
                            return x[:, m, :].rearrange("p (a i) -> p a i", i=P)
                        TT(by_head(ct), four(3 + m), along(bg_[:, m, :], P), MUL)
                        TT(by_head(lo), four(3 + m), along(egs[:, m, 1, :], P), MUL)
                        last = TT(by_head(xx), four(5 + m), along(beta[:, m, :], P), MUL)
                    last.then_inc(S["tok_ready"], 1)
                    w, b = s("cconv"), s("cbias")
                    conv([xc[:, u, :] for u in range(4)], [z[:, 18 + u, :] for u in range(4)],
                         [[w[:, 4 * u + k:4 * u + k + 1] for k in range(4)] for u in range(4)],
                         [b[:, u:u + 1] for u in range(4)]).then_inc(S["xc_ready"], 1)
                    for ch in range(SEQ // CHUNK):
                        m, r = ch // 2, ch % 2
                        rows = slice(CHUNK * r, CHUNK * (r + 1))
                        dve.wait_ge(S["vn_full"], ch + 1)
                        V.tensor_copy(vn[rows, :], bank[3 + ch % 2][rows, :]).then_inc(S["vn_ready"], 1)
                        if ch == 3:
                            break
                        dve.wait_ge(S["s_full"], ch + 1)
                        if not ch:
                            last = V.tensor_copy(state, bank[7][:, :])
                        else:
                            for hd in range(B_HEADS):
                                at = slice(hd * P, (hd + 1) * P)
                                last = STT(state[:, at], state[:, at], egs[:, m, 2 + r, hd:hd + 1], bank[7][:, at],
                                           MUL, ADD)
                        last.then_inc(S["s_ready"], 1)
                        dve.wait_ge(S["s_ready"], ch + 1)
                    for i in range(2):
                        lower_n("ya", i, ya)
                    dve.wait_ge(S["lru_gates"], 8)
                    TT(li[:, :, :], li[:, :, :], xc[:, :, :], MUL)
                    dve.wait_ge(S["tanh_ready"], 4)
                    TS(lr[:, :, :], lt[:, :, :], -1.0, 1.0, MUL, ADD)
                    o.link(TS(lw[:, :, :], lt[:, :, :], 1.0, None, ADD))
                    o.link(V.reciprocal(lw[:, :, :], lw[:, :, :]))
                    dve.wait_ge(S["o_root"], 2)
                    o.link(V.reciprocal(ors[:, :, :], ors[:, :, :]))
                    o.link(STT(ob[:, :, :], ob[:, :, :], s("dnorm"), ors[:, :, :], MUL, MUL))
                    TT(ob[:, :, :], ob[:, :, :], z[:, 22:26, :], MUL).then_inc(S["yb_ready"], 1)
                    TT(lr[:, :, :], lr[:, :, :], lw[:, :, :], MUL)
                    dve.wait_ge(S["lru_sqrt"], 1)
                    o.link(TT(lt[:, :, :], lroot[:, :, :], lw[:, :, :], MUL))
                    o.link(STT(li[:, :, :], li[:, :, :], 2.0, lt[:, :, :], MUL, MUL))
                    for i in range(2):
                        t = slice(2 * i, 2 * i + 2)
                        lower("ob", i, n_low[:, 2 * i + 4:2 * i + 6, :], ob[:, t, :], n_high[:, 2 * i + 4:2 * i + 6, :])
                    for u in range(4):
                        last = V.tensor_tensor_scan(xc[:, u, :], lr[:, u, :], li[:, u, :], 0.0, MUL, ADD)
                    o.link(last)
                    TT(yc[:, :, :], xc[:, :, :], z[:, 26:30, :], MUL).then_inc(S["yc_ready"], 1)
                    for i in range(2):
                        t = slice(2 * i, 2 * i + 2)
                        lower("yc", i, yc_low[:, t, :], yc[:, t, :], yc_high[:, t, :])

                    for q, name in enumerate(("wa0", "wa1", "wb0", "wb1", "wc0", "wc1")):
                        used(name)
                        for k in range(2):
                            t = 4 * (q % 2) + 2 * k
                            gate = z[:, 30 + 8 * (q // 2) + t:32 + 8 * (q // 2) + t, :]
                            src = two(3 + 2 * (q % 2) + k)
                            if q < 2:
                                last = TT(mix[:, t:t + 2, :], src, gate, MUL)
                            else:
                                o.link(TT(mixt, src, gate, MUL))
                                last = TT(mix[:, t:t + 2, :], mix[:, t:t + 2, :], mixt, ADD)
                                if k == 0:
                                    o.link(last)
                        last.then_inc(S["br_read"], 1)
                        dve.wait_ge(S["br_read"], q + 1)
                        if q >= 4:
                            for i in (2 * q - 8, 2 * q - 7):
                                lower_n("mix", i, mix)
                    for i, bk in enumerate((7, 2, 3, 4)):
                        used(f"wo{i}")
                        TT(h[:, 2 * i:2 * i + 2, :], h[:, 2 * i:2 * i + 2, :], two(bk), ADD).then_inc(S["h_new"], 1)
                    normalise(2, "n_ffn")

                    def best16(values, rest, top, index):
                        all_ = range(len(values))
                        for k in all_:
                            last = V.max(top[k][:, 0:8], values[k])
                        o.link(last)
                        for k in all_:
                            V.max_index(index[k][:, 0:8], top[k][:, 0:8], values[k])
                            last = V.match_replace(rest[k], top[k][:, 0:8], values[k], -3.4028235e38)
                        o.link(last)
                        for k in all_:
                            last = V.max(top[k][:, 8:16], rest[k])
                        o.link(last)
                        for k in all_:
                            last = V.max_index(index[k][:, 8:16], top[k][:, 8:16], rest[k])
                        o.link(last)

                    def cut(x, size, count):
                        return [x[:, k * size:(k + 1) * size] for k in range(count)]

                    dve.wait_ge(S["sub_ready"], 8)
                    iota16 = c("iota")[:, 0:TOPK]
                    shape4 = [P, HEADS, TOPK, TOPK]
                    for m in range(MT_):
                        best16(cut(sub[:, m, :], P, 16), cut(sub2, P, 16),
                               cut(tops[:, m, :], TOPK, 16), cut(topi[:, m, :], TOPK, 16))
                        V.tensor_copy(topf[:, m, :], topi[:, m, :])
                        sides = tops[:, m, :].rearrange("p (h s k) -> p h s k", s=2, k=TOPK)
                        pairs = cand.rearrange("p (h a b) -> p h a b", a=TOPK, b=TOPK)
                        o.link(TT(pairs, sides[:, :, 0, :].unsqueeze(3).to_broadcast(shape4),
                                  sides[:, :, 1, :].unsqueeze(2).to_broadcast(shape4), ADD))
                        best16(cut(cand, 256, HEADS), cut(cand2, 256, HEADS),
                               cut(best[:, m, :], TOPK, HEADS), cut(besti[:, m, :], TOPK, HEADS))
                        keys_ = topf[:, m, :].rearrange("p (h s k) -> p h s k", s=2, k=TOPK)
                        for side in range(2):
                            if side == 0:
                                o.link(TS(half[:, m, :], besti[:, m, :], 4, None, ALU.logical_shift_right))
                            else:
                                o.link(TS(half[:, m, :], besti[:, m, :], 15, None, ALU.bitwise_and))
                            o.link(V.tensor_copy(halff[:, m, :], half[:, m, :]))
                            flat = cand.rearrange("p (k c) -> p k c", c=TOPK)
                            o.link(TT(flat, along(halff[:, m, :], TOPK), over(iota16, P), ALU.is_equal))
                            o.link(TT(pairs, pairs, keys_[:, :, side, :].unsqueeze(2).to_broadcast(shape4), MUL))
                            o.link(V.tensor_reduce(picks[:, m, side, :], flat, AX, ADD))
                        bests = best[:, m, :].rearrange("p (h k) -> p h k", k=TOPK)
                        gate = picks[:, m, 2, :].rearrange("p (h k) -> p h k", k=TOPK)
                        last = TT(gate, bests, bests[:, :, 0:1].to_broadcast([P, HEADS, TOPK]), SUB)
                        if m == 0:
                            o.link(last)
                    last.then_inc(S["exp_in"], 1)
                    dve.wait_ge(S["exp_out"], 1)
                    for m in range(MT_):
                        gate = picks[:, m, 2, :].rearrange("p (h k) -> p h k", k=TOPK)
                        o.link(V.tensor_reduce(gsum[:, m, :], gate, AX, ADD))
                        o.link(V.reciprocal(gsum[:, m, :], gsum[:, m, :]))
                        TT(gate, gate, along(gsum[:, m, :], TOPK), MUL).then_inc(S["picks_ready"], 1)
                    dve.wait_ge(S["tr_full"], 1)
                    for m in range(MT_):
                        last = V.tensor_copy(route[:, :, m * P:(m + 1) * P], four(6 + m)[:, 0:3, :])
                    last.then_inc(S["route_ready"], 1)
                    dve.wait_ge(S["route_ready"], 1)
                    dve.wait_ge(S["pj_free"], 99)
                    by_token = act_h[:, :, :].rearrange("p j t -> p t j")

                    def first(g, token):
                        keys_ = route[:, 0, bass.ds(token, 4)].unsqueeze(2).to_broadcast([P, 4, P])
                        TT(hot1[:, 4 * g:4 * g + 4, :], keys_, over(c("iota"), 4), ALU.is_equal)\
                            .then_inc(S["ones_ready"], 1)

                    def coefficients(g, group):
                        dve.wait_ge(S["gates_full"], group + 1)
                        acts = by_token[:, bass.ds(group * 4, 4), :]
                        TT(acts, four(GATE_BANKS[g]), acts, MUL).then_inc(S["coef_ready"], 1)

                    for g in range(3):
                        first(g, 4 * g)
                    with dve.Fori(0, GROUPS // 4 - 1) as it:
                        for g in range(4):
                            coefficients(g, it * 4 + g)
                            first((g + 3) % 4, it * 16 + 4 * (g + 3))
                    for g in range(4):
                        coefficients(g, GROUPS - 4 + g)
                        if g == 0:
                            first(3, SEQ - 4)

                    def coef_low(i, lap=None):
                        src = act_h[:, 2 * i:2 * i + 2, :] if lap is None else \
                            act_h[:, bass.ds(lap * (2 * RING) + 2 * i, 2), :]
                        t = slice(2 * (i % 4), 2 * (i % 4) + 2)
                        k = MOVING["coef"] + i + 1
                        dve.wait_ge(S["x_high"], k if lap is None else lap * RING + k)
                        TT(n_low[:, t, :], src, n_high[:, t, :].bitcast(f32), SUB).then_inc(S["x_low"], 1)
                    with dve.Fori(0, 64 // RING) as lap:
                        for i in range(4):
                            coef_low(i, lap)
                    used("v63")
                    for i in range(4):
                        TT(h[:, 2 * i:2 * i + 2, :], h[:, 2 * i:2 * i + 2, :], two(2 + i), ADD).then_inc(S["h_new"], 1)
                    normalise(3, "n_ple")
                    used("pp")
                    for i in range(4):
                        dve.wait_ge(S["pj_free"], 100 + i)
                        o.link(TT(mixt, two(PLE_BANKS[i]), z[:, 2 * i:2 * i + 2, :], MUL))
                        last = TT(h[:, 2 * i:2 * i + 2, :], h[:, 2 * i:2 * i + 2, :], mixt, ADD)
                        last.then_inc(S["h_new"], 1)
                        dve.wait_ge(S["h_new"], 9 + i)

            nc.all_engine_barrier(sems_to_clear=layer_sems)

        with nc.Block() as block:
            @block.scalar
            def _(act):
                nc.scalar.activation(sq[:, :, :], h[:, :, :], ACT.Square).then_inc(S["squares"], 1)
                act.wait_ge(S["sums"], 1)
                nc.scalar.activation(rms, bank[2][:, 0:SEQ], ACT.Sqrt, scale=1.0 / D_MODEL, bias=eps[:, :])\
                    .then_inc(S["rms_ready"], 1)

            @block.tensor
            def _(pe):
                pe.wait_ge(S["squares"], 1)
                for t in range(KT):
                    last = nc.tensor.matmul(bank[2][:, 0:SEQ], ones, sq[:, t, :], start=t == 0, stop=t == KT - 1)
                last.then_inc(S["sums"], 1)

            @block.vector
            def _(dve):
                dve.wait_ge(S["rms_ready"], 1)
                nc.vector.reciprocal(rstd, rms).then_inc(S["rstd_ready"], 1)
                dve.wait_ge(S["rstd_ready"], 1)
                for t in range(KT):
                    nc.vector.scalar_tensor_tensor(n[:, t, :], h[:, t, :], c("final")[:, t:t + 1], rstd, MUL, MUL)\
                        .then_inc(S["n_ready"], 1)

            @block.sync
            def _(sync):
                for half_ in range(2):
                    sync.wait_ge(S["n_ready"], 4 * half_ + 4)
                    sync.dma_start(out[:, 4 * half_:4 * half_ + 4, :], n[:, 4 * half_:4 * half_ + 4, :])\
                        .then_inc(stored_out, 16)
                sync.wait_ge(stored_out, 32)


def constants():
    p = np.arange(P)
    f = np.float32
    chunk = p // CHUNK
    same = chunk[:, None] == chunk[None, :]
    out = np.zeros((P, NCONST), f)

    def put(name, value):
        a, b = CONST[name]
        out[:, a:b] = value
    put("ident", np.eye(P))
    put("ones", 1.0)
    put("tri", same & (p[:, None] <= p[None, :]))
    put("blk", same)
    put("chunk", np.repeat(chunk[:, None] == np.arange(2)[None, :], P, axis=1))
    levels = []
    for level in range(6):
        size = 1 << level
        levels.append((p[:, None] // (2 * size) == p[None, :] // (2 * size))
                      & (p[:, None] // size % 2 == 0) & (p[None, :] // size % 2 == 1))
    put("level", np.concatenate(levels, 1))
    half = A_DH // 2
    partner = p // A_DH * A_DH + (p + half) % A_DH
    put("rot", p[:, None] == partner[None, :])
    for m, name in enumerate(("mask0", "mask1")):
        q, k = (m * P + p)[:, None] // CHUNK, np.arange((m + 1) * P)[None, :] // CHUNK
        put(name, np.where((k == q) | (k == q - 1), 0.0, -1e30))
    put("iota", p[None, :])
    put("freq", (ROPE_THETA ** (-np.arange(half, dtype=f) / f(half))).astype(f)[p % half][:, None])
    put("sign", np.where(p % A_DH < half, -1.0, 1.0)[:, None])
    return out


def units(w):
    k, m = w.shape
    return w.reshape(k // P, P, m // P, P).transpose(2, 1, 0, 3)


def pairs(u):
    return u.reshape(-1, 2, P, 1024).transpose(0, 2, 1, 3).reshape(-1, P, 2048)


def lay_out(x, p, positions, norm_mix, w_in, attn_sinks, dn_conv, dn_a_log, dn_dt_bias, dn_norm, lru_conv_w,
            lru_conv_b, lru_w_a, lru_b_a, lru_w_i, lru_b_i, lru_lambda, w_branch_a, w_branch_b, w_branch_c,
            w_out, norm_ffn, peer_w_q, peer_sub_keys, peer_u, peer_v, norm_ple, ple_w_gate, ple_w_proj,
            norm_final):
    const = constants()
    const[:, slice(*CONST["final"])] = norm_final.reshape(KT, P).T
    order = np.concatenate([np.arange(hd * A_DH, (hd + 1) * A_DH) for i in range(4) for hd in (i, 4 + i)])
    sizes = [512, 128, 128, 1536, 4, 4, 512, 512, 512, 1024, 1024, 1024]
    stream = np.empty((DEPTH * NPAIR, P, 2048), np.float32)
    small = np.zeros((DEPTH, P, NSMALL), np.float32)
    for l in range(DEPTH):
        aq, ak, av, bqkv, bbeta, balpha, bgate, cx, cy, ga, gb, gc = np.split(w_in[l], np.cumsum(sizes)[:-1], axis=1)
        base = l * NPAIR

        def put(name, value):
            at = base + AT[name]
            stream[at:at + len(value)] = value
        main = np.concatenate([bqkv, aq[:, order], ak, av, cx, bgate, cy, ga, gb, gc], axis=1)
        put("bqkv0", pairs(units(main)))
        lru = np.zeros((P, 16, P), np.float32)
        for i, w in enumerate((lru_w_a[l], lru_w_i[l])):
            for t in range(4):
                for e in range(2):
                    lru[64 * e:64 * e + 64, 4 * i + t, 64 * e:64 * e + 64] = w[2 * t + e]
        put("lru", lru.reshape(1, P, 2048))
        for name, w in (("wa0", w_branch_a[l][order]), ("wb0", w_branch_b[l]), ("wc0", w_branch_c[l])):
            put(name, units(w).reshape(2, 4, P, 512).transpose(0, 2, 1, 3).reshape(2, P, 2048))
        put("wo0", pairs(units(w_out[l])))
        put("wq0", pairs(units(peer_w_q[l])))
        put("keys", peer_sub_keys[l].transpose(3, 0, 1, 2).reshape(1, P, 2048))
        put("u0", pairs(peer_u[l].reshape(NKEYS, NKEYS, KT, P).transpose(1, 3, 2, 0)))
        put("v0", pairs(peer_v[l].reshape(NKEYS, NKEYS, D_MODEL).transpose(1, 0, 2)))
        put("pp", units(ple_w_proj[l]).transpose(1, 0, 2, 3).reshape(1, P, 2048))
        put("pg0", pairs(units(ple_w_gate[l])))

        def col(name, value):
            a, b = SMALL[name]
            small[l, :, a:b] = value
        col("n_mix", norm_mix[l].reshape(KT, P).T)
        col("n_ffn", norm_ffn[l].reshape(KT, P).T)
        col("n_ple", norm_ple[l].reshape(KT, P).T)
        col("bconv", dn_conv[l].reshape(4, 12, P).transpose(2, 1, 0).reshape(P, 48))
        col("cconv", lru_conv_w[l].reshape(4, 4, P).transpose(2, 1, 0).reshape(P, 16))
        col("cbias", lru_conv_b[l].reshape(4, P).T)
        col("ba", lru_b_a[l].reshape(4, P).T)
        col("bi", lru_b_i[l].reshape(4, P).T)
        col("lam", lru_lambda[l].reshape(4, P).T)
        col("dnorm", dn_norm[l][:, None])
        col("sink", attn_sinks[l][None, :])
        col("alog", dn_a_log[l][None, :])
        col("dt", dn_dt_bias[l][None, :])
        col("wba", np.concatenate([bbeta, balpha], 1).reshape(KT, P, 8).transpose(1, 0, 2).reshape(P, 64))
    return {
        "stream": stream,
        "small": small,
        "p": np.ascontiguousarray(p[:, 0].transpose(0, 2, 1).reshape(DEPTH, 2, P, SEQ).transpose(0, 2, 1, 3)),
        "x": np.ascontiguousarray(x[0].T.reshape(KT, P, SEQ).transpose(1, 0, 2)),
        "positions": np.ascontiguousarray(positions[0]),
        "const": const,
    }


def kernel(**inputs):
    import concourse.bacc as _bacc
    from concourse.bass_utils import run_bass_kernel_spmd as _run

    arrays = lay_out(**{k: np.asarray(v) for k, v in inputs.items()})
    nc = _bacc.Bacc("TRN2", target_bir_lowering=False, num_devices=1, dynamic_dma_scratch_size=1024)
    aps = {name: nc.dram_tensor(f"in_{name}", a.shape, mybir.dt.from_np(a.dtype), kind="ExternalInput").ap()
           for name, a in arrays.items()}
    out = nc.dram_tensor("out", (P, KT, SEQ), mybir.dt.float32, kind="ExternalOutput").ap()
    build_trunk(nc, aps["stream"], aps["small"], aps["p"], aps["x"], aps["positions"], aps["const"], out)
    r = _run(nc, [{f"in_{k}": v for k, v in arrays.items()}], core_ids=[0])
    got = r.results[0]["out"]
    return np.ascontiguousarray(got.transpose(2, 1, 0).reshape(1, SEQ, D_MODEL))
```

```python
from contextlib import ExitStack

import numpy as np

import concourse.bass as bass
from concourse import mybir

D_MODEL, SEQ, DEPTH, CHUNK = 1024, 256, 2, 64
A_HEADS, A_KV, A_DH = 8, 2, 64
B_HEADS, B_DH, C_WIDTH = 4, 128, 512
PLE_DIM = 256
HEADS, NKEYS, TOPK = 8, 128, 16
EPS = 1e-6
ROPE_THETA = 10000.0
LRU_C = 8.0
P = 128
KT = D_MODEL // P
MT_ = SEQ // P
RING = 4
HIGHS = 2

STREAM = ([f"bqkv{i}" for i in range(6)] + ["aq0", "aq1", "akv", "cx0", "cx1", "bg0", "lru", "bg1"]
          + ["cy0", "cy1"] + [f"ga{i}" for i in range(4)] + [f"gb{i}" for i in range(4)]
          + [f"gc{i}" for i in range(4)]
          + ["wa0", "wa1", "wc0", "wc1", "wb0", "wb1"] + [f"wo{i}" for i in range(4)]
          + [f"wq{i}" for i in range(8)] + ["keys"]
          + [f"u{i}" for i in range(64)] + [f"v{i}" for i in range(64)]
          + ["pp"] + [f"pg{i}" for i in range(4)])
NPAIR = len(STREAM)
AHEAD = 3
assert NPAIR % RING == 0 and NPAIR % HIGHS == 0 and DEPTH == 2
AT = {name: n for n, name in enumerate(STREAM)}

UNIT = {"bqkv": 0, "aq": 12, "ak": 16, "av": 17, "cx": 18, "bg": 22, "cy": 26, "ga": 30, "gb": 38, "gc": 46}
NUNIT = 54
PROJ = [name for name in STREAM[:AT["wa0"]] if name != "lru"]
USE = {name: n + (4 if AT[name] > AT["lru"] else 0) for n, name in enumerate(PROJ)}
USE["lru"] = USE["bg1"] - 4
for _name, _n in (("wq", 8), ("u", 64), ("pg", 4)):
    for _i in range(_n):
        USE[f"{_name}{_i}"] = 1 + max(USE.values())
WHOLE = [AT[name] for name in ("lru", "keys", "pp")]


def split_units(pair, unit=0):
    return 2 * (pair - 1 - sum(w < pair for w in WHOLE)) + unit + 1


MOVING, _at = {}, 0
for _name, _n in [("norm1", 4), ("ya", 2), ("yc", 2), ("ob", 2), ("mix", 4), ("norm2", 4), ("coef", 64), ("norm3", 4)]:
    MOVING[_name] = _at
    _at += _n

CONST = {}
_at = 0
for _name, _n in [("ident", P), ("ones", P), ("iota", P), ("freq", 1), ("sign", 1), ("final", KT)]:
    CONST[_name] = (_at, _at + _n)
    _at += _n
NCONST = _at
MIXC = {}
_at = 0
for _name, _n in [("tri", P), ("blk", P), ("chunk", 2 * P), ("level", 6 * P), ("rot", P), ("mask0", P),
                  ("mask1", 2 * P)]:
    MIXC[_name] = (_at, _at + _n)
    _at += _n
NMIXC = _at
SMALL = {}
_at = 0
for _name, _n in [("n_mix", KT), ("n_ffn", KT), ("n_ple", KT), ("bconv", 48), ("cconv", 16), ("cbias", 4),
                  ("ba", 4), ("bi", 4), ("lam", 4), ("dnorm", 1), ("sink", A_HEADS), ("alog", B_HEADS),
                  ("dt", B_HEADS), ("wba", KT * 8)]:
    SMALL[_name] = (_at, _at + _n)
    _at += _n
NSMALL = _at


def build_trunk(nc, stream, small_dram, p_dram, x_in, pos_in, const_in, mixc_dram, out):
    f32, f32r, i32, u32 = mybir.dt.float32, mybir.dt.float32r, mybir.dt.int32, mybir.dt.uint32
    bf16 = mybir.dt.bfloat16
    ALU = mybir.AluOpType
    ACT = mybir.ActivationFunctionType
    AX = mybir.AxisListType.X
    ADD, SUB, MUL, MAX = ALU.add, ALU.subtract, ALU.mult, ALU.max
    ctx = ExitStack()
    with ctx:
        start_of = {}

        def sb(name, shape, dt=f32):
            start_of[name] = (nc.sbuf_base + 31) // 32 * 32
            return ctx.enter_context(nc.sbuf_tensor(name, shape, dt))

        def over_(name, shape, dt, under, words=0):
            return nc.alloc_sbuf_tensor_at(name, shape, dt, offset=start_of[under] + 4 * words)

        ring = [sb(f"ring{i}", [P, 2048]) for i in range(RING)]
        low = [over_(f"low{i}", [P, 2048], f32r, f"ring{i}") for i in range(RING)]
        high = [sb(f"high{i}", [P, 2048], f32r) for i in range(HIGHS)]
        h = sb("h", [P, KT, SEQ])
        n = sb("n", [P, KT, SEQ])
        n_low = over_("n_low", [P, KT, SEQ], f32r, "n")
        n_high = sb("n_high", [P, KT, SEQ], f32r)
        big = sb("big", [P, 32768])
        const = sb("const", [P, NCONST])
        mixc = sb("mixc", [P, NMIXC])
        small = sb("small", [P, NSMALL])
        ple = sb("ple", [P, 2, SEQ])
        cos = sb("cos", [P, SEQ])
        sin = sb("sin", [P, SEQ])
        tiny = sb("tiny", [P, 320])
        eps = sb("eps", [P, 1])
        picks_ = sb("picks", [P, 6, P])
        wba_high = sb("wba_high", [P, KT * 8], f32r)
        wba_low = sb("wba_low", [P, KT * 8], f32r)
        route = sb("route", [P, 3, SEQ])
        bank = [ctx.enter_context(nc.psum_tensor(f"bank{i}", [P, 512], f32)) for i in range(8)]

        def c(name):
            a, b = CONST[name] if name in CONST else MIXC[name]
            return (const if name in CONST else mixc)[:, a:b]

        def s(name):
            a, b = SMALL[name]
            return small[:, a:b]

        def area(at, *shape):
            size = int(np.prod(shape))
            v = big[:, at:at + size]
            if len(shape) == 2:
                v = v.rearrange("p (a b) -> p a b", a=shape[0])
            elif len(shape) == 3:
                v = v.rearrange("p (a b c) -> p a b c", a=shape[0], b=shape[1])
            return v

        def two(b):
            return bank[b][:, :].rearrange("p (u t) -> p u t", u=2)

        def four(b):
            return bank[b][:, :].rearrange("p (u t) -> p u t", u=4)

        ident, ones, tri = c("ident"), c("ones"), c("tri")

        z = area(0, NUNIT, SEQ)
        CV = NUNIT * SEQ
        cv = area(CV, 12, SEQ)
        sq = area(CV, KT, SEQ)
        F0 = CV + 12 * SEQ
        qk = area(F0, 5, SEQ)
        sc0 = area(F0 + 1280, A_HEADS, P)
        sc1 = area(F0 + 2304, A_HEADS, SEQ)
        pt0 = area(F0 + 4352, A_HEADS, P)
        pt1 = area(F0 + 5376, 2, 1024)
        ropet = area(F0 + 4352, 5, SEQ)
        ya = area(12 * SEQ, 4, SEQ)
        xc = area(0, 4, SEQ)
        lr = area(1024, 4, SEQ)
        li = area(2048, 4, SEQ)
        yc = area(18 * SEQ, 4, SEQ)
        G0 = F0 + 7424
        l2 = area(G0, 8, SEQ)
        egb = area(G0, 2, 512)
        dec = area(G0 + 1024, 2, 512)
        lo = area(G0 + 2048, 2, 512)
        qkd = area(G0 + 3072, 2, 512)
        ct = area(G0 + 4096, 2, 512)
        mm_ = area(G0 + 5120, 2, 512)
        mt = area(G0 + 6144, 2, 512)
        xx = area(G0 + 7168, 2, 512)
        lt = area(G0 + 5120, 4, SEQ)
        lw = area(G0 + 6144, 4, SEQ)
        vn = area(G0 + 5120, 512)
        state = area(G0 + 5632, 512)
        ob = area(1024, 4, SEQ)
        osq = area(2048, 4, SEQ)
        vtok = area(16 * SEQ, 2, P)
        mix = area(CV, KT, SEQ)
        mixt = area(F0, 2, SEQ)
        assert G0 + 8192 <= 32768
        ob_high = over_("ob_high", [P, 4, SEQ], f32r, "big", G0)
        ob_low = over_("ob_low", [P, 4, SEQ], f32r, "big", G0 + 1024)
        act_h = area(0, NKEYS, SEQ)
        Q0 = 16384
        qt = area(Q0, 16, SEQ)
        sub = area(Q0 + 4096, 2, 2048)
        sub2 = area(Q0 + 8192, 2048)
        cand = area(Q0 + 12288, 2048)
        cand2 = area(Q0 + 14336, 2048)
        tops = area(Q0, 2, 256)
        topi = big[:, Q0 + 512:Q0 + 1024].bitcast(u32).rearrange("p (m k) -> p m k", m=2)
        best = area(Q0 + 1536, 2, P)
        besti = big[:, Q0 + 1792:Q0 + 2048].bitcast(u32).rearrange("p (m k) -> p m k", m=2)
        half = big[:, Q0 + 2048:Q0 + 2304].bitcast(u32).rearrange("p (m k) -> p m k", m=2)
        halff = area(Q0 + 2304, 2, P)
        picks = picks_[:, :, :].rearrange("p (m k) c -> p m k c", m=2)
        gsum = area(Q0 + 3328, 2, HEADS)
        mx = tiny[:, 0:16].rearrange("p (m a) -> p m a", m=2)
        nmx = tiny[:, 16:32].rearrange("p (m a) -> p m a", m=2)
        den = tiny[:, 32:48].rearrange("p (m a) -> p m a", m=2)
        esink = tiny[:, 48:64].rearrange("p (m a) -> p m a", m=2)
        sp = tiny[:, 64:76]
        sa, se, ss, ssq, spo = (tiny[:, 76 + 12 * i:88 + 12 * i] for i in range(5))
        beta = tiny[:, 136:144].rearrange("p (m a) -> p m a", m=2)
        ag = tiny[:, 144:152].rearrange("p (m a) -> p m a", m=2)
        gs = tiny[:, 152:184].rearrange("p (m k a) -> p m k a", m=2, k=4)
        egs = tiny[:, 184:216].rearrange("p (m k a) -> p m k a", m=2, k=4)
        bg_ = tiny[:, 216:224].rearrange("p (m a) -> p m a", m=2)
        nea = tiny[:, 224:228]
        lrs = tiny[:, 228:232]
        lrn = tiny[:, 232:236]
        rn = tiny[:, 240:256]
        on = tiny[:, 256:264]
        rq = tiny[:, 264:266]
        warm_ = tiny[:, 319:320]

        HALF = NKEYS // 2
        GROUPS = SEQ // 4
        FREE_BANK = (2, 1)
        hot1 = [over_(f"hot1_{b}", [P, 4, P], bf16, "mixc", b * 768) for b in range(2)]
        hot2 = [over_(f"hot2_{b}", [P, 4, 3, HALF], bf16, "mixc", b * 768 + 384) for b in range(2)]
        gate3 = over_("gate3", [P, SEQ, 3], bf16, "picks")
        assert 2 * 768 <= NMIXC
        PLE_BANKS = (6, 7, 0, 1)

        def sem(name):
            return ctx.enter_context(nc.semaphore(name))

        slot = [sem(f"slot{i}") for i in range(RING)]
        names = """
            ple_in used coef_ready n_ready low_ready x_low sq_added squares sums rms_inv rstd_full
            hot_ready gates_full pj_free wba_low ba_full rot_full l2sq_ready l2_sums alpha_ready g_full
            roped vtok_ready l2_inv l2_full xc_ready lru_full g_dif qkn_ready scores_full masked gcb_full
            kk_full normed dec_exp pt_full level_ready pt_ready qk_full pv_full ya_ready inverse_ready
            x_full x_ready transpose_ready qkd_ready p_full tok_full tok_ready w_full w_ready qg_ready
            vn_full s_ready o_ready vn_ready s_full o_full br_read osq_ready osum_full o_inv o_spread
            sub_ready sub_full picks_ready tr_full v_full achain high_ready x_high h_new rms_ready
            conv_ready silu_ready wba_split sp_in sp_exp l2_root tanh_ready lru_a lru_sqrt rowmax_ready
            exps_ready g_exp dif_ready yc_ready o_root yb_ready exp_in exp_out vchain route_ready
            ones_ready""".split()
        S = {name: sem(name) for name in names}
        layer_sems = range(slot[0].num, S[names[-1]].num + 1)
        assert len(layer_sems) == RING + len(names)
        ahead = [sem(f"ahead{i}") for i in range(AHEAD)]
        small_in = sem("small_in")
        mixc_in = sem("mixc_in")
        io = sem("io")
        first = {name: sem(f"first_{name}") for name in ("squares", "sums", "root", "inv", "high", "low")}
        x_half = [sem(f"x_half{i}") for i in range(2)]
        setup = sem("setup")
        setup2 = sem("setup2")
        angle = sem("angle")
        trig = sem("trig")
        stored = sem("stored")
        stored_out = sem("stored_out")

        class Order:
            def __init__(self, engine, chain):
                self.engine, self.chain, self.n = engine, chain, 0

            def link(self, ins):
                self.n += 1
                ins.then_inc(self.chain, 1)
                self.engine.wait_ge(self.chain, self.n)

        def sums_of_squares(b, tiles):
            for t in tiles:
                for m in range(MT_):
                    last = nc.tensor.matmul(bank[b][:, m:m + 1], sq[:, t, m * P:(m + 1) * P], ones[:, 0:1],
                                            start=t == 0 and m == 0, stop=t == KT - 1, skip_group_check=True)
            return last

        def root_of(b):
            return nc.scalar.activation(rq, bank[b][:, 0:MT_], ACT.Sqrt, scale=1.0 / D_MODEL, bias=eps[:, :])

        def spread(b):
            for m in range(MT_):
                last = nc.tensor.matmul(bank[b][:, 256 + m * P:256 + (m + 1) * P], rq[:, m:m + 1].to_broadcast([P, P]),
                                        ident, start=True, stop=True)
            return last

        with nc.Block() as block:
            @block.sync
            def _(sync):
                sync.dma_start(area(0, 256).bitcast(i32), pos_in.partition_broadcast(P)).then_inc(io, 16)
                sync.dma_start(const[:, :], const_in).then_inc(io, 16)
                for half_ in range(2):
                    tiles = slice(4 * half_, 4 * half_ + 4)
                    sync.dma_start(h[:, tiles, :], x_in[:, tiles, :]).then_inc(x_half[half_], 16)
                sync.dma_start(ring[0][:, :], stream[0]).then_inc(ahead[0], 16)
                sync.dma_start(small[:, :], small_dram[0]).then_inc(small_in, 16)
                sync.dma_start(mixc[:, :], mixc_dram).then_inc(mixc_in, 16)
                for i in range(1, AHEAD):
                    sync.dma_start(ring[i][:, :], stream[i]).then_inc(ahead[i], 16)

            @block.vector
            def _(dve):
                o = Order(dve, setup)
                ang, turns, rest, cosr = area(256, 256), area(512, 256), area(768, 256), area(1024, 256)
                dve.wait_ge(io, 32)
                o.link(nc.vector.tensor_copy(turns, area(0, 256).bitcast(i32)))
                o.link(nc.vector.tensor_scalar(ang, turns, c("freq"), None, MUL))
                o.link(nc.vector.tensor_scalar(turns, ang, float(1 / (2 * np.pi)), 12582912.0, MUL, ADD))
                o.link(nc.vector.tensor_scalar(turns, turns, -12582912.0, None, ADD))
                step1 = 6.28125
                step2 = round((2 * np.pi - step1) * 2 ** 20) / 2 ** 20
                step3 = float(2 * np.pi - step1 - step2)
                o.link(nc.vector.scalar_tensor_tensor(rest, turns, -step1, ang, MUL, ADD))
                o.link(nc.vector.scalar_tensor_tensor(rest, turns, -step2, rest, MUL, ADD))
                o.link(nc.vector.scalar_tensor_tensor(rest, turns, -step3, rest, MUL, ADD))
                o.link(nc.vector.tensor_scalar(cosr, rest, float(np.pi / 2), None, ADD))
                o.link(nc.vector.tensor_scalar(turns, cosr, float(np.pi), float(2 * np.pi), ALU.is_gt, MUL))
                o.link(nc.vector.tensor_tensor(cosr, cosr, turns, SUB))
                top = 3.1415925
                nc.vector.tensor_scalar(rest, rest, -top, top, MAX, ALU.min).then_inc(angle, 1)
                nc.vector.tensor_scalar(cosr, cosr, -top, top, MAX, ALU.min).then_inc(angle, 1)
                dve.wait_ge(trig, 2)
                nc.vector.tensor_scalar(sin[:, :], sin[:, :], c("sign"), None, MUL).then_inc(setup2, 1)
                dve.wait_ge(setup2, 1)
                dve.wait_ge(first["root"], 1)
                nc.vector.reciprocal(rq, rq).then_inc(first["inv"], 1)

            @block.gpsimd
            def _(pool):
                nc.gpsimd.memset(eps[:, :], EPS).then_inc(stored, 1)
                pool.wait_ge(stored, 1)
                for unit in range(2):
                    cols = slice(unit * 1024, (unit + 1) * 1024)
                    pool.wait_ge(first["high"], unit + 1)
                    nc.gpsimd.tensor_tensor(low[0][:, cols], ring[0][:, cols], high[0][:, cols].bitcast(f32), SUB)\
                        .then_inc(first["low"], 1)
                pool.wait_ge(first["low"], 2)

            @block.tensor
            def _(pe):
                for t in range(KT):
                    pe.wait_ge(first["squares"], t + 1)
                    last = sums_of_squares(5, (t,))
                last.then_inc(first["sums"], 1)
                pe.wait_ge(first["inv"], 1)
                spread(5)

            @block.scalar
            def _(act):
                act.wait_ge(stored, 1)
                for t in range(KT):
                    if t % 4 == 0:
                        act.wait_ge(x_half[t // 4], 16)
                    nc.scalar.activation(sq[:, t, :], h[:, t, :], ACT.Square).then_inc(first["squares"], 1)
                act.wait_ge(angle, 2)
                nc.scalar.activation(sin[:, :], area(768, 256), ACT.Sin).then_inc(trig, 1)
                nc.scalar.activation(cos[:, :], area(1024, 256), ACT.Sin).then_inc(trig, 1)
                act.wait_ge(ahead[0], 16)
                for unit in range(2):
                    cols = slice(unit * 1024, (unit + 1) * 1024)
                    nc.scalar.activation(high[0][:, cols], ring[0][:, cols], ACT.Copy).then_inc(first["high"], 1)
                act.wait_ge(first["sums"], 1)
                root_of(5).then_inc(first["root"], 1)

        with nc.Fori(0, DEPTH) as layer:
            with nc.Block() as block:

                @block.sync
                def _(sync):
                    def load(i, pair, to=None):
                        sync.dma_start(ring[i][:, :], stream[pair]).then_inc(to or slot[i], 16)

                    for i in range(AHEAD, RING):
                        load(i, layer * NPAIR + i)
                    sync.dma_start(ple[:, :, :], p_dram[layer]).then_inc(S["ple_in"], 16)
                    with sync.Fori(1, NPAIR // RING) as lap:
                        for i in range(RING):
                            sync.wait_ge(S["used"], (lap - 1) * (2 * RING) + 2 * (i + 1))
                            load(i, layer * NPAIR + lap * RING + i)
                    sync.wait_ge(S["coef_ready"], 2 * GROUPS)
                    sync.dma_start(mixc[:, :], mixc_dram).then_inc(mixc_in, 16)
                    sync.wait_ge(S["n_ready"], 12)
                    sync.dma_start(small[:, :], small_dram[1 - layer]).then_inc(small_in, 16)
                    for i in range(AHEAD):
                        sync.wait_ge(S["used"], 2 * (AT["pg0"] + i + 1))
                        load(i, (1 - layer) * NPAIR + i, ahead[i])

                @block.tensor
                def _(pe):
                    mmul = nc.tensor.matmul

                    def arrived(pair, lap=None):
                        i, k = pair % RING, 16 * (pair // RING + (pair % RING >= AHEAD))
                        pe.wait_ge(slot[i], k if lap is None else lap * 16 + k)
                        return ring[i]

                    def parts(pair, unit, lap=None):
                        k = split_units(pair, unit)
                        if pair:
                            pe.wait_ge(S["low_ready"], k if lap is None else lap * (2 * RING) + k)
                        return high[pair % HIGHS], low[pair % RING]

                    def moving(name, step=None):
                        pe.wait_ge(S["x_low"], MOVING[name] + step + 1)

                    def product(dst, w, at, x_high, x_low, first, final, loose=False):
                        w_high, w_low = w[0][:, at:at + P], w[1][:, at:at + P]
                        mmul(dst, w_high, x_high, start=first, stop=False, skip_group_check=loose)
                        mmul(dst, w_high, x_low, start=False, stop=False, skip_group_check=loose)
                        return mmul(dst, w_low, x_high, start=False, stop=final, skip_group_check=loose)

                    def keep_clock(count, b):
                        for _ in range(count):
                            mmul(bank[b][:, 0:P], ident, ident, start=True, stop=True)

                    def norm_sums(k, b):
                        pe.wait_ge(S["sq_added"], k + 1)
                        sums_of_squares(b, (0,))
                        pe.wait_ge(S["squares"], 4 * k + 4)
                        sums_of_squares(b, (6, 7)).then_inc(S["sums"], 1)

                    def norm_spread(k, b):
                        pe.wait_ge(S["rms_inv"], k + 1)
                        spread(b).then_inc(S["rstd_full"], 1)

                    def gates(b, group):
                        pe.wait_ge(S["hot_ready"], group + 1)
                        for k in range(4):
                            for part_ in range(3):
                                last = mmul(bank[6 + b][:, k * HALF:(k + 1) * HALF], hot1[b][:, k, :],
                                            hot2[b][:, k, part_, :], start=part_ == 0, stop=part_ == 2)
                        last.then_inc(S["gates_full"], 1)

                    def project(name, lap=None, fresh=None, base=0, group=None, before=None):
                        pair, use = AT[name], USE[name]
                        if use >= 2:
                            pe.wait_ge(S["pj_free"], use - 1 if lap is None else lap * RING + (use - 1))
                        dst = two(base + use % 2)
                        if fresh:
                            w = [parts(pair, u) for u in range(2)]
                            for t in range(KT):
                                if t % 2 == 0:
                                    moving(fresh, t // 2)
                                for u in range(2):
                                    last = product(dst[:, u, :], w[u], (u * KT + t) * P, n_high[:, t, :], n_low[:, t, :],
                                                   not t and not u, t == KT - 1, loose=True)
                            last.then_inc(S["used"], 2)
                            return
                        for u in range(2):
                            if group is not None and not u:
                                gates(0, group)
                                gates(1, group + 1)
                            if before:
                                before(u)
                            w = parts(pair, u, lap)
                            for t in range(KT):
                                last = product(dst[:, u, :], w, (u * KT + t) * P, n_high[:, t, :], n_low[:, t, :],
                                               t == 0, t == KT - 1)
                            last.then_inc(S["used"], 1)

                    def heads(m):
                        return [(hd, slice(hd * P, (hd + 1) * P)) for hd in range(B_HEADS)]

                    keep_clock(12, 6)
                    project("bqkv0", fresh="norm1")
                    ba = [(m, t) for m in range(MT_) for t in range(KT)]
                    pe.wait_ge(S["wba_low"], 1)

                    def ba_products(count):
                        for _ in range(count):
                            m, t = ba.pop(0)
                            cols = slice(t * 8, (t + 1) * 8)
                            for k, (x, w) in enumerate(((n_high, wba_high), (n_low, wba_high), (n_high, wba_low))):
                                last = mmul(bank[3][:, m * 8:(m + 1) * 8], x[:, t, m * P:(m + 1) * P], w[:, cols],
                                            start=not t and not k, stop=t == KT - 1 and k == 2)
                        if not ba:
                            last.then_inc(S["ba_full"], 1)

                    for i in range(1, 6):
                        project(f"bqkv{i}", before=lambda u: ba_products(2) if ba else None)
                    for name in ("aq0", "aq1", "akv", "cx0"):
                        project(name)
                    pe.wait_ge(S["pj_free"], 9)
                    for u in range(5):
                        last = mmul(two(4 + u // 2)[:, u % 2, :], c("rot"), z[:, 12 + u, :], start=True, stop=True)
                    last.then_inc(S["rot_full"], 1)
                    for m in range(MT_):
                        last = nc.tensor.transpose(bank[7][:, m * P:(m + 1) * P], z[:, 17, m * P:(m + 1) * P], ident)
                    last.then_inc(S["rot_full"], 1)
                    pe.wait_ge(S["l2sq_ready"], 1)

                    def l2_products(m):
                        for u in range(8):
                            last = mmul(bank[2][:, 2 * u + m:2 * u + m + 1], l2[:, u, m * P:(m + 1) * P], ones[:, 0:1],
                                        start=True, stop=True)
                        if m:
                            last.then_inc(S["l2_sums"], 1)

                    project("cx1", before=l2_products)
                    project("bg0")
                    pe.wait_ge(S["alpha_ready"], 1)
                    for m in range(MT_):
                        chunk = c("chunk")
                        for k, w in enumerate((tri, c("blk"), chunk[:, 0:P], chunk[:, P:2 * P])):
                            at = m * 16 + k * 4
                            last = mmul(bank[3][:, at:at + 4], w, ag[:, m, :], start=True, stop=True)
                    last.then_inc(S["g_full"], 1)
                    pe.wait_ge(S["roped"], 1)
                    pe.wait_ge(S["vtok_ready"], 1)
                    pe.wait_ge(S["l2_inv"], 1)
                    for u in range(8):
                        for m in range(MT_):
                            k = 2 * u + m
                            last = mmul(two(4 + u // 2)[:, u % 2, m * P:(m + 1) * P], rn[:, k:k + 1].to_broadcast([P, P]),
                                        ident, start=True, stop=True)
                    last.then_inc(S["l2_full"], 1)
                    pe.wait_ge(S["xc_ready"], 1)
                    w = arrived(AT["lru"])
                    for k in range(8):
                        use = USE["lru"] + k // 2
                        if k % 2 == 0:
                            pe.wait_ge(S["pj_free"], use - 1)
                        last = mmul(two(use % 2)[:, k % 2, :], w[:, k * P:(k + 1) * P], xc[:, k % 4, :],
                                    start=True, stop=True)
                        if k % 2 == 1 and k < 7:
                            last.then_inc(S["lru_full"], 1)
                    last.then_inc(S["used"], 2)
                    project("bg1")

                    pe.wait_ge(S["g_dif"], 1)
                    for m in range(MT_):
                        if m:
                            pe.wait_ge(S["qkn_ready"], 1)
                        for hd in range(A_HEADS):
                            half_ = slice(64 * (hd // 4), 64 * (hd // 4) + 64)
                            keys = (m + 1) * P
                            dst = four(2 + hd // 4)[:, hd % 4, :] if m == 0 else two(4 + hd // 2)[:, hd % 2, :]
                            last = mmul(dst, qk[half_, hd % 4, m * P:(m + 1) * P], qk[half_, 4, 0:keys],
                                        start=True, stop=True)
                        last.then_inc(S["scores_full"], 1)
                    project("cy0")
                    project("cy1")
                    pe.wait_ge(S["masked"], 6)
                    for m, b in enumerate((7, 2)):
                        for hd, at in heads(m):
                            last = mmul(bank[b][:, at], ag[:, m, hd:hd + 1].to_broadcast([P, P]), tri,
                                        start=True, stop=True)
                    last.then_inc(S["gcb_full"], 1)
                    for m, b in enumerate((3, 4)):
                        for hd, at in heads(m):
                            last = mmul(bank[b][:, at], beta[:, m, hd:hd + 1].to_broadcast([P, P]), ident,
                                        start=True, stop=True)
                    for m, b in enumerate((5, 6)):
                        for hd, at in heads(m):
                            k = cv[:, 4 + hd, m * P:(m + 1) * P]
                            last = mmul(bank[b][:, at], k, k, start=True, stop=True)
                    last.then_inc(S["kk_full"], 1)
                    project("ga0")
                    project("ga1")
                    pe.wait_ge(S["normed"], 1)
                    pe.wait_ge(S["dec_exp"], 1)
                    for hd in range(A_HEADS):
                        last = nc.tensor.transpose(four((7, 2)[hd // 4])[:, hd % 4, :], sc0[:, hd, :], ident)
                    last.then_inc(S["pt_full"], 1)
                    project("ga2")
                    pe.wait_ge(S["normed"], 2)
                    pe.wait_ge(S["level_ready"], 1)
                    for kt in range(MT_):
                        for hd in range(A_HEADS):
                            last = nc.tensor.transpose(four(3 + 2 * kt + hd // 4)[:, hd % 4, :],
                                                       sc1[:, hd, kt * P:(kt + 1) * P], ident)
                    last.then_inc(S["pt_full"], 1)
                    pe.wait_ge(S["pt_ready"], 2)
                    for m, b in enumerate((7, 2)):
                        for hd, at in heads(m):
                            last = mmul(bank[b][:, at], cv[:, 4 + hd, m * P:(m + 1) * P],
                                        cv[:, hd, m * P:(m + 1) * P], start=True, stop=True)
                    last.then_inc(S["qk_full"], 1)
                    project("ga3")
                    pe.wait_ge(S["pt_ready"], 6)
                    for g in range(A_KV):
                        mmul(bank[3 + g][:, :], vtok[:, 0, :], pt0[:, 4 * g:4 * g + 4, :], start=True, stop=True)
                        for kt in range(MT_):
                            last = mmul(bank[5 + g][:, :], vtok[:, kt, :], pt1[:, kt, g * 512:(g + 1) * 512],
                                        start=kt == 0, stop=kt == MT_ - 1)
                    last.then_inc(S["pv_full"], 1)
                    project("gb0")

                    pe.wait_ge(S["ya_ready"], 1)
                    for level in range(6):
                        pe.wait_ge(S["level_ready"], level + 1)
                        for m, b in enumerate((3, 4)):
                            if level:
                                pe.wait_ge(S["inverse_ready"], 2 * level - 1 + m)
                            for hd, at in heads(m):
                                last = mmul(bank[b][:, at], ct[:, m, at], mm_[:, m, at] if level else ident,
                                            start=True, stop=True)
                            last.then_inc(S["x_full"], 1)
                        if not level:
                            project("gb1")
                            continue
                        for m in range(MT_):
                            pe.wait_ge(S["x_ready"], 2 * level - 1 + m)
                            pe.wait_ge(S["transpose_ready"], 2 * level - 1 + m)
                            if level == 1 and not m:
                                pe.wait_ge(S["qkd_ready"], 1)
                            if level < 5:
                                for hd, at in heads(m):
                                    mmul(bank[5 + m][:, at], mt[:, m, at], xx[:, m, at], start=True, stop=True)
                            for hd, at in heads(m):
                                last = mmul(bank[(7, 2)[m]][:, at], xx[:, m, at], mt[:, m, at], start=True, stop=True)
                            last.then_inc(S["p_full"], 1)
                    for m in range(MT_):
                        for hd, at in heads(m):
                            nc.tensor.transpose(bank[3 + m][:, at], cv[:, 4 + hd, m * P:(m + 1) * P], ident)
                            last = nc.tensor.transpose(bank[5 + m][:, at], cv[:, 8 + hd, m * P:(m + 1) * P], ident)
                    last.then_inc(S["tok_full"], 1)
                    project("gb2")
                    pe.wait_ge(S["transpose_ready"], 12)
                    pe.wait_ge(S["tok_ready"], 1)
                    for m, b in enumerate((7, 2)):
                        for hd, at in heads(m):
                            last = mmul(bank[b][:, at], ct[:, m, at], mt[:, m, at], start=True, stop=True)
                    last.then_inc(S["w_full"], 1)
                    project("gb3")
                    pe.wait_ge(S["w_ready"], 2)
                    pe.wait_ge(S["qg_ready"], 1)

                    def new_values(ch):
                        for hd, at in heads(ch // 2):
                            last = mmul(bank[3 + ch % 2][:, at], mt[:, ch // 2, at], xx[:, ch // 2, at],
                                        start=not hd, stop=not ch, skip_group_check=True)
                        return last

                    new_values(0).then_inc(S["vn_full"], 1)
                    for ch in range(SEQ // CHUNK):
                        m, r = ch // 2, ch % 2
                        rows = slice(CHUNK * r, CHUNK * (r + 1))
                        outs = [(bank[5 + ch % 2][:, hd * CHUNK:(hd + 1) * CHUNK],
                                 slice(hd * P + CHUNK * r, hd * P + CHUNK * (r + 1))) for hd in range(B_HEADS)]
                        if ch:
                            pe.wait_ge(S["s_ready"], ch)
                            for hd, at in heads(m):
                                last = mmul(bank[3 + ch % 2][:, at], dec[:, m, at], state[:, at], start=False, stop=True,
                                            skip_group_check=True)
                            last.then_inc(S["vn_full"], 1)
                            if ch >= 2:
                                pe.wait_ge(S["o_ready"], ch - 1)
                            for hd, at in heads(m):
                                mmul(outs[hd][0], state[:, at], egb[:, m, outs[hd][1]], start=not hd, stop=False,
                                     skip_group_check=True)
                        else:
                            project("gc0")
                        pe.wait_ge(S["vn_ready"], ch + 1)
                        if ch < 3:
                            for hd, at in heads(m):
                                last = mmul(bank[7][:, at], lo[rows, m, at], vn[rows, at], start=True, stop=True)
                            last.then_inc(S["s_full"], 1)
                        for hd, at in heads(m):
                            last = mmul(outs[hd][0], vn[rows, at], qkd[rows, m, outs[hd][1]], start=not ch and not hd,
                                        stop=True, skip_group_check=True)
                        last.then_inc(S["o_full"], 1)
                        if ch < 3:
                            new_values(ch + 1)
                            project(f"gc{ch + 1}")
                    y_parts = {"ya": (n_high[:, 0:4, :], n_low[:, 0:4, :]), "yc": (n_high[:, 4:8, :], n_low[:, 4:8, :]),
                               "ob": (ob_high, ob_low)}
                    for q, (name, y) in enumerate((("wa0", "ya"), ("wa1", "ya"), ("wc0", "yc"), ("wc1", "yc"),
                                                   ("wb0", "ob"), ("wb1", "ob"))):
                        moving(y, 1)
                        if q >= 2:
                            pe.wait_ge(S["br_read"], q - 1)
                        for u in range(2):
                            w = parts(AT[name], u)
                            for j in (2 * u, 2 * u + 1):
                                for t in range(4):
                                    last = product(two(3 + 2 * (q % 2) + j // 2)[:, j % 2, :], w, (j * 4 + t) * P,
                                                   y_parts[y][0][:, t, :], y_parts[y][1][:, t, :], t == 0, t == 3)
                            last.then_inc(S["used"], 1)
                        if not q:
                            pe.wait_ge(S["osq_ready"], 1)
                            for hd in range(B_HEADS):
                                for m in range(MT_):
                                    k = 2 * hd + m
                                    last = mmul(bank[2][:, k:k + 1], osq[:, hd, m * P:(m + 1) * P], ones[:, 0:1],
                                                start=True, stop=True)
                            last.then_inc(S["osum_full"], 1)
                        if q == 1:
                            pe.wait_ge(S["o_inv"], 1)
                            for k in range(8):
                                last = mmul(two((7, 2)[k // 4])[:, k // 2 % 2, k % 2 * P:(k % 2 + 1) * P],
                                            on[:, k:k + 1].to_broadcast([P, P]), ident, start=True, stop=True)
                            last.then_inc(S["o_spread"], 1)
                    wo_parts = {}
                    for tiles in (range(0, 4), range(4, 8)):
                        for i, b in enumerate((7, 2)):
                            for u in range(2):
                                if not tiles[0]:
                                    wo_parts[i, u] = parts(AT[f"wo{i}"], u)
                                for t in tiles:
                                    if not i and not u and t % 2 == 0:
                                        moving("mix", t // 2)
                                    last = product(two(b)[:, u, :], wo_parts[i, u], (u * KT + t) * P, n_high[:, t, :],
                                                   n_low[:, t, :], t == 0 and not u, t == KT - 1, loose=True)
                                if tiles[0]:
                                    last.then_inc(S["used"], 1)
                    for i, b in ((2, 3), (3, 4)):
                        if i == 2:
                            pe.wait_ge(S["br_read"], 6)
                        for u in range(2):
                            w = parts(AT[f"wo{i}"], u)
                            for t in range(KT):
                                last = product(two(b)[:, u, :], w, (u * KT + t) * P, n_high[:, t, :], n_low[:, t, :],
                                               t == 0, t == KT - 1)
                            last.then_inc(S["used"], 1)

                    keep_clock(4, 5)
                    norm_sums(0, 6)
                    keep_clock(3, 5)
                    norm_spread(0, 6)
                    keep_clock(9, 5)
                    for i in range(8):
                        project(f"wq{i}", fresh=None if i else "norm2")
                    w = arrived(AT["keys"])
                    pe.wait_ge(S["pj_free"], USE["u0"])
                    for m in range(MT_):
                        for hs in range(16):
                            b = 2 + (4 * m + hs // 4) % 6
                            if m and hs == 8:
                                pe.wait_ge(S["sub_ready"], 2)
                            last = mmul(four(b)[:, hs % 4, :], qt[:, hs, m * P:(m + 1) * P],
                                        w[:, hs * P:(hs + 1) * P], start=True, stop=True)
                        if m == 0:
                            last.then_inc(S["sub_full"], 1)
                    last.then_inc(S["used"], 2)
                    with pe.Fori(0, 7) as lap:
                        for i in range(RING):
                            project(f"u{i}", lap)
                    pe.wait_ge(S["picks_ready"], 2)
                    pe.wait_ge(S["sub_ready"], 8)
                    for m in range(MT_):
                        for k in range(3):
                            last = nc.tensor.transpose(four(6 + m)[:, k, :], picks[:, m, k, :], ident)
                    last.then_inc(S["tr_full"], 1)
                    for i in range(28, 32):
                        project(f"u{i}")
                    with pe.Fori(0, 8) as lap:
                        for i in range(RING):
                            project(f"u{32 + i}", lap, group=lap * (2 * RING) + 2 * i)

                    def values(v, lap=None, first=False, final=False, group=None):
                        pair = AT["v0"] + v
                        k = MOVING["coef"] + v + 1
                        for e in range(2):
                            if group is not None and not e:
                                gates(0, group)
                                gates(1, group + 1)
                            if not e:
                                pe.wait_ge(S["x_low"], k if lap is None else lap * RING + k)
                            w = parts(pair, e, lap)
                            at = 2 * (v % 4) + e
                            for t in range(KT):
                                last = product(two(2 + t // 2)[:, t % 2, :], w, (e * KT + t) * P,
                                               n_high[:, at, :], n_low[:, at, :],
                                               first and not e and t % 2 == 0, final and e == 1, loose=True)
                            last.then_inc(S["used"], 1)

                    for v in range(4):
                        values(v, first=not v, group=GROUPS + 2 * v)
                    with pe.Fori(0, 7) as lap:
                        for v in range(4, 8):
                            values(v, lap, group=lap * (2 * RING) + (GROUPS + 2 * v))
                    with pe.Fori(0, 7) as lap:
                        for v in range(32, 36):
                            values(v, lap)
                    for v in range(60, 63):
                        values(v)
                    pe.wait_ge(S["x_low"], MOVING["coef"] + 64)
                    last_parts = [parts(AT["v63"], e) for e in range(2)]
                    for t in range(KT):
                        for e in range(2):
                            last = product(two(2 + t // 2)[:, t % 2, :], last_parts[e], (e * KT + t) * P,
                                           n_high[:, 6 + e, :], n_low[:, 6 + e, :], False, e == 1, loose=True)
                        if t % 2 and t < KT - 1:
                            last.then_inc(S["v_full"], 1)
                    last.then_inc(S["used"], 2)

                    w = arrived(AT["pp"])
                    pe.wait_ge(S["ple_in"], 16)
                    for t in range(KT):
                        if t == 4:
                            norm_sums(1, 2)
                        if t == 6:
                            norm_spread(1, 2)
                        for k in range(2):
                            at = (t * 2 + k) * P
                            last = mmul(two(PLE_BANKS[t // 2])[:, t % 2, :], w[:, at:at + P], ple[:, k, :],
                                        start=k == 0, stop=k == 1)
                    last.then_inc(S["used"], 2)
                    for i in range(4):
                        project(f"pg{i}", fresh=None if i else "norm3", base=3)
                    keep_clock(9, 2)
                    norm_sums(2, 5)
                    keep_clock(4, 2)
                    norm_spread(2, 5)

                @block.scalar
                def _(act):
                    A = nc.scalar.activation
                    o = Order(act, S["achain"])

                    def used(units, lap=None):
                        act.wait_ge(S["used"], units if lap is None else lap * (2 * RING) + units)

                    def split(pair, unit, lap=None):
                        if pair in WHOLE or pair > NPAIR:
                            return
                        if not unit:
                            i, k = pair % RING, 16 * (pair // RING + (pair % RING >= AHEAD))
                            if pair < AHEAD:
                                act.wait_ge(ahead[pair], layer * 16 + 16)
                            elif pair == NPAIR:
                                act.wait_ge(ahead[0], layer * 16 + 32)
                            else:
                                act.wait_ge(slot[i], k if lap is None else lap * 16 + k)
                        if pair >= HIGHS:
                            used(2 * (pair - HIGHS) + unit + 1, lap)
                        cols = slice(unit * 1024, (unit + 1) * 1024)
                        A(high[pair % HIGHS][:, cols], ring[pair % RING][:, cols], ACT.Copy).then_inc(S["high_ready"], 1)

                    def empty(name, out_, func, lap=None, base=0):
                        pair, use = AT[name], USE[name]
                        split(pair + HIGHS, 0, lap)
                        used(2 * (pair + 1), lap)
                        A(out_, two(base + use % 2), func).then_inc(S["pj_free"], 1)
                        split(pair + HIGHS, 1, lap)

                    def split_moving(dst, src):
                        A(dst, src, ACT.Copy).then_inc(S["x_high"], 1)

                    def split_n(k, i):
                        act.wait_ge(S["n_ready"], 4 * (k - 1) + i + 1)
                        split_moving(n_high[:, 2 * i:2 * i + 2, :], n[:, 2 * i:2 * i + 2, :])

                    def fill(*names):
                        for name in names:
                            k = PROJ.index(name)
                            func = {"bg": ACT.Silu, "cy": ACT.Gelu_apprx_tanh, "ga": ACT.Sigmoid, "gb": ACT.Sigmoid,
                                    "gc": ACT.Sigmoid}.get(name[:2], ACT.Copy)
                            empty(name, z[:, 2 * k:2 * k + 2, :], func)

                    def warm(func):
                        A(warm_, eps[:, :], func)

                    def square(k, i):
                        act.wait_ge(S["h_new"], 4 * k + i + 1)
                        A(sq[:, 2 * i:2 * i + 2, :], h[:, 2 * i:2 * i + 2, :], ACT.Square).then_inc(S["squares"], 1)

                    def root(k, b):
                        warm(ACT.Sqrt)
                        act.wait_ge(S["sums"], k + 1)
                        root_of(b).then_inc(S["rms_ready"], 1)

                    warm(ACT.Copy)
                    for i in range(4):
                        split_n(1, i)
                    split(1, 0)
                    split(1, 1)

                    def silu(i):
                        act.wait_ge(S["conv_ready"], i + 1)
                        A(cv[:, 2 * i:2 * i + 2, :], cv[:, 2 * i:2 * i + 2, :], ACT.Silu).then_inc(S["silu_ready"], 1)

                    A(wba_high[:, :], s("wba"), ACT.Copy).then_inc(S["wba_split"], 1)
                    fill("bqkv0", "bqkv1")
                    silu(0)
                    fill("bqkv2")
                    silu(1)
                    fill("bqkv3")
                    silu(2)
                    fill("bqkv4")
                    silu(3)
                    act.wait_ge(S["silu_ready"], 4)
                    A(l2[:, :, :], cv[:, 0:8, :], ACT.Square).then_inc(S["l2sq_ready"], 1)
                    fill("bqkv5")
                    silu(4)
                    fill("aq0")
                    silu(5)
                    act.wait_ge(S["sp_in"], 1)
                    A(nea, s("alog"), ACT.Exp).then_inc(S["sp_exp"], 1)
                    A(se, sa, ACT.Exp, scale=-1.0).then_inc(S["sp_exp"], 1)
                    A(beta, beta, ACT.Exp, scale=-1.0).then_inc(S["sp_exp"], 1)
                    fill("aq1", "akv", "cx0")
                    act.wait_ge(S["rot_full"], 2)
                    act.wait_ge(S["roped"], 1)
                    A(vtok[:, :, :], bank[7][:, 0:2 * P].rearrange("p (m c) -> p m c", m=2), ACT.Copy)\
                        .then_inc(S["vtok_ready"], 1)
                    act.wait_ge(S["l2_sums"], 1)
                    A(rn, bank[2][:, 0:16], ACT.Sqrt, bias=eps[:, :]).then_inc(S["l2_root"], 1)
                    fill("cx1", "bg0")
                    warm(ACT.Sigmoid)
                    for k in range(8):
                        if k % 2 == 0 and k < 6:
                            act.wait_ge(S["lru_full"], k // 2 + 1)
                        elif k == 6:
                            used(2 * (AT["lru"] + 1))
                        src = two((USE["lru"] + k // 2) % 2)[:, k % 2, :]
                        gate = A((lr if k < 4 else li)[:, k % 4, :], src, ACT.Sigmoid,
                                 bias=s("ba" if k < 4 else "bi")[:, k % 4:k % 4 + 1])
                        if k % 2 == 1:
                            gate.then_inc(S["pj_free"], 1)
                        if k == 5:
                            split(AT["lru"] + 2, 0)
                    split(AT["lru"] + 2, 1)
                    fill("bg1")
                    act.wait_ge(S["pj_free"], USE["bg1"])
                    for k in range(4):
                        A(lt[:, k, :], lr[:, k, :], ACT.Tanh, scale=lrs[:, k:k + 1]).then_inc(S["tanh_ready"], 1)
                    for k in range(4):
                        act.wait_ge(S["tanh_ready"], k + 1)
                        A(lr[:, k, :], lr[:, k, :], ACT.Exp, scale=lrn[:, k:k + 1]).then_inc(S["lru_a"], 1)
                    A(lt[:, :, :], lt[:, :, :], ACT.Sqrt).then_inc(S["lru_sqrt"], 1)
                    warm(ACT.Exp)
                    for m, sc in ((0, sc0), (1, sc1)):
                        act.wait_ge(S["rowmax_ready"], m + 1)
                        for hd in range(A_HEADS):
                            A(sc[:, hd, :], sc[:, hd, :], ACT.Exp, bias=nmx[:, m, hd:hd + 1],
                              accum_out=den[:, m, hd:hd + 1]).then_inc(S["exps_ready"], 1)
                        A(esink[:, m, :], esink[:, m, :], ACT.Exp).then_inc(S["exps_ready"], 1)
                    A(egs, gs, ACT.Exp).then_inc(S["g_exp"], 1)
                    fill("cy0", "cy1")
                    act.wait_ge(S["dif_ready"], 1)
                    A(dec[:, :, :], dec[:, :, :], ACT.Exp)
                    A(egb[:, 0, :], bank[7][:, :], ACT.Exp)
                    A(egb[:, 1, :], bank[2][:, :], ACT.Exp).then_inc(S["dec_exp"], 1)
                    fill("ga0", "ga1")
                    act.wait_ge(S["pt_full"], 1)
                    for k, b in enumerate((7, 2)):
                        A(pt0[:, 4 * k:4 * k + 4, :], four(b), ACT.Copy).then_inc(S["pt_ready"], 1)
                    fill("ga2")
                    act.wait_ge(S["pt_full"], 2)
                    for b in range(4):
                        A(pt1[:, b // 2, (b % 2) * 512:(b % 2 + 1) * 512], bank[3 + b][:, :], ACT.Copy)\
                            .then_inc(S["pt_ready"], 1)
                    fill("ga3", "gb0", "gb1")
                    for level in range(1, 6):
                        for m in range(MT_):
                            act.wait_ge(S["x_full"], 2 * level + m + 1)
                            A(xx[:, m, :], bank[3 + m][:, :], ACT.Copy).then_inc(S["x_ready"], 1)
                    fill("gb2")
                    act.wait_ge(S["w_full"], 1)
                    for m, b in enumerate((7, 2)):
                        A(dec[:, m, :], bank[b][:, :], ACT.Copy, scale=-1.0).then_inc(S["w_ready"], 1)
                    fill("gb3", "gc0")
                    for ch in range(SEQ // CHUNK):
                        act.wait_ge(S["o_full"], ch + 1)
                        A(ob[:, :, ch * CHUNK:(ch + 1) * CHUNK],
                          bank[5 + ch % 2][:, 0:256].rearrange("p (a i) -> p a i", a=4), ACT.Copy)\
                            .then_inc(S["o_ready"], 1)
                        if ch < 3:
                            fill(f"gc{ch + 1}")
                            if ch == 2:
                                for i in range(2):
                                    split_moving(n_high[:, 2 * i:2 * i + 2, :], ya[:, 2 * i:2 * i + 2, :])
                    act.wait_ge(S["o_ready"], 4)
                    A(osq[:, :, :], ob[:, :, :], ACT.Square).then_inc(S["osq_ready"], 1)
                    act.wait_ge(S["yc_ready"], 1)
                    for i in range(2):
                        split_moving(n_high[:, 2 * i + 4:2 * i + 6, :], yc[:, 2 * i:2 * i + 2, :])
                    warm(ACT.Sqrt)
                    act.wait_ge(S["osum_full"], 1)
                    A(on, bank[2][:, 0:8], ACT.Sqrt, scale=1.0 / B_DH, bias=eps[:, :]).then_inc(S["o_root"], 1)

                    def split_pairs(first, end):
                        for pair in range(first, end):
                            split(pair, 0)
                            split(pair, 1)

                    wa0 = AT["wa0"]
                    split_pairs(wa0 + 2, wa0 + 4)
                    act.wait_ge(S["yb_ready"], 1)
                    for i in range(2):
                        split_moving(ob_high[:, 2 * i:2 * i + 2, :], ob[:, 2 * i:2 * i + 2, :])
                    split_pairs(wa0 + 4, wa0 + 6)
                    wo0 = AT["wo0"]
                    for half_ in range(2):
                        split(wo0 + half_, 0)
                        split(wo0 + half_, 1)
                        act.wait_ge(S["br_read"], 5 + half_)
                        for i in (2 * half_, 2 * half_ + 1):
                            split_moving(n_high[:, 2 * i:2 * i + 2, :], mix[:, 2 * i:2 * i + 2, :])
                    for i in range(4):
                        if i:
                            square(0, i - 1)
                        split(wo0 + 2 + i, 0)
                        if i < 3:
                            split(wo0 + 2 + i, 1)
                    square(0, 3)
                    split(wo0 + 5, 1)
                    root(0, 6)
                    for i in range(4):
                        split_n(2, i)
                    for i in range(8):
                        empty(f"wq{i}", qt[:, 2 * i:2 * i + 2, :], ACT.Copy)
                    act.wait_ge(S["sub_full"], 1)
                    for k in range(8):
                        if k == 4:
                            used(2 * (AT["keys"] + 1))
                        A(sub[:, k // 4, (k % 4) * 512:(k % 4 + 1) * 512], bank[2 + k % 6][:, :], ACT.Copy)\
                            .then_inc(S["sub_ready"], 1)
                        if k == 3:
                            split(AT["u1"], 0)
                            split(AT["u1"], 1)

                    def gelus(laps, done):
                        with act.Fori(0, laps) as lap:
                            for i in range(done, done + RING):
                                empty(f"u{i}", act_h[:, bass.ds(lap * (2 * RING) + 2 * i, 2), :],
                                      ACT.Gelu_apprx_tanh, lap)

                    gelus(6, 0)
                    act.wait_ge(S["exp_in"], 1)
                    A(picks[:, :, 2, :], picks[:, :, 2, :], ACT.Exp).then_inc(S["exp_out"], 1)
                    gelus(2, 24)
                    act.wait_ge(S["picks_ready"], 2)
                    gelus(7, 32)

                    def coefs(i, lap=None):
                        src = act_h[:, 2 * i:2 * i + 2, :] if lap is None else \
                            act_h[:, bass.ds(lap * (2 * RING) + 2 * i, 2), :]
                        at = 2 * (i % 4)
                        k = MOVING["coef"] + i
                        act.wait_ge(S["x_low"], k if lap is None else lap * RING + k)
                        A(two(0), src, ACT.Copy)
                        split_moving(n_high[:, at:at + 2, :], src)

                    for i in range(60, 63):
                        empty(f"u{i}", act_h[:, 2 * i:2 * i + 2, :], ACT.Gelu_apprx_tanh)
                    split(AT["v1"], 0)
                    used(2 * AT["v0"])
                    act.wait_ge(S["coef_ready"], GROUPS)
                    split_moving(n_high[:, 0:2, :], act_h[:, 0:2, :])
                    A(act_h[:, 126:128, :], two(USE["u63"] % 2), ACT.Gelu_apprx_tanh).then_inc(S["pj_free"], 1)
                    act.wait_ge(S["pj_free"], USE["pg0"])
                    split(AT["v1"], 1)
                    coefs(1)

                    def coefs_and_v(i, lap=None):
                        split(AT["v0"] + i, 0, lap)
                        coefs(i, lap)
                        split(AT["v0"] + i, 1, lap)

                    with act.Fori(0, 7) as lap:
                        for i in range(2, 6):
                            coefs_and_v(i, lap)
                    for i in range(30, 32):
                        coefs_and_v(i)
                    split(AT["v32"], 0)
                    split(AT["v32"], 1)
                    act.wait_ge(S["coef_ready"], 2 * GROUPS)
                    coefs(32)
                    coefs_and_v(33)
                    with act.Fori(0, 7) as lap:
                        for i in range(34, 38):
                            coefs_and_v(i, lap)
                    for i in range(62, 64):
                        coefs_and_v(i)
                    for i in range(3):
                        square(1, i)
                    split(AT["pg0"], 0)
                    square(1, 3)
                    split(AT["pg0"], 1)
                    root(1, 2)
                    for i in range(4):
                        split_n(3, i)
                    split(AT["pg1"], 0)
                    split(AT["pg1"], 1)
                    for i in range(4):
                        empty(f"pg{i}", z[:, 2 * i:2 * i + 2, :], ACT.Sigmoid, base=3)
                        square(2, i)
                    root(2, 5)

                @block.gpsimd
                def _(pool):
                    TT = nc.gpsimd.tensor_tensor

                    def lower(pair, lap=None):
                        for unit in range(2):
                            k = split_units(pair, unit)
                            pool.wait_ge(S["high_ready"], k if lap is None else lap * (2 * RING) + k)
                            cols = slice(unit * 1024, (unit + 1) * 1024)
                            TT(low[pair % RING][:, cols], ring[pair % RING][:, cols],
                               high[pair % HIGHS][:, cols].bitcast(f32), SUB).then_inc(S["low_ready"], 1)

                    def lower_all(first, end):
                        laps = (end - first) // RING
                        with pool.Fori(0, laps) as lap:
                            for i in range(RING):
                                lower(first + i, lap)
                        for pair in range(first + laps * RING, end):
                            lower(pair)

                    lower_all(1, AT["lru"])
                    lower_all(AT["lru"] + 1, AT["keys"])
                    lower_all(AT["u0"], AT["pp"])
                    lower_all(AT["pg0"], NPAIR + 1)

                @block.vector
                def _(dve):
                    V = nc.vector
                    o = Order(dve, S["vchain"])
                    TS, TT, STT = V.tensor_scalar, V.tensor_tensor, V.scalar_tensor_tensor

                    def over(ap, count):
                        return ap.unsqueeze(1).to_broadcast([P, count, ap.shape[1]])

                    def along(ap, count):
                        return ap.unsqueeze(2).to_broadcast([P, ap.shape[1], count])

                    def used(name):
                        dve.wait_ge(S["used"], 2 * (AT[name] + 1))

                    def lower(name, step, dst, src, high_):
                        dve.wait_ge(S["x_high"], MOVING[name] + step + 1)
                        TT(dst, src, high_.bitcast(f32), SUB).then_inc(S["x_low"], 1)

                    def lower_n(name, i, src=n):
                        t = slice(2 * i, 2 * i + 2)
                        lower(name, i, n_low[:, t, :], src[:, t, :], n_high[:, t, :])

                    def add_squares(k, i):
                        dve.wait_ge(S["squares"], 4 * k + i + 1)
                        if i:
                            o.link(TT(sq[:, 0, :], sq[:, 0, :], sq[:, 2 * i, :], ADD))
                        last = TT(sq[:, 0, :], sq[:, 0, :], sq[:, 2 * i + 1, :], ADD)
                        if i < 2:
                            o.link(last)
                        else:
                            last.then_inc(S["sq_added"], 1)

                    def invert(k):
                        dve.wait_ge(S["rms_ready"], k + 1)
                        V.reciprocal(rq, rq).then_inc(S["rms_inv"], 1)

                    def normalise(k, weight, b):
                        for i in range(4):
                            for t in (2 * i, 2 * i + 1):
                                last = STT(n[:, t, :], h[:, t, :], s(weight)[:, t:t + 1], bank[b][:, 256:512], MUL, MUL)
                            last.then_inc(S["n_ready"], 1)
                            if i:
                                lower_n(f"norm{k}", i - 1)
                        lower_n(f"norm{k}", 3)

                    def conv(dst, src, w, bias=None):
                        units = range(len(src))
                        for u in units:
                            last = TS(dst[u], src[u], w[u][3], None, MUL) if bias is None else \
                                TS(dst[u], src[u], w[u][3], bias[u], MUL, ADD)
                        for tap in (2, 1, 0):
                            o.link(last)
                            back = 3 - tap
                            for u in units:
                                last = STT(dst[u][:, back:], src[u][:, :SEQ - back], w[u][tap], dst[u][:, back:], MUL, ADD)
                        return last

                    dve.wait_ge(small_in, layer * 16 + 16)
                    dve.wait_ge(mixc_in, layer * 16 + 16)
                    normalise(1, "n_mix", 5)

                    dve.wait_ge(S["wba_split"], 1)
                    TT(wba_low[:, :], s("wba"), wba_high[:, :].bitcast(f32), SUB).then_inc(S["wba_low"], 1)

                    for i in range(6):
                        dve.wait_ge(S["pj_free"], i + 1)
                        us = (2 * i, 2 * i + 1)
                        w = s("bconv")
                        conv([cv[:, u, :] for u in us], [z[:, u, :] for u in us],
                             [[w[:, 4 * u + k:4 * u + k + 1] for k in range(4)] for u in us]).then_inc(S["conv_ready"], 1)
                    dve.wait_ge(S["ba_full"], 1)
                    for m in range(MT_):
                        V.tensor_copy(beta[:, m, :], bank[3][:, m * 8:m * 8 + 4])
                        TT(sp[:, 4 * m:4 * m + 4], bank[3][:, m * 8 + 4:m * 8 + 8], s("dt"), ADD)
                    o.link(TS(sp[:, 8:12], s("lam"), -1.0, None, MUL))
                    STT(sa, sp, -1.0, sp, MUL, MAX).then_inc(S["sp_in"], 1)
                    dve.wait_ge(S["sp_exp"], 3)
                    o.link(TS(ss, se, 2.0, None, ADD))
                    o.link(V.reciprocal(ss, ss))
                    o.link(TT(ss, ss, se, MUL))
                    o.link(TT(ssq, ss, ss, MUL))
                    o.link(TS(spo, ssq, 1.0 / 17, None, MUL))
                    for k in range(7, 0, -1):
                        o.link(STT(spo, spo, 1.0 / (2 * k + 1), ssq, ADD, MUL))
                    o.link(STT(spo, spo, 1.0, ss, ADD, MUL))
                    o.link(TS(spo, spo, 2.0, None, MUL))
                    o.link(STT(sp, sp, 0.0, spo, MAX, ADD))
                    o.link(TS(beta, beta, 1.0, None, ADD))
                    V.reciprocal(beta, beta)
                    TS(lrs, sp[:, 8:12], LRU_C / 2, None, MUL)
                    TS(lrn, sp[:, 8:12], -LRU_C, None, MUL)
                    for m in range(MT_):
                        last = STT(ag[:, m, :], sp[:, 4 * m:4 * m + 4], -1.0, nea, MUL, MUL)
                    last.then_inc(S["alpha_ready"], 1)

                    dve.wait_ge(S["rot_full"], 1)
                    TT(ropet[:, 0:2, :], two(4), over(sin[:, :], 2), MUL)
                    TT(ropet[:, 2:4, :], two(5), over(sin[:, :], 2), MUL)
                    TT(ropet[:, 4, :], bank[6][:, 0:SEQ], sin[:, :], MUL)
                    o.link(TT(qk[:, :, :], z[:, 12:17, :], over(cos[:, :], 5), MUL))
                    TT(qk[:, :, :], qk[:, :, :], ropet[:, :, :], ADD).then_inc(S["roped"], 1)
                    dve.wait_ge(S["l2_root"], 1)
                    o.link(V.reciprocal(rn, rn))
                    TS(rn[:, 0:8], rn[:, 0:8], float(B_DH) ** -0.5, None, MUL).then_inc(S["l2_inv"], 1)
                    w, b = s("cconv"), s("cbias")
                    for u0 in (0, 2):
                        dve.wait_ge(S["pj_free"], USE["cx0"] + u0 // 2 + 1)
                        us = (u0, u0 + 1)
                        last = conv([xc[:, u, :] for u in us], [z[:, 18 + u, :] for u in us],
                                    [[w[:, 4 * u + k:4 * u + k + 1] for k in range(4)] for u in us],
                                    [b[:, u:u + 1] for u in us])
                    last.then_inc(S["xc_ready"], 1)
                    dve.wait_ge(S["g_full"], 1)
                    o.link(V.tensor_copy(gs, bank[3][:, 0:32].rearrange("p (m k a) -> p m k a", m=2, k=4)))
                    TT(gs[:, :, 1, :], gs[:, :, 1, :], gs[:, :, 0, :], SUB).then_inc(S["g_dif"], 1)
                    dve.wait_ge(S["l2_full"], 1)
                    dve.wait_ge(S["silu_ready"], 6)
                    for i in range(4):
                        last = TT(cv[:, 2 * i:2 * i + 2, :], cv[:, 2 * i:2 * i + 2, :], two(4 + i), MUL)
                    last.then_inc(S["qkn_ready"], 1)
                    scale = float(A_DH) ** -0.5
                    for m, (sc, mask, banks) in enumerate(((sc0, "mask0", (2, 3)), (sc1, "mask1", (4, 5, 6, 7)))):
                        dve.wait_ge(S["scores_full"], m + 1)
                        k = A_HEADS // len(banks)
                        for i, b in enumerate(banks):
                            last = STT(sc[:, k * i:k * i + k, :], bank[b][:, :].rearrange("p (a i) -> p a i", a=k), scale,
                                       over(c(mask), k), MUL, ADD)
                            last.then_inc(S["masked"], 1)
                        dve.wait_ge(S["masked"], (2, 6)[m])
                        o.link(V.tensor_reduce(mx[:, m, :], sc[:, :, :], AX, MAX))
                        o.link(TT(mx[:, m, :], mx[:, m, :], s("sink"), MAX))
                        TS(nmx[:, m, :], mx[:, m, :], -1.0, None, MUL)
                        TT(esink[:, m, :], s("sink"), mx[:, m, :], SUB).then_inc(S["rowmax_ready"], 1)
                    dve.wait_ge(S["lru_sqrt"], 1)
                    TT(li[:, :, :], li[:, :, :], xc[:, :, :], MUL)
                    o.link(STT(lw[:, :, :], lr[:, :, :], 1.0, lt[:, :, :], ADD, MUL))
                    o.link(TT(li[:, :, :], li[:, :, :], lw[:, :, :], MUL))
                    for u in range(4):
                        last = V.tensor_tensor_scan(xc[:, u, :], lr[:, u, :], li[:, u, :], 0.0, MUL, ADD)
                    o.link(last)
                    dve.wait_ge(S["gcb_full"], 1)
                    for m, b in enumerate((7, 2)):
                        for hd in range(B_HEADS):
                            at = slice(hd * P, (hd + 1) * P)
                            last = TS(dec[:, m, at], bank[b][:, at], gs[:, m, 0, hd:hd + 1], 0.0, SUB, ALU.min)
                    last.then_inc(S["dif_ready"], 1)
                    for m, sc in enumerate((sc0, sc1)):
                        dve.wait_ge(S["exps_ready"], 9 * (m + 1))
                        o.link(TT(den[:, m, :], den[:, m, :], esink[:, m, :], ADD))
                        o.link(V.reciprocal(den[:, m, :], den[:, m, :]))
                        TT(sc[:, :, :], sc[:, :, :], along(den[:, m, :], P * (m + 1)), MUL).then_inc(S["normed"], 1)
                    dve.wait_ge(S["pj_free"], USE["cy1"] + 1)
                    TT(yc[:, :, :], xc[:, :, :], z[:, 26:30, :], MUL).then_inc(S["yc_ready"], 1)

                    dve.wait_ge(S["g_exp"], 1)
                    TT(bg_, beta, egs[:, :, 0, :], MUL)
                    dve.wait_ge(S["dec_exp"], 1)
                    heads8 = dec[:, :, :].rearrange("p m (a i) -> p (m a) i", i=P)
                    o.link(TT(heads8, heads8, over(tri, 8), MUL))
                    dve.wait_ge(S["kk_full"], 1)
                    for m in range(MT_):
                        last = TT(lo[:, m, :], bank[5 + m][:, :], dec[:, m, :], MUL)
                    o.link(last)
                    for m in range(MT_):
                        last = TT(lo[:, m, :], bank[3 + m][:, :], lo[:, m, :], MUL)
                    o.link(last)
                    lo8, ct8, mt8 = (x[:, :, :].rearrange("p m (a i) -> p (m a) i", i=P) for x in (lo, ct, mt))

                    def part(level):
                        mask = c("level")[:, level * P:(level + 1) * P]
                        TT(ct8, lo8, over(mask, 8), MUL).then_inc(S["level_ready"], 1)

                    part(0)
                    for m in range(MT_):
                        e = egb[:, m, :].rearrange("p (a i) -> p a i", i=P)
                        last = TT(e, cv[:, 0:4, m * P:(m + 1) * P], e, MUL)
                    last.then_inc(S["qg_ready"], 1)
                    dve.wait_ge(S["level_ready"], 1)
                    STT(mt8, ct8, -1.0, over(ident, 8), MUL, ADD).then_inc(S["transpose_ready"], 2)
                    dve.wait_ge(S["transpose_ready"], 2)
                    dve.wait_ge(S["qk_full"], 1)
                    for m, b in enumerate((7, 2)):
                        last = TT(qkd[:, m, :], bank[b][:, :], dec[:, m, :], MUL)
                    last.then_inc(S["qkd_ready"], 1)
                    dve.wait_ge(S["pv_full"], 1)
                    for m in range(MT_):
                        for g in range(A_KV):
                            mine = slice(64 * g, 64 * g + 64)
                            last = V.tensor_copy(ya[mine, :, m * P:(m + 1) * P], four(3 + 2 * m + g)[mine, :, :])
                    last.then_inc(S["ya_ready"], 1)
                    for m in range(MT_):
                        dve.wait_ge(S["x_full"], m + 1)
                        STT(mm_[:, m, :].rearrange("p (a i) -> p a i", i=P), four(3 + m), -1.0,
                            over(ident, 4), MUL, ADD).then_inc(S["inverse_ready"], 1)
                    part(1)
                    for level in range(1, 6):
                        if level < 5:
                            dve.wait_ge(S["x_full"], 2 * level + 2)
                            part(level + 1)
                        for m, b in enumerate((7, 2)):
                            dve.wait_ge(S["p_full"], 2 * level - 1 + m)
                            if level < 5:
                                TT(mm_[:, m, :], mm_[:, m, :], bank[5 + m][:, :], SUB).then_inc(S["inverse_ready"], 1)
                            TT(mt[:, m, :], mt[:, m, :], bank[b][:, :], SUB).then_inc(S["transpose_ready"], 1)
                    dve.wait_ge(S["tok_full"], 1)
                    for m in range(MT_):
                        def by_head(x):
                            return x[:, m, :].rearrange("p (a i) -> p a i", i=P)
                        TT(by_head(ct), four(3 + m), along(bg_[:, m, :], P), MUL)
                        TT(by_head(lo), four(3 + m), along(egs[:, m, 1, :], P), MUL)
                        last = TT(by_head(xx), four(5 + m), along(beta[:, m, :], P), MUL)
                    last.then_inc(S["tok_ready"], 1)
                    for ch in range(SEQ // CHUNK):
                        m, r = ch // 2, ch % 2
                        rows = slice(CHUNK * r, CHUNK * (r + 1))
                        dve.wait_ge(S["vn_full"], ch + 1)
                        V.tensor_copy(vn[rows, :], bank[3 + ch % 2][rows, :]).then_inc(S["vn_ready"], 1)
                        if ch == 3:
                            break
                        dve.wait_ge(S["s_full"], ch + 1)
                        if not ch:
                            last = V.tensor_copy(state, bank[7][:, :])
                        else:
                            for hd in range(B_HEADS):
                                at = slice(hd * P, (hd + 1) * P)
                                last = STT(state[:, at], state[:, at], egs[:, m, 2 + r, hd:hd + 1], bank[7][:, at],
                                           MUL, ADD)
                        last.then_inc(S["s_ready"], 1)
                        dve.wait_ge(S["s_ready"], ch + 1)
                    for i in range(2):
                        lower_n("ya", i, ya)
                    for i in range(2):
                        t, to = slice(2 * i, 2 * i + 2), slice(2 * i + 4, 2 * i + 6)
                        lower("yc", i, n_low[:, to, :], yc[:, t, :], n_high[:, to, :])

                    for q, (name, g0) in enumerate((("wa0", 30), ("wa1", 34), ("wc0", 46), ("wc1", 50),
                                                    ("wb0", 38), ("wb1", 42))):
                        used(name)
                        for k in range(2):
                            t = 4 * (q % 2) + 2 * k
                            gate = z[:, g0 + 2 * k:g0 + 2 * k + 2, :]
                            src = two(3 + 2 * (q % 2) + k)
                            if q < 2:
                                last = TT(mix[:, t:t + 2, :], src, gate, MUL)
                            else:
                                o.link(TT(mixt, src, gate, MUL))
                                last = TT(mix[:, t:t + 2, :], mix[:, t:t + 2, :], mixt, ADD)
                                if k == 0:
                                    o.link(last)
                        last.then_inc(S["br_read"], 1)
                        dve.wait_ge(S["br_read"], q + 1)
                        if not q:
                            dve.wait_ge(S["o_root"], 1)
                            V.reciprocal(on, on).then_inc(S["o_inv"], 1)
                            o.link(STT(ob[:, :, :], ob[:, :, :], s("dnorm"), z[:, 22:26, :], MUL, MUL))
                        if q == 1:
                            dve.wait_ge(S["o_spread"], 1)
                            for k, b in enumerate((7, 2)):
                                last = TT(ob[:, 2 * k:2 * k + 2, :], ob[:, 2 * k:2 * k + 2, :], two(b), MUL)
                            last.then_inc(S["yb_ready"], 1)
                            for i in range(2):
                                t = slice(2 * i, 2 * i + 2)
                                lower("ob", i, ob_low[:, t, :], ob[:, t, :], ob_high[:, t, :])
                        if q >= 4:
                            for i in (2 * q - 8, 2 * q - 7):
                                lower_n("mix", i, mix)
                    for i, bk in enumerate((7, 2, 3, 4)):
                        used(f"wo{i}")
                        TT(h[:, 2 * i:2 * i + 2, :], h[:, 2 * i:2 * i + 2, :], two(bk), ADD).then_inc(S["h_new"], 1)
                        if i < 3:
                            add_squares(0, i)
                    invert(0)
                    dve.wait_ge(S["rstd_full"], 1)
                    normalise(2, "n_ffn", 6)

                    def best16(values, rest, top, index):
                        all_ = range(len(values))
                        for k in all_:
                            last = V.max(top[k][:, 0:8], values[k])
                        o.link(last)
                        for k in all_:
                            V.max_index(index[k][:, 0:8], top[k][:, 0:8], values[k])
                            last = V.match_replace(rest[k], top[k][:, 0:8], values[k], -3.4028235e38)
                        o.link(last)
                        for k in all_:
                            last = V.max(top[k][:, 8:16], rest[k])
                        o.link(last)
                        for k in all_:
                            last = V.max_index(index[k][:, 8:16], top[k][:, 8:16], rest[k])
                        o.link(last)

                    def cut(x, size, count):
                        return [x[:, k * size:(k + 1) * size] for k in range(count)]

                    dve.wait_ge(S["sub_ready"], 8)
                    tops_ps, topf_ps, iota16 = bank[2][:, 0:256], bank[2][:, 256:512], bank[3][:, 0:TOPK]
                    V.tensor_copy(iota16, c("iota")[:, 0:TOPK])
                    shape4 = [P, HEADS, TOPK, TOPK]
                    for m in range(MT_):
                        best16(cut(sub[:, m, :], P, 16), cut(sub2, P, 16),
                               cut(tops[:, m, :], TOPK, 16), cut(topi[:, m, :], TOPK, 16))
                        V.tensor_copy(topf_ps, topi[:, m, :])
                        o.link(V.tensor_copy(tops_ps, tops[:, m, :]))
                        sides = tops[:, m, :].rearrange("p (h s k) -> p h s k", s=2, k=TOPK)
                        sides_ps = tops_ps.rearrange("p (h s k) -> p h s k", s=2, k=TOPK)
                        pairs = cand.rearrange("p (h a b) -> p h a b", a=TOPK, b=TOPK)
                        o.link(TT(pairs, sides[:, :, 0, :].unsqueeze(3).to_broadcast(shape4),
                                  sides_ps[:, :, 1, :].unsqueeze(2).to_broadcast(shape4), ADD))
                        best16(cut(cand, 256, HEADS), cut(cand2, 256, HEADS),
                               cut(best[:, m, :], TOPK, HEADS), cut(besti[:, m, :], TOPK, HEADS))
                        keys_ = topf_ps.rearrange("p (h s k) -> p h s k", s=2, k=TOPK)
                        for side in range(2):
                            if side == 0:
                                o.link(TS(half[:, m, :], besti[:, m, :], 4, None, ALU.logical_shift_right))
                            else:
                                o.link(TS(half[:, m, :], besti[:, m, :], 15, None, ALU.bitwise_and))
                            o.link(V.tensor_copy(halff[:, m, :], half[:, m, :]))
                            flat = cand.rearrange("p (k c) -> p k c", c=TOPK)
                            o.link(TT(flat, along(halff[:, m, :], TOPK), over(iota16, P), ALU.is_equal))
                            o.link(TT(pairs, pairs, keys_[:, :, side, :].unsqueeze(2).to_broadcast(shape4), MUL))
                            o.link(V.tensor_reduce(picks[:, m, side, :], flat, AX, ADD))
                        bests = best[:, m, :].rearrange("p (h k) -> p h k", k=TOPK)
                        gate = picks[:, m, 2, :].rearrange("p (h k) -> p h k", k=TOPK)
                        last = TT(gate, bests, bests[:, :, 0:1].to_broadcast([P, HEADS, TOPK]), SUB)
                        if m == 0:
                            o.link(last)
                    last.then_inc(S["exp_in"], 1)
                    dve.wait_ge(S["exp_out"], 1)
                    for m in range(MT_):
                        gate = picks[:, m, 2, :].rearrange("p (h k) -> p h k", k=TOPK)
                        o.link(V.tensor_reduce(gsum[:, m, :], gate, AX, ADD))
                        o.link(V.reciprocal(gsum[:, m, :], gsum[:, m, :]))
                        TT(gate, gate, along(gsum[:, m, :], TOPK), MUL).then_inc(S["picks_ready"], 1)
                    dve.wait_ge(S["tr_full"], 1)
                    for m in range(MT_):
                        last = V.tensor_copy(route[:, :, m * P:(m + 1) * P], four(6 + m)[:, 0:3, :])
                    last.then_inc(S["route_ready"], 1)
                    dve.wait_ge(S["route_ready"], 1)
                    rest = route[:, 2, :]
                    for k in range(3):
                        o.link(V.tensor_copy(gate3[:, :, k], rest))
                        if k < 2:
                            o.link(TT(rest, rest, gate3[:, :, k], SUB))
                    by_token = act_h[:, :, :].rearrange("p j t -> p t j")
                    o.link(V.tensor_copy(bank[FREE_BANK[0]][:, 0:P], c("iota")))

                    def key(k, token, count):
                        return route[:, k, bass.ds(token, 4)].unsqueeze(2).to_broadcast([P, 4, count])

                    def hot(b, half_, group, token, during):
                        free = bank[FREE_BANK[during]]
                        iota_ps, key2 = free[:, 0:P], free[:, 256:512].rearrange("p (k j) -> p k j", k=4)
                        if not isinstance(group, int) or group:
                            dve.wait_ge(S["hot_ready"], group)
                        TT(key2, key(1, token, HALF), over(iota_ps[:, half_ * HALF:(half_ + 1) * HALF], 4),
                           ALU.is_equal).then_inc(S["ones_ready"], 1)
                        TT(hot1[b][:, :, :], key(0, token, P), over(iota_ps, 4), ALU.is_equal)
                        dve.wait_ge(S["ones_ready"], group + 1)
                        shape = [P, 4, 3, HALF]
                        TT(hot2[b][:, :, :, :], key2.unsqueeze(2).to_broadcast(shape),
                           gate3[:, bass.ds(token, 4), :].unsqueeze(3).to_broadcast(shape), MUL)\
                               .then_inc(S["hot_ready"], 1)

                    def coefficients(b, half_, group, token):
                        dve.wait_ge(S["gates_full"], group + 1)
                        acts = by_token[:, bass.ds(token, 4), half_ * HALF:(half_ + 1) * HALF]
                        TT(acts, bank[6 + b][:, 0:4 * HALF].rearrange("p (k j) -> p k j", k=4), acts, MUL)\
                            .then_inc(S["coef_ready"], 1)

                    for b in range(2):
                        hot(b, 0, b, 4 * b, 0)
                    dve.wait_ge(S["pj_free"], USE["u32"])
                    with dve.Fori(0, GROUPS // 2 - 1) as it:
                        for b in range(2):
                            coefficients(b, 0, it * 2 + b, it * 8 + 4 * b)
                            hot(b, 0, it * 2 + (2 + b), it * 8 + (8 + 4 * b), 0)
                    for b in range(2):
                        coefficients(b, 0, GROUPS - 2 + b, SEQ - 8 + 4 * b)
                        hot(b, 1, GROUPS + b, 4 * b, 0)

                    def coef_low(i, lap=None):
                        t = slice(2 * (i % 4), 2 * (i % 4) + 2)
                        k = MOVING["coef"] + i + 1
                        dve.wait_ge(S["x_high"], k if lap is None else lap * RING + k)
                        TT(n_low[:, t, :], two(0), n_high[:, t, :].bitcast(f32), SUB).then_inc(S["x_low"], 1)

                    lower("coef", 0, n_low[:, 0:2, :], act_h[:, 0:2, :], n_high[:, 0:2, :])
                    dve.wait_ge(S["pj_free"], USE["pg0"])
                    o.link(V.tensor_copy(bank[FREE_BANK[1]][:, 0:P], c("iota")))
                    with dve.Fori(0, 7) as lap:
                        for i in range(4):
                            for b in range(2):
                                g = 2 * i + b
                                coefficients(b, 1, lap * 8 + (GROUPS + g), lap * 32 + 4 * g)
                                hot(b, 1, lap * 8 + (GROUPS + g + 2), lap * 32 + (4 * g + 8), 1)
                            coef_low(i + 1, lap)
                    for i in range(4):
                        for b in range(2):
                            g = 56 + 2 * i + b
                            coefficients(b, 1, GROUPS + g, 4 * g)
                            if g + 2 < GROUPS:
                                hot(b, 1, GROUPS + g + 2, 4 * g + 8, 1)
                        coef_low(29 + i)
                    with dve.Fori(0, 7) as lap:
                        for i in range(33, 37):
                            coef_low(i, lap)
                    for i in range(61, 64):
                        coef_low(i)
                    for i in range(4):
                        if i < 3:
                            dve.wait_ge(S["v_full"], i + 1)
                        else:
                            used("v63")
                        TT(h[:, 2 * i:2 * i + 2, :], h[:, 2 * i:2 * i + 2, :], two(2 + i), ADD).then_inc(S["h_new"], 1)
                        if i:
                            add_squares(1, i - 1)
                    invert(1)
                    dve.wait_ge(S["rstd_full"], 2)
                    normalise(3, "n_ple", 2)
                    used("pp")
                    for i in range(4):
                        dve.wait_ge(S["pj_free"], USE["pg0"] + i + 1)
                        o.link(TT(mixt, two(PLE_BANKS[i]), z[:, 2 * i:2 * i + 2, :], MUL))
                        last = TT(h[:, 2 * i:2 * i + 2, :], h[:, 2 * i:2 * i + 2, :], mixt, ADD)
                        last.then_inc(S["h_new"], 1)
                        dve.wait_ge(S["h_new"], 9 + i)
                        if i < 3:
                            add_squares(2, i)
                    invert(2)

            nc.all_engine_barrier(sems_to_clear=layer_sems)

        with nc.Block() as block:
            @block.vector
            def _(dve):
                for t in range(KT):
                    nc.vector.scalar_tensor_tensor(n[:, t, :], h[:, t, :], c("final")[:, t:t + 1], bank[5][:, 256:512],
                                                   MUL, MUL)\
                        .then_inc(S["n_ready"], 1)

            @block.sync
            def _(sync):
                for half_ in range(2):
                    sync.wait_ge(S["n_ready"], 4 * half_ + 4)
                    sync.dma_start(out[:, 4 * half_:4 * half_ + 4, :], n[:, 4 * half_:4 * half_ + 4, :])\
                        .then_inc(stored_out, 16)
                sync.wait_ge(stored_out, 32)
                for done in [small_in, mixc_in] + ahead:
                    sync.wait_ge(done, 16 * (DEPTH + 1))


def constants():
    p = np.arange(P)
    f = np.float32
    chunk = p // CHUNK
    same = chunk[:, None] == chunk[None, :]
    out, mixc = np.zeros((P, NCONST), f), np.zeros((P, NMIXC), f)

    def put(name, value):
        a, b = CONST[name] if name in CONST else MIXC[name]
        (out if name in CONST else mixc)[:, a:b] = value
    put("ident", np.eye(P))
    put("ones", 1.0)
    put("tri", same & (p[:, None] <= p[None, :]))
    put("blk", same)
    put("chunk", np.repeat(chunk[:, None] == np.arange(2)[None, :], P, axis=1))
    levels = []
    for level in range(6):
        size = 1 << level
        levels.append((p[:, None] // (2 * size) == p[None, :] // (2 * size))
                      & (p[:, None] // size % 2 == 0) & (p[None, :] // size % 2 == 1))
    put("level", np.concatenate(levels, 1))
    half = A_DH // 2
    partner = p // A_DH * A_DH + (p + half) % A_DH
    put("rot", p[:, None] == partner[None, :])
    for m, name in enumerate(("mask0", "mask1")):
        q, k = (m * P + p)[:, None] // CHUNK, np.arange((m + 1) * P)[None, :] // CHUNK
        put(name, np.where((k == q) | (k == q - 1), 0.0, -1e30))
    put("iota", p[None, :])
    put("freq", (ROPE_THETA ** (-np.arange(half, dtype=f) / f(half))).astype(f)[p % half][:, None])
    put("sign", np.where(p % A_DH < half, -1.0, 1.0)[:, None])
    return out, mixc


def units(w):
    k, m = w.shape
    return w.reshape(k // P, P, m // P, P).transpose(2, 1, 0, 3)


def pairs(u):
    return u.reshape(-1, 2, P, 1024).transpose(0, 2, 1, 3).reshape(-1, P, 2048)


def lay_out(x, p, positions, norm_mix, w_in, attn_sinks, dn_conv, dn_a_log, dn_dt_bias, dn_norm, lru_conv_w,
            lru_conv_b, lru_w_a, lru_b_a, lru_w_i, lru_b_i, lru_lambda, w_branch_a, w_branch_b, w_branch_c,
            w_out, norm_ffn, peer_w_q, peer_sub_keys, peer_u, peer_v, norm_ple, ple_w_gate, ple_w_proj,
            norm_final):
    const, mixc = constants()
    const[:, slice(*CONST["final"])] = norm_final.reshape(KT, P).T
    order = np.concatenate([np.arange(hd * A_DH, (hd + 1) * A_DH) for i in range(4) for hd in (i, 4 + i)])
    sizes = [512, 128, 128, 1536, 4, 4, 512, 512, 512, 1024, 1024, 1024]
    stream = np.empty((DEPTH * NPAIR, P, 2048), np.float32)
    small = np.zeros((DEPTH, P, NSMALL), np.float32)
    for l in range(DEPTH):
        aq, ak, av, bqkv, bbeta, balpha, bgate, cx, cy, ga, gb, gc = np.split(w_in[l], np.cumsum(sizes)[:-1], axis=1)
        base = l * NPAIR

        def put(name, value):
            at = base + AT[name]
            stream[at:at + len(value)] = value
        main = np.concatenate([bqkv, aq[:, order], ak, av, cx, bgate, cy, ga, gb, gc], axis=1)
        for name, value in zip(PROJ, pairs(units(main))):
            put(name, value[None])
        lru = np.zeros((P, 16, P), np.float32)
        for i, w in enumerate((lru_w_a[l], lru_w_i[l])):
            for t in range(4):
                for e in range(2):
                    lru[64 * e:64 * e + 64, 4 * i + t, 64 * e:64 * e + 64] = w[2 * t + e]
        put("lru", lru.reshape(1, P, 2048))
        for name, w in (("wa0", w_branch_a[l][order]), ("wb0", w_branch_b[l]), ("wc0", w_branch_c[l])):
            put(name, units(w).reshape(2, 4, P, 512).transpose(0, 2, 1, 3).reshape(2, P, 2048))
        put("wo0", pairs(units(w_out[l])))
        put("wq0", pairs(units(peer_w_q[l])))
        put("keys", peer_sub_keys[l].transpose(3, 0, 1, 2).reshape(1, P, 2048))
        put("u0", pairs(peer_u[l].reshape(NKEYS, NKEYS, KT, P).transpose(1, 3, 2, 0)))
        put("v0", pairs(peer_v[l].reshape(NKEYS, NKEYS, D_MODEL).transpose(1, 0, 2)))
        put("pp", units(ple_w_proj[l]).transpose(1, 0, 2, 3).reshape(1, P, 2048))
        put("pg0", pairs(units(ple_w_gate[l])))

        def col(name, value):
            a, b = SMALL[name]
            small[l, :, a:b] = value
        col("n_mix", norm_mix[l].reshape(KT, P).T)
        col("n_ffn", norm_ffn[l].reshape(KT, P).T)
        col("n_ple", norm_ple[l].reshape(KT, P).T)
        col("bconv", dn_conv[l].reshape(4, 12, P).transpose(2, 1, 0).reshape(P, 48))
        col("cconv", lru_conv_w[l].reshape(4, 4, P).transpose(2, 1, 0).reshape(P, 16))
        col("cbias", lru_conv_b[l].reshape(4, P).T)
        col("ba", lru_b_a[l].reshape(4, P).T)
        col("bi", lru_b_i[l].reshape(4, P).T)
        col("lam", lru_lambda[l].reshape(4, P).T)
        col("dnorm", dn_norm[l][:, None])
        col("sink", attn_sinks[l][None, :])
        col("alog", dn_a_log[l][None, :])
        col("dt", dn_dt_bias[l][None, :])
        col("wba", np.concatenate([bbeta, balpha], 1).reshape(KT, P, 8).transpose(1, 0, 2).reshape(P, 64))
    return {
        "stream": stream,
        "small": small,
        "p": np.ascontiguousarray(p[:, 0].transpose(0, 2, 1).reshape(DEPTH, 2, P, SEQ).transpose(0, 2, 1, 3)),
        "x": np.ascontiguousarray(x[0].T.reshape(KT, P, SEQ).transpose(1, 0, 2)),
        "positions": np.ascontiguousarray(positions[0]),
        "const": const,
        "mixc": mixc,
    }


def kernel(**inputs):
    import concourse.bacc as _bacc
    from concourse.bass_utils import run_bass_kernel_spmd as _run

    arrays = lay_out(**{k: np.asarray(v) for k, v in inputs.items()})
    nc = _bacc.Bacc("TRN2", target_bir_lowering=False, num_devices=1, dynamic_dma_scratch_size=1024)
    aps = {name: nc.dram_tensor(f"in_{name}", a.shape, mybir.dt.from_np(a.dtype), kind="ExternalInput").ap()
           for name, a in arrays.items()}
    out = nc.dram_tensor("out", (P, KT, SEQ), mybir.dt.float32, kind="ExternalOutput").ap()
    build_trunk(nc, aps["stream"], aps["small"], aps["p"], aps["x"], aps["positions"], aps["const"],
                aps["mixc"], out)
    r = _run(nc, [{f"in_{k}": v for k, v in arrays.items()}], core_ids=[0])
    got = r.results[0]["out"]
    return np.ascontiguousarray(got.transpose(2, 1, 0).reshape(1, SEQ, D_MODEL))
```
